# Optimizing a Trainium2 kernel written in Bass

```python
import jax
import jax.numpy as jnp
from jax import lax
import numpy as np
import jax, jax.numpy as jnp

D_MODEL = 1024
BATCH = 1
SEQ = 256
DEPTH = 2

HGRN_WIDTH = D_MODEL // 2
HGRN_HEAD_DIM = 128
HGRN_HEADS = HGRN_WIDTH // HGRN_HEAD_DIM
HGRN_CHUNK = 64
HGRN_PROJ = 4 * HGRN_WIDTH
RWKV_WIDTH = D_MODEL // 2
RWKV_HEAD_DIM = 64
RWKV_HEADS = RWKV_WIDTH // RWKV_HEAD_DIM
RWKV_DECAY_LORA = 64
RWKV_AAA_LORA = 64
RWKV_GATE_LORA = 128
RWKV_LN_EPS = 64e-5
RWKV_PROJ = 3 * RWKV_WIDTH + RWKV_DECAY_LORA + RWKV_AAA_LORA + RWKV_GATE_LORA
AR_PROJ = HGRN_PROJ + RWKV_PROJ
ATTN_HEADS = 8
ATTN_HEAD_DIM = D_MODEL // ATTN_HEADS
MOBA_BLOCK = 256
MOBA_TOPK = 3
MOBA_QCHUNK = 64
ROPE_THETA = 10000.0
D_FF = 4 * D_MODEL
PLE_DIM = 256
N_EVEN = (DEPTH + 1) // 2
N_ODD = DEPTH // 2
NORM_EPS = 1e-6


def rms_norm(x, g, eps=NORM_EPS):
    xf = x.astype(jnp.float32)
    y = xf * lax.rsqrt(jnp.mean(xf * xf, axis=-1, keepdims=True) + eps)
    return (y * g.astype(jnp.float32)).astype(x.dtype)

def head_layer_norm(y, w, b, eps=RWKV_LN_EPS):
    yf = y.astype(jnp.float32)
    mu = jnp.mean(yf, axis=-1, keepdims=True)
    var = jnp.mean(jnp.square(yf - mu), axis=-1, keepdims=True)
    return (yf - mu) * lax.rsqrt(var + eps) * w + b

def rotary(x, pos):
    half = x.shape[-1] // 2
    inv_freq = jnp.power(ROPE_THETA, -jnp.arange(half, dtype=jnp.float32) / half)
    ang = pos.astype(jnp.float32)[:, None] * inv_freq[None, :]
    cos = jnp.cos(ang)[None, :, None, :]
    sin = jnp.sin(ang)[None, :, None, :]
    xf = x.astype(jnp.float32)
    x1, x2 = xf[..., :half], xf[..., half:]
    return jnp.concatenate([x1 * cos - x2 * sin, x2 * cos + x1 * sin], axis=-1).astype(x.dtype)

def token_shift(u):
    return jnp.pad(u[:, :-1], ((0, 0), (1, 0), (0, 0)))

def hgrn2_chunked(q, k, v, log_f):
    B, H, S, dk = q.shape
    dv = v.shape[-1]
    C = HGRN_CHUNK
    n = S // C

    def to_chunks(t):
        return t.reshape(B, H, n, C, t.shape[-1]).transpose(2, 0, 1, 3, 4)

    causal = jnp.tril(jnp.ones((C, C), dtype=bool))

    def step(state, inp):
        qc, kc, vc, gc = inp
        b = jnp.cumsum(gc, axis=2)
        o_inter = jnp.einsum('bhtk,bhkv->bhtv', qc * jnp.exp(b), state)
        diff = jnp.where(causal[None, None, :, :, None],
                         b[:, :, :, None, :] - b[:, :, None, :, :], -jnp.inf)
        scores = jnp.einsum('bhtk,bhsk,bhtsk->bhts', qc, kc, jnp.exp(diff))
        o_intra = jnp.einsum('bhts,bhsv->bhtv', scores, vc)
        b_last = b[:, :, -1:, :]
        state = (state * jnp.exp(b_last)[:, :, 0, :, None]
                 + jnp.einsum('bhsk,bhsv->bhkv', kc * jnp.exp(b_last - b), vc))
        return state, o_inter + o_intra

    state0 = jnp.zeros((B, H, dk, dv), jnp.float32)
    _, o = lax.scan(step, state0, (to_chunks(q), to_chunks(k), to_chunks(v), to_chunks(log_f)))
    return o.transpose(1, 2, 0, 3, 4).reshape(B, H, S, dv)

def rwkv7_scan(r, decay, k, v, kk, a):
    B, S, H, N = r.shape

    def step(state, inp):
        r_t, w_t, k_t, v_t, kk_t, a_t = inp
        sa = jnp.einsum('bhvk,bhk->bhv', state, -kk_t)
        state = (state * w_t[:, :, None, :]
                 + sa[..., None] * (kk_t * a_t)[:, :, None, :]
                 + v_t[..., None] * k_t[:, :, None, :])
        return state, jnp.einsum('bhvk,bhk->bhv', state, r_t)

    xs = (r.transpose(1, 0, 2, 3), decay.transpose(1, 0, 2, 3), k.transpose(1, 0, 2, 3),
          v.transpose(1, 0, 2, 3), kk.transpose(1, 0, 2, 3), a.transpose(1, 0, 2, 3))
    state0 = jnp.zeros((B, H, N, N), jnp.float32)
    _, y = lax.scan(step, state0, xs)
    return y.transpose(1, 0, 2, 3)

def hgrn_rwkv_mixer(h, w_in, w_out, lb, onorm, mu, w0, w2, a0, a2, g2, k_k, k_a, r_k, ln_w, ln_b):
    B, S, _ = h.shape
    u = (h @ w_in).astype(jnp.float32)
    hq, hf, hi, hg, ur = jnp.split(u, [HGRN_WIDTH, 2 * HGRN_WIDTH, 3 * HGRN_WIDTH, HGRN_PROJ], axis=-1)

    def heads(t, n_heads):
        return t.reshape(B, S, n_heads, -1).transpose(0, 2, 1, 3)

    f = lb + (1.0 - lb) * jax.nn.sigmoid(hf)
    o_a = hgrn2_chunked(heads(jax.nn.silu(hq), HGRN_HEADS), heads(1.0 - f, HGRN_HEADS),
                        heads(hi, HGRN_HEADS), heads(jnp.log(f), HGRN_HEADS))
    o_a = rms_norm(o_a.transpose(0, 2, 1, 3), onorm.reshape(HGRN_HEADS, HGRN_HEAD_DIM))
    o_a = o_a.reshape(B, S, HGRN_WIDTH) * jax.nn.silu(hg)

    ur = ur + (token_shift(ur) - ur) * mu
    r, k, v, wd, ad, gd = jnp.split(
        ur, [RWKV_WIDTH, 2 * RWKV_WIDTH, 3 * RWKV_WIDTH, 3 * RWKV_WIDTH + RWKV_DECAY_LORA,
             3 * RWKV_WIDTH + RWKV_DECAY_LORA + RWKV_AAA_LORA], axis=-1)
    w = -jax.nn.softplus(-(w0 + jnp.tanh(wd) @ w2)) - 0.5
    decay = jnp.exp(-jnp.exp(w))
    a = jax.nn.sigmoid(a0 + ad @ a2)
    g = jax.nn.sigmoid(gd) @ g2
    kk = (k * k_k).reshape(B, S, RWKV_HEADS, RWKV_HEAD_DIM)
    kk = kk / jnp.maximum(jnp.sqrt(jnp.sum(kk * kk, axis=-1, keepdims=True)), 1e-12)
    k = k * (1.0 + (a - 1.0) * k_a)

    def rh(t):
        return t.reshape(B, S, RWKV_HEADS, RWKV_HEAD_DIM)

    r4, k4, v4 = rh(r), rh(k), rh(v)
    y = rwkv7_scan(r4, rh(decay), k4, v4, kk, rh(a))
    y = head_layer_norm(y, ln_w.reshape(RWKV_HEADS, RWKV_HEAD_DIM),
                        ln_b.reshape(RWKV_HEADS, RWKV_HEAD_DIM))
    bonus = jnp.sum(r4 * k4 * r_k.reshape(RWKV_HEADS, RWKV_HEAD_DIM), axis=-1, keepdims=True) * v4
    o_b = (y + bonus).reshape(B, S, RWKV_WIDTH) * g

    o = jnp.concatenate([o_a, o_b], axis=-1).astype(h.dtype)
    return o @ w_out

def moba_attention(q, k, v):
    B, H, S, Dh = q.shape
    nb = -(-S // MOBA_BLOCK)
    pad = nb * MOBA_BLOCK - S
    kb = jnp.pad(k, ((0, 0), (0, 0), (0, pad), (0, 0))).reshape(B, H, nb, MOBA_BLOCK, Dh)
    vb = jnp.pad(v, ((0, 0), (0, 0), (0, pad), (0, 0))).reshape(B, H, nb, MOBA_BLOCK, Dh)
    scale = Dh ** -0.5
    q_blk = jnp.arange(S) // MOBA_BLOCK
    n_sel = min(MOBA_TOPK, nb - 1)
    if n_sel > 0:
        k_mean = jnp.mean(kb.astype(jnp.float32), axis=3)
        gate = jnp.einsum('bhsd,bhnd->bhsn', q.astype(jnp.float32), k_mean)
        past = jnp.arange(nb)[None, :] < q_blk[:, None]
        gate = jnp.where(past, gate, -jnp.inf)
        _, sel = lax.top_k(gate, n_sel)
    else:
        sel = jnp.zeros((B, H, S, 0), jnp.int32)
    valid = jnp.arange(n_sel)[None, :] < q_blk[:, None]

    qc_size = MOBA_QCHUNK
    nc = S // qc_size
    q_chunks = q.reshape(B, H, nc, qc_size, Dh).transpose(2, 0, 1, 3, 4)
    sel_chunks = sel.reshape(B, H, nc, qc_size, n_sel).transpose(2, 0, 1, 3, 4)
    valid_chunks = valid.reshape(nc, qc_size, n_sel)
    bi = jnp.arange(B)[:, None, None]
    hi = jnp.arange(H)[None, :, None]

    def attend_chunk(inp):
        c, qc, sel_c, valid_c = inp
        q_pos = c * qc_size + jnp.arange(qc_size)
        own = (c * qc_size) // MOBA_BLOCK
        k_own = lax.dynamic_index_in_dim(kb, own, axis=2, keepdims=False)
        v_own = lax.dynamic_index_in_dim(vb, own, axis=2, keepdims=False)
        k_pos = own * MOBA_BLOCK + jnp.arange(MOBA_BLOCK)
        s_own = jnp.einsum('bhqd,bhkd->bhqk', qc, k_own).astype(jnp.float32) * scale
        scores = [jnp.where(k_pos[None, :] <= q_pos[:, None], s_own, -jnp.inf)]
        for j in range(n_sel):
            k_sel = kb[bi, hi, sel_c[..., j]]
            s = jnp.einsum('bhqd,bhqkd->bhqk', qc, k_sel).astype(jnp.float32) * scale
            scores.append(jnp.where(valid_c[:, j][:, None], s, -jnp.inf))
        probs = jax.nn.softmax(jnp.concatenate(scores, axis=-1), axis=-1).astype(vb.dtype)
        out = jnp.einsum('bhqk,bhkd->bhqd', probs[..., :MOBA_BLOCK], v_own)
        for j in range(n_sel):
            v_sel = vb[bi, hi, sel_c[..., j]]
            p_j = probs[..., (j + 1) * MOBA_BLOCK:(j + 2) * MOBA_BLOCK]
            out = out + jnp.einsum('bhqk,bhqkd->bhqd', p_j, v_sel)
        return out

    o = lax.map(attend_chunk, (jnp.arange(nc), q_chunks, sel_chunks, valid_chunks))
    return o.transpose(1, 2, 0, 3, 4).reshape(B, H, S, Dh)

def moba_mixer(h, w_qkv, w_o, q_gain, k_gain, pos):
    B, S, D = h.shape
    q, k, v = jnp.split(h @ w_qkv, 3, axis=-1)
    q = q.reshape(B, S, ATTN_HEADS, ATTN_HEAD_DIM)
    k = k.reshape(B, S, ATTN_HEADS, ATTN_HEAD_DIM)
    v = v.reshape(B, S, ATTN_HEADS, ATTN_HEAD_DIM)
    q = rotary(rms_norm(q, q_gain), pos)
    k = rotary(rms_norm(k, k_gain), pos)
    o = moba_attention(q.transpose(0, 2, 1, 3), k.transpose(0, 2, 1, 3), v.transpose(0, 2, 1, 3))
    return o.transpose(0, 2, 1, 3).reshape(B, S, D) @ w_o

def first_inputs(seed: int = 0) -> dict:
    key = jax.random.key(seed)
    ks = iter(jax.random.split(key, 40))

    def normal(shape, scale):
        return jax.random.normal(next(ks), shape, jnp.float32) * scale

    def gain(shape):
        return 1.0 + normal(shape, 0.05)

    D = D_MODEL
    mix_w = HGRN_WIDTH + RWKV_WIDTH
    return {
        'x': normal((BATCH, SEQ, D), 1.0),
        'p': normal((DEPTH, BATCH, SEQ, PLE_DIM), 1.0),
        'attn_norm': gain((DEPTH, D)),
        'mlp_norm': gain((DEPTH, D)),
        'w_in_ar': normal((N_EVEN, D, AR_PROJ), D ** -0.5),
        'w_out_ar': normal((N_EVEN, mix_w, D), mix_w ** -0.5),
        'hgrn_lb': normal((DEPTH + 1, HGRN_WIDTH), 0.5),
        'hgrn_onorm': gain((N_EVEN, HGRN_WIDTH)),
        'rwkv_mu': jax.random.uniform(next(ks), (N_EVEN, RWKV_PROJ), jnp.float32),
        'rwkv_w0': jax.random.uniform(next(ks), (N_EVEN, RWKV_WIDTH), jnp.float32, -3.0, 1.0),
        'rwkv_w2': normal((N_EVEN, RWKV_DECAY_LORA, RWKV_WIDTH), 0.1 * RWKV_DECAY_LORA ** -0.5),
        'rwkv_a0': normal((N_EVEN, RWKV_WIDTH), 0.5),
        'rwkv_a2': normal((N_EVEN, RWKV_AAA_LORA, RWKV_WIDTH), 0.1 * RWKV_AAA_LORA ** -0.5),
        'rwkv_g2': normal((N_EVEN, RWKV_GATE_LORA, RWKV_WIDTH), RWKV_GATE_LORA ** -0.5),
        'rwkv_kk': 0.85 + normal((N_EVEN, RWKV_WIDTH), 0.05),
        'rwkv_ka': 1.0 + normal((N_EVEN, RWKV_WIDTH), 0.05),
        'rwkv_rk': normal((N_EVEN, RWKV_WIDTH), 0.1),
        'rwkv_ln_w': gain((N_EVEN, RWKV_WIDTH)),
        'rwkv_ln_b': normal((N_EVEN, RWKV_WIDTH), 0.02),
        'w_qkv': normal((N_ODD, D, 3 * D), D ** -0.5),
        'w_o_attn': normal((N_ODD, D, D), D ** -0.5),
        'q_norm': gain((N_ODD, ATTN_HEAD_DIM)),
        'k_norm': gain((N_ODD, ATTN_HEAD_DIM)),
        'w_up': normal((DEPTH, D, D_FF), D ** -0.5),
        'w_down': normal((DEPTH, D_FF, D), D_FF ** -0.5),
        'ple_proj': normal((DEPTH, PLE_DIM, D), PLE_DIM ** -0.5),
        'ple_norm': gain((DEPTH, D)),
        'ple_gate': normal((DEPTH, D, D), D ** -0.5),
    }

def first_block(x, p, attn_norm, mlp_norm, w_in_ar, w_out_ar, hgrn_lb, hgrn_onorm,
              rwkv_mu, rwkv_w0, rwkv_w2, rwkv_a0, rwkv_a2, rwkv_g2, rwkv_kk, rwkv_ka, rwkv_rk,
              rwkv_ln_w, rwkv_ln_b, w_qkv, w_o_attn, q_norm, k_norm, w_up, w_down,
              ple_proj, ple_norm, ple_gate):
    S = x.shape[1]
    pos = jnp.arange(S)
    lb_all = jnp.cumsum(jax.nn.softmax(hgrn_lb.astype(jnp.float32), axis=0), axis=0)
    for l in range(DEPTH):
        h = rms_norm(x, attn_norm[l])
        if l % 2 == 0:
            e = l // 2
            mix = hgrn_rwkv_mixer(h, w_in_ar[e], w_out_ar[e], lb_all[l], hgrn_onorm[e],
                                  rwkv_mu[e], rwkv_w0[e], rwkv_w2[e], rwkv_a0[e], rwkv_a2[e],
                                  rwkv_g2[e], rwkv_kk[e], rwkv_ka[e], rwkv_rk[e],
                                  rwkv_ln_w[e], rwkv_ln_b[e])
        else:
            o = l // 2
            mix = moba_mixer(h, w_qkv[o], w_o_attn[o], q_norm[o], k_norm[o], pos)
        x = x + mix.astype(x.dtype)
        h = rms_norm(x, mlp_norm[l])
        x = x + jnp.square(jax.nn.relu(h @ w_up[l])) @ w_down[l]
        ple = rms_norm(p[l] @ ple_proj[l], ple_norm[l])
        x = x + ple * jax.nn.sigmoid(x @ ple_gate[l])
    return x


DEPTH_2 = 1

CHUNK = 64
D_MIX = D_MODEL
C_CONV = D_MIX // 4
CONV_WIDTH = 31
N_HEADS = 8
HEAD_DIM = 64
D_ATT = N_HEADS * HEAD_DIM
D_Q_LAT = 256
D_KV_LAT = 128
IDX_HEADS = 8
IDX_DIM = 64
TOPK_MAX = 256
Q_BLOCK = 128
C_POOL = D_MIX // 4
POOL_WINDOWS = (2, 4, 8, 16)
POOL_GROUP = C_POOL // 4
N_GROUPS = 4
EXPERTS_PER_GROUP = 8
N_EXPERTS = N_GROUPS * EXPERTS_PER_GROUP
D_EXPERT = 512
MOE_BLOCK = 128
EPS = 1e-6
IN_SPLITS = (C_CONV, C_CONV, D_Q_LAT, D_KV_LAT, IDX_HEADS * IDX_DIM, IDX_DIM, IDX_HEADS, C_POOL)
N_IN = sum(IN_SPLITS)


def _rmsnorm(x, g):
    xf = x.astype(jnp.float32)
    y = xf * lax.rsqrt(jnp.mean(xf * xf, axis=-1, keepdims=True) + EPS)
    return y.astype(x.dtype) * g

def _layernorm(x, g, b):
    xf = x.astype(jnp.float32)
    mu = jnp.mean(xf, axis=-1, keepdims=True)
    var = jnp.mean(jnp.square(xf - mu), axis=-1, keepdims=True)
    return ((xf - mu) * lax.rsqrt(var + EPS)).astype(x.dtype) * g + b

def _conv_module(a_val, a_gate, conv_k, conv_b, ln_g, ln_b):
    u = a_val * jax.nn.sigmoid(a_gate)
    u = lax.conv_general_dilated(
        u, conv_k[:, None, :].astype(u.dtype), window_strides=(1,),
        padding=[(CONV_WIDTH - 1, 0)], dimension_numbers=('NWC', 'WIO', 'NWC'),
        feature_group_count=C_CONV) + conv_b
    return jax.nn.silu(_layernorm(u, ln_g, ln_b))

def _dsa_attention(cq, ckv, qi, ki, wi, q_norm_g, kv_norm_g, w_uq, w_uk, w_uv):
    B, S, _ = ckv.shape
    topk = min(TOPK_MAX, S // 4)
    nb = S // Q_BLOCK
    cq = _rmsnorm(cq, q_norm_g)
    ckv = _rmsnorm(ckv, kv_norm_g)
    q = jnp.einsum('btc,chd->bthd', cq, w_uq)
    q_abs = jnp.einsum('bthd,khd->bthk', q, w_uk)
    qi = qi.reshape(B, S, IDX_HEADS, IDX_DIM)
    key_chunk = jnp.arange(S) // CHUNK
    idx_scale = (IDX_HEADS * IDX_DIM) ** -0.5
    att_scale = HEAD_DIM ** -0.5

    def to_blocks(a):
        return jnp.moveaxis(a.reshape(B, nb, Q_BLOCK, *a.shape[2:]), 1, 0)

    def block(args):
        qa, qib, wib, bi = args
        qchunk = (bi * Q_BLOCK + jnp.arange(Q_BLOCK)) // CHUNK
        allowed = key_chunk[None, :] <= qchunk[:, None]
        rel = jax.nn.relu(jnp.einsum('bqhd,bsd->bqhs', qib, ki).astype(jnp.float32))
        score = jnp.einsum('bqhs,bqh->bqs', rel, wib.astype(jnp.float32)) * idx_scale
        score = jnp.where(allowed[None], score, -jnp.inf)
        _, idx = lax.top_k(score, topk)
        kv_sel = jax.vmap(lambda a, i: a[i])(ckv, idx)
        logits = jnp.einsum('bqhc,bqkc->bqhk', qa, kv_sel).astype(jnp.float32) * att_scale
        valid = (idx // CHUNK) <= qchunk[None, :, None]
        logits = jnp.where(valid[:, :, None, :], logits, -jnp.inf)
        p = jax.nn.softmax(logits, axis=-1).astype(kv_sel.dtype)
        return jnp.einsum('bqhk,bqkc->bqhc', p, kv_sel)

    ctx = lax.map(block, (to_blocks(q_abs), to_blocks(qi), to_blocks(wi), jnp.arange(nb)))
    ctx = jnp.moveaxis(ctx, 0, 1).reshape(B, S, N_HEADS, D_KV_LAT)
    o = jnp.einsum('bthc,chd->bthd', ctx, w_uv)
    return o.reshape(B, S, D_ATT)

def _pool_mixer(u, pool_w, pool_scale):
    B, S, _ = u.shape
    n_pos = jnp.arange(1, S + 1, dtype=jnp.float32)
    outs = []
    for g, w in enumerate(POOL_WINDOWS):
        ug = u[..., g * POOL_GROUP:(g + 1) * POOL_GROUP]
        ugf = ug.astype(jnp.float32)
        cs = jnp.cumsum(ugf, axis=1)
        prev = jnp.pad(cs, ((0, 0), (w, 0), (0, 0)))[:, :S]
        mean = (cs - prev) / jnp.minimum(n_pos, w)[None, :, None]
        outs.append((mean - ugf).astype(u.dtype) @ pool_w[g])
    return jnp.concatenate(outs, axis=-1) * pool_scale

def _hier_moe(h, rg_w, rg_b, re_w, re_b, w1, w3, w2):
    B, S, D = h.shape
    T = B * S
    A = 2 * T
    hf = h.reshape(T, D)
    g_prob = jax.nn.softmax((hf @ rg_w).astype(jnp.float32) + rg_b, axis=-1)
    g_p, g_idx = lax.top_k(g_prob, 1)
    e_logits = jnp.einsum('td,dge->tge', hf, re_w).astype(jnp.float32) + re_b
    e_sel = jnp.take_along_axis(e_logits, g_idx[:, :, None], axis=1)[:, 0]
    e_p, e_idx = lax.top_k(jax.nn.softmax(e_sel, axis=-1), 2)
    e_p = e_p / jnp.sum(e_p, axis=-1, keepdims=True)
    gates = (g_p * e_p).reshape(A)
    a_exp = (g_idx * EXPERTS_PER_GROUP + e_idx).reshape(A).astype(jnp.int32)
    a_tok = jnp.repeat(jnp.arange(T, dtype=jnp.int32), 2)
    order = jnp.argsort(a_exp)
    s_exp = a_exp[order]
    counts = jnp.bincount(a_exp, length=N_EXPERTS)
    starts = jnp.cumsum(counts) - counts
    pcounts = (counts + MOE_BLOCK - 1) // MOE_BLOCK * MOE_BLOCK
    pends = jnp.cumsum(pcounts)
    pstarts = pends - pcounts
    dst = pstarts[s_exp] + jnp.arange(A) - starts[s_exp]
    n_blk = -(-(A + N_EXPERTS * (MOE_BLOCK - 1)) // MOE_BLOCK)
    P = n_blk * MOE_BLOCK
    slot_tok = jnp.zeros((P,), jnp.int32).at[dst].set(a_tok[order])
    slot_gate = jnp.zeros((P,), jnp.float32).at[dst].set(gates[order])
    blk_exp = jnp.minimum(jnp.searchsorted(pends, jnp.arange(n_blk) * MOE_BLOCK, side='right'), N_EXPERTS - 1)

    def run(args):
        tok, e = args
        hb = hf[tok]
        return (jax.nn.silu(hb @ w1[e]) * (hb @ w3[e])) @ w2[e]

    y = lax.map(run, (slot_tok.reshape(n_blk, MOE_BLOCK), blk_exp)).reshape(P, D)
    out = jnp.zeros((T, D), h.dtype).at[slot_tok].add(y * slot_gate[:, None].astype(y.dtype))
    return out.reshape(B, S, D)

def second_inputs(seed: int = 0) -> dict:
    key = jax.random.key(seed)
    ks = jax.random.split(key, 27)

    def nrm(k, shape, scale):
        return jax.random.normal(k, shape, jnp.float32) * scale

    L = DEPTH_2
    return {
        'x': nrm(ks[0], (BATCH, SEQ, D_MODEL), 1.0),
        'c': nrm(ks[1], (BATCH, D_MODEL), 1.0),
        'mod_w': nrm(ks[2], (L, D_MODEL, 6 * D_MODEL), 0.5 * D_MODEL ** -0.5),
        'mod_b': nrm(ks[3], (L, 6 * D_MODEL), 0.1),
        'norm1_g': 1.0 + nrm(ks[4], (L, D_MODEL), 0.05),
        'w_in': nrm(ks[5], (L, D_MODEL, N_IN), D_MODEL ** -0.5),
        'conv_k': nrm(ks[6], (L, CONV_WIDTH, C_CONV), CONV_WIDTH ** -0.5),
        'conv_b': nrm(ks[7], (L, C_CONV), 0.02),
        'conv_ln_g': 1.0 + nrm(ks[8], (L, C_CONV), 0.05),
        'conv_ln_b': nrm(ks[9], (L, C_CONV), 0.02),
        'q_norm_g': 1.0 + nrm(ks[10], (L, D_Q_LAT), 0.05),
        'kv_norm_g': 1.0 + nrm(ks[11], (L, D_KV_LAT), 0.05),
        'w_uq': nrm(ks[12], (L, D_Q_LAT, N_HEADS, HEAD_DIM), D_Q_LAT ** -0.5),
        'w_uk': nrm(ks[13], (L, D_KV_LAT, N_HEADS, HEAD_DIM), D_KV_LAT ** -0.5),
        'w_uv': nrm(ks[14], (L, D_KV_LAT, N_HEADS, HEAD_DIM), D_KV_LAT ** -0.5),
        'pool_w': nrm(ks[15], (L, len(POOL_WINDOWS), POOL_GROUP, POOL_GROUP), POOL_GROUP ** -0.5),
        'pool_scale': 1.0 + nrm(ks[16], (L, C_POOL), 0.1),
        'w_out': nrm(ks[17], (L, D_MIX, D_MODEL), D_MIX ** -0.5),
        'norm2_g': 1.0 + nrm(ks[18], (L, D_MODEL), 0.05),
        'router_g_w': nrm(ks[19], (L, D_MODEL, N_GROUPS), D_MODEL ** -0.5),
        'router_g_b': nrm(ks[20], (L, N_GROUPS), 0.01),
        'router_e_w': nrm(ks[21], (L, D_MODEL, N_GROUPS, EXPERTS_PER_GROUP), D_MODEL ** -0.5),
        'router_e_b': nrm(ks[22], (L, N_GROUPS, EXPERTS_PER_GROUP), 0.01),
        'exp_w1': nrm(ks[23], (L, N_EXPERTS, D_MODEL, D_EXPERT), D_MODEL ** -0.5),
        'exp_w3': nrm(ks[24], (L, N_EXPERTS, D_MODEL, D_EXPERT), D_MODEL ** -0.5),
        'exp_w2': nrm(ks[25], (L, N_EXPERTS, D_EXPERT, D_MODEL), D_EXPERT ** -0.5),
        'final_g': 1.0 + nrm(ks[26], (D_MODEL,), 0.05),
    }

def second_block(x, c, mod_w, mod_b, norm1_g, w_in, conv_k, conv_b, conv_ln_g, conv_ln_b,
              q_norm_g, kv_norm_g, w_uq, w_uk, w_uv, pool_w, pool_scale, w_out, norm2_g,
              router_g_w, router_g_b, router_e_w, router_e_b, exp_w1, exp_w3, exp_w2, final_g):
    cond = jax.nn.silu(c)
    split_at = np.cumsum(IN_SPLITS)[:-1].tolist()
    for l in range(DEPTH_2):
        mod = cond @ mod_w[l] + mod_b[l]
        sh1, sc1, g1, sh2, sc2, g2 = [m[:, None, :] for m in jnp.split(mod, 6, axis=-1)]
        h = _rmsnorm(x, norm1_g[l]) * (1 + sc1) + sh1
        z = h @ w_in[l]
        a_val, a_gate, cq, ckv, qi, ki, wi, u_pool = jnp.split(z, split_at, axis=-1)
        y_conv = _conv_module(a_val, a_gate, conv_k[l], conv_b[l], conv_ln_g[l], conv_ln_b[l])
        y_att = _dsa_attention(cq, ckv, qi, ki, wi, q_norm_g[l], kv_norm_g[l], w_uq[l], w_uk[l], w_uv[l])
        y_pool = _pool_mixer(u_pool, pool_w[l], pool_scale[l])
        mix = jnp.concatenate([y_conv, y_att, y_pool], axis=-1) @ w_out[l]
        x = x + g1 * mix
        h = _rmsnorm(x, norm2_g[l]) * (1 + sc2) + sh2
        x = x + g2 * _hier_moe(h, router_g_w[l], router_g_b[l], router_e_w[l], router_e_b[l],
                               exp_w1[l], exp_w3[l], exp_w2[l])
    return _rmsnorm(x, final_g)


def setup_inputs(seed=0):
    out = dict(first_inputs(seed))
    for name, value in second_inputs(seed + 1).items():
        if name != "x":
            out[name + "_2"] = value
    return out


def reference(
    x, p, attn_norm, mlp_norm, w_in_ar, w_out_ar, hgrn_lb, hgrn_onorm, rwkv_mu, rwkv_w0,
    rwkv_w2, rwkv_a0, rwkv_a2, rwkv_g2, rwkv_kk, rwkv_ka, rwkv_rk, rwkv_ln_w, rwkv_ln_b, w_qkv,
    w_o_attn, q_norm, k_norm, w_up, w_down, ple_proj, ple_norm, ple_gate, c_2, mod_w_2, mod_b_2,
    norm1_g_2, w_in_2, conv_k_2, conv_b_2, conv_ln_g_2, conv_ln_b_2, q_norm_g_2, kv_norm_g_2,
    w_uq_2, w_uk_2, w_uv_2, pool_w_2, pool_scale_2, w_out_2, norm2_g_2, router_g_w_2,
    router_g_b_2, router_e_w_2, router_e_b_2, exp_w1_2, exp_w3_2, exp_w2_2, final_g_2,
):
    x = first_block(
        x, p, attn_norm, mlp_norm, w_in_ar, w_out_ar, hgrn_lb, hgrn_onorm, rwkv_mu, rwkv_w0,
        rwkv_w2, rwkv_a0, rwkv_a2, rwkv_g2, rwkv_kk, rwkv_ka, rwkv_rk, rwkv_ln_w, rwkv_ln_b,
        w_qkv, w_o_attn, q_norm, k_norm, w_up, w_down, ple_proj, ple_norm, ple_gate,
    )
    return second_block(
        x, c_2, mod_w_2, mod_b_2, norm1_g_2, w_in_2, conv_k_2, conv_b_2, conv_ln_g_2,
        conv_ln_b_2, q_norm_g_2, kv_norm_g_2, w_uq_2, w_uk_2, w_uv_2, pool_w_2, pool_scale_2,
        w_out_2, norm2_g_2, router_g_w_2, router_g_b_2, router_e_w_2, router_e_b_2, exp_w1_2,
        exp_w3_2, exp_w2_2, final_g_2,
    )


_drawn_inputs = setup_inputs


def setup_inputs(seed=0):
    import zlib

    import numpy as np

    out = dict(_drawn_inputs(seed))
    spreads = {}
    factors = {'hgrn_lb': 3.672,
     'hgrn_onorm': 2.802,
     'rwkv_w2': 8.0,
     'rwkv_a2': 3.958,
     'rwkv_kk': 8.0,
     'rwkv_ka': 2.883,
     'rwkv_ln_w': 3.048,
     'rwkv_ln_b': 6.899,
     'q_norm': 8.0,
     'k_norm': 8.0,
     'norm1_g_2': 8.0,
     'conv_b_2': 8.0,
     'conv_ln_g_2': 8.0,
     'conv_ln_b_2': 8.0,
     'q_norm_g_2': 8.0,
     'kv_norm_g_2': 8.0,
     'w_uq_2': 3.973,
     'w_uk_2': 3.839,
     'pool_scale_2': 7.923,
     'norm2_g_2': 6.173,
     'router_g_b_2': 8.0,
     'router_e_b_2': 8.0}
    for name, (base, spread) in spreads.items():
        noise = np.random.default_rng([zlib.crc32(name.encode()), seed]).standard_normal(out[name].shape)
        drawn = base * np.exp(spread * noise) if base else spread * noise
        out[name] = jnp.asarray(drawn.astype(out[name].dtype))
    for name, factor in factors.items():
        out[name] = (out[name] * factor).astype(out[name].dtype)
    return out
```

```python
from contextlib import ExitStack

import numpy as np

import concourse.bass as bass
from concourse import mybir

P = 128
ALU = mybir.AluOpType
ACT = mybir.ActivationFunctionType
F32 = mybir.dt.float32
I32 = mybir.dt.int32
AX = mybir.AxisListType

D = 1024
S = 256
NT = S // P
KC = D // P
D_FF = 4 * D
FC = D_FF // P
HG_HEADS = 4
RW_HEADS = 8
RW_PAIRS = RW_HEADS // 2
HEADS = 8
PLE = 256
N_EXP = 32
D_EXP = 512
EC = D_EXP // P
EPS = 1e-6
LN_EPS = 64e-5
NEG = -1e30
TAPS = 31
DECAY_SCALE = -float(np.exp(-0.5))
UNIT = 4096
SLOTS = 3
LEVELS = [1, 2, 4, 8, 16, 32, 64]
LAG = 4

CONST_WIDTHS = [
    ("ident", P), ("level", P * len(LEVELS)), ("strict", P), ("upto", P), ("ones", P), ("pairs", P),
    ("cos", NT * 64), ("sin", NT * 64), ("causal", S), ("allowed", NT * S), ("pool_inv", 2 * S),
    ("first", 8), ("eps", 1), ("ln_eps", 1), ("zero", P),
]

VECS1 = [
    ("attn_norm", 16), ("mlp_norm", 16), ("hgrn_lb", 12), ("hgrn_onorm", 4), ("rwkv_mu", 14), ("rwkv_w0", 4),
    ("rwkv_a0", 4), ("rwkv_kk", 4), ("rwkv_ka", 4), ("rwkv_rk", 4), ("rwkv_ln_w", 4), ("rwkv_ln_b", 4),
]
VECS2 = [
    ("mod_b_2", 48), ("norm1_g_2", 8), ("norm2_g_2", 8), ("conv_b_2", 2), ("conv_ln_g_2", 2), ("conv_ln_b_2", 2),
    ("q_norm_g_2", 2), ("pool_scale_2", 2), ("c_2", 8),
]
ROWS = [("q_norm", 128), ("k_norm", 128), ("kv_norm_g_2", 128), ("router_g_b_2", 4), ("router_e_b_2", 32)]


def offsets(table):
    at, out = 0, {}
    for name, width in table:
        out[name] = (at, at + width)
        at += width
    return out, at


def constants():
    at, n = offsets(CONST_WIDTHS)
    c = np.zeros((P, n), np.float32)

    def put(name, value):
        s, e = at[name]
        c[:, s:e] = value

    s_, t_ = np.arange(P)[:, None], np.arange(P)[None, :]
    put("ident", np.eye(P))
    put("level", np.concatenate(
        [(s_ // (2 * m) == t_ // (2 * m)) & (s_ // m % 2 == 0) & (t_ // m % 2 == 1) for m in LEVELS], axis=1))
    put("strict", s_ < t_)
    put("upto", s_ <= t_)
    put("ones", 1.0)
    put("pairs", s_ // 64 == t_ // 64)
    half = 64
    inv = np.power(np.float32(10000.0), -np.arange(half, dtype=np.float32) / half).astype(np.float32)
    ang = np.arange(S, dtype=np.float32)[:, None] * inv[None, :]
    put("cos", np.cos(ang).reshape(NT, P, half).transpose(1, 0, 2).reshape(P, -1))
    put("sin", np.sin(ang).reshape(NT, P, half).transpose(1, 0, 2).reshape(P, -1))
    put("causal", np.concatenate([np.zeros((P, P)), np.where(t_ <= s_, 0.0, NEG)], axis=1))
    q = np.arange(S).reshape(NT, P)
    ok = np.arange(S)[None, None, :] // 64 <= q[:, :, None] // 64
    put("allowed", np.where(ok, 0.0, NEG).transpose(1, 0, 2).reshape(P, -1))
    windows = np.array([[2, 8], [4, 16]])[(np.arange(P) // 64)]
    put("pool_inv", (1.0 / np.minimum(np.arange(1, S + 1)[None, None, :], windows[:, :, None])).reshape(P, -1))
    put("first", 8.0 - np.arange(8))
    put("eps", EPS)
    put("ln_eps", LN_EPS)
    return c


class Bank:

    def __init__(self, ap, full, freed, use):
        self.ap, self.full, self.freed, self.use = ap, full, freed, use


class Banks:

    def __init__(self, aps, full, freed):
        self.aps, self.full, self.freed, self.n, self.uses = aps, full, freed, 0, {}

    def take(self, pe, *name):
        b = self.n % len(self.aps)
        use = self.n // len(self.aps)
        self.n += 1
        assert name not in self.uses, name
        self.uses[name] = Bank(self.aps[b], self.full[b], self.freed[b], use)
        if use:
            pe.wait_ge(self.freed[b], use)
        return self.uses[name]

    def read(self, eng, *name):
        bank = self.uses[name]
        eng.wait_ge(bank.full, bank.use + 1)
        return bank

    def wait_read(self, eng, *name):
        bank = self.uses[name]
        eng.wait_ge(bank.freed, bank.use + 1)


class Chain:

    def __init__(self, eng, sem):
        self.eng, self.sem, self.n = eng, sem, 0

    def __call__(self, ins):
        ins.then_inc(self.sem, 1)
        self.n += 1
        self.eng.wait_ge(self.sem, self.n)


def kcn(w):
    return w.rearrange("(k p) n -> p k n", p=P)


def weight_units(a):
    units = []

    def grid(lo, k, n):
        return lambda s: s[:, lo:lo + k * n].rearrange("p (k n) -> p k n", k=k)

    def whole(name, w, n, width=512):
        for c in range(n):
            units.append(((*name, c), [(grid(0, KC, width), kcn(w[:, c * width:(c + 1) * width]))]))

    whole(("w_in",), a["w_in_ar"][0], 7)
    units.append((("w_in", 7), [(grid(0, KC, 256), kcn(a["w_in_ar"][0][:, 3584:3840]))]))
    units.append((("lora",), [(lambda s: s[0:64, 0:512], a["rwkv_w2"][0]),
                              (lambda s: s[64:128, 0:512], a["rwkv_a2"][0]),
                              (lambda s: s[:, 512:1024], a["rwkv_g2"][0])]))
    whole(("mod",), a["mod_w_2"][0], 12)
    whole(("w_out",), a["w_out_ar"][0], 2)

    def mlp(l):
        whole(("up", l), a["w_up"][l], 8)
        for n in range(2):
            for k in range(4):
                part = kcn(a["w_down"][l][k * D:(k + 1) * D, n * 512:(n + 1) * 512])
                units.append((("down", l, n, k), [(grid(0, KC, 512), part)]))
        units.append((("ple", l), [(grid(0, 2, D), kcn(a["ple_proj"][l]))]))
        whole(("gate", l), a["ple_gate"][l], 2)

    mlp(0)
    whole(("qkv",), a["w_qkv"][0], 6)
    whole(("w_o",), a["w_o_attn"][0], 2)
    mlp(1)
    w = kcn(a["w_in_2"][0])
    units.append((("in2", 0), [(grid(0, KC, 512), w[:, :, 0:512])]))
    units.append((("in2", 1), [(grid(0, KC, 384), w[:, :, 512:896])]))
    units.append((("in2", 2), [(grid(0, KC, 512), w[:, :, 896:1408])]))
    twice = lambda d: lambda s: s[:, 0:KC * P].rearrange("p (k d n) -> p k d n", k=KC, d=2)[:, :, d, :]
    units.append((("in2", 3), [(twice(0), w[:, :, 1408:1472]), (twice(1), w[:, :, 1408:1472]),
                               (grid(KC * P, KC, 256), w[:, :, 1480:1736]),
                               (grid(KC * 384, KC, 8), w[:, :, 1472:1480])]))
    units.append((("dsa",), [
        (grid(0, 2, 512), a["w_uq_2"][0].rearrange("(k p) h d -> p k (h d)", p=P)),
        (lambda s: s[:, 1024:1536], a["w_uk_2"][0].rearrange("p h d -> p (h d)")),
        (lambda s: s[:, 1536:2048], a["w_uv_2"][0].rearrange("p h d -> p (h d)")),
        (grid(2048, 2, 64), a["pool_w_2"][0].rearrange("(c g) i o -> (g i) c o", c=2)),
        (lambda s: s[0:TAPS, 2176:2432], a["conv_k_2"][0]),
    ]))
    whole(("w_out2",), a["w_out_2"][0], 2)
    return units


def build(nc, a, out, stop=99):
    ctx = ExitStack()
    with ctx:
        def sb(name, cols, dt=F32):
            return ctx.enter_context(nc.sbuf_tensor(name, [P, cols], dt))

        cols_at, n_const = offsets(CONST_WIDTHS)
        v1_at, n_v1 = offsets(VECS1)
        v2_at, n_v2 = offsets(VECS2)
        rows_at, n_rows = offsets(ROWS)

        const = sb("const", n_const)
        rows = sb("rows", n_rows)
        vec = sb("vec", 2 * P)
        x = sb("x", NT * D)
        xn = sb("xn", NT * D)
        hT = sb("hT", KC * S)
        ring = sb("ring", SLOTS * UNIT)
        arena = sb("arena", 27 * 1024)
        big_row_t = sb("big_row", D)
        small = sb("small", 768)
        router = sb("router", KC * 36)
        big_row = big_row_t[:, :]
        gates_dram = nc.dram_tensor("gates_scratch", [N_EXP, S], F32, kind="Internal").ap()

        sems = {}

        def sem(name):
            if name not in sems:
                sems[name] = ctx.enter_context(nc.semaphore(name))
            return sems[name]

        banks_mem = [ctx.enter_context(nc.psum_tensor(f"bank{i}", [P, 512], F32)) for i in range(8)]
        bank_aps = [b[:, :] for b in banks_mem]
        banks = Banks(bank_aps, [sem(f"bank_full{i}") for i in range(8)], [sem(f"bank_freed{i}") for i in range(8)])

        def c_(name, lo=0, hi=None):
            s, e = cols_at[name]
            return const[:, s + lo:(e if hi is None else s + hi)]

        ident, ones, pairs = c_("ident"), c_("ones"), c_("pairs")
        zeros = c_("zero")

        def level_mask(m):
            i = LEVELS.index(m)
            return c_("level", i * P, (i + 1) * P)

        def v1(name, i, n=1):
            s = v1_at[name][0] + i
            return vec[:, s:s + n]

        def v2(name, i, n=1):
            s = P + v2_at[name][0] + i
            return vec[:, s:s + n]

        def row(name, lo=0, hi=None):
            s, e = rows_at[name]
            return rows[:, s + lo:(e if hi is None else s + hi)]

        small_used = [0]

        def tiny(n):
            at = small_used[0]
            small_used[0] += n
            assert small_used[0] <= 768
            return small[:, at:at + n]

        def page(i, n=1):
            return arena[:, i * 1024:(i + n) * 1024]

        def half(i, n=1):
            return arena[:, i * 512:(i + n) * 512]

        def blocks(ap, j):
            return ap.rearrange("p (j t) -> p j t", j=j)

        def mid(ap, n):
            return ap.unsqueeze(1).to_broadcast([ap.shape[0], n, ap.shape[1]])

        def tail(ap, w):
            return ap.unsqueeze(2).to_broadcast([ap.shape[0], ap.shape[1], w])

        x3, xn3, hT3 = blocks(x[:, :], NT), blocks(xn[:, :], NT), blocks(hT[:, :], KC)
        vec_rows = page(26)[:, 0:2 * P]

        raw = arena[:, 0:14 * 257].rearrange("p (b t) -> p b t", b=14)
        mixed = page(4, 4)
        r_mix, k_mix, logdec, kk = (blocks(page(i), 4) for i in (4, 5, 6, 7))
        v_mix, low = blocks(page(8), 4), blocks(half(18), 2)
        a_gate, g_out, cum, k_adj = (blocks(page(i), 4) for i in (10, 11, 12, 13))
        ar = page(14, 2).rearrange("p (j t a s) -> p j t a s", j=4, t=NT, a=2)
        b_til, k_til, bonus = (blocks(page(i), 4) for i in (16, 17, 18))
        v_tok = blocks(page(19), NT)
        bk_tok = page(20).rearrange("p (b j s) -> p b j s", b=2, j=4)
        y_tok = blocks(page(21), NT)
        w_sb, sa_sb = half(44), half(45)
        ab = page(23, 4).rearrange("p (i a s) -> p i a s", i=16, a=2)
        ak = page(4, 4).rearrange("p (i a s) -> p i a s", i=16, a=2)
        inv, invT = blocks(page(0, 2), 16), blocks(page(2, 2), 16)
        a_inv = blocks(xn[:, :], 16)
        s1 = arena[:, 19 * 512:19 * 512 + 256].rearrange("p (j v) -> p j v", j=4)
        hq, hk, hf, hgT = (blocks(page(i), 4) for i in (13, 14, 15, 16))
        hv = blocks(page(17), NT)
        h_end = [page(18), page(22)]
        st = page(19).rearrange("p (t h s) -> p t h s", t=NT, h=4)
        sx = blocks(half(40), 4)
        o_a, o_sq = blocks(page(21), NT), blocks(page(23), NT)

        q_tok, k_tok, v_att = (blocks(page(i, 2), NT) for i in (0, 2, 4))
        qT, kT = blocks(page(6, 2), HEADS), blocks(page(8, 2), HEADS)
        rot, sq = page(10, 2), page(12, 2)
        prob, probT = blocks(page(14, 2), 8), page(16).rearrange("p (b k q) -> p b k q", b=4, k=2)

        actT = blocks(page(0, 8), FC)
        relu = blocks(page(8, 2), 4)
        p_tok, pT = blocks(half(40), NT), blocks(half(41), 2)
        ple_raw, gate_s = blocks(page(21, 2), NT), blocks(page(23, 2), NT)

        u_pad = arena[:, 0:2 * (S + TAPS - 1)].rearrange("p (c t) -> p c t", c=2)
        conv_acc, conv_sq, sig_gate = blocks(half(2), 2), blocks(half(3), 2), blocks(half(4), 2)
        conv_col = half(5)[:, 0:2 * TAPS].rearrange("p (c k) -> p c k", c=2)
        conv_m = blocks(half(6), 2)
        cq_tok = page(4)[:, 0:768].rearrange("p (t n) -> p t n", t=NT)
        cqT = blocks(half(10), 2)
        ckvT, ckv_tok = page(5)[:, 512:768], blocks(page(5)[:, 768:1024], NT)
        qiT = blocks(page(6), 4)
        kiT, wi = page(7)[:, 0:256], page(7)[:, 256:272].rearrange("p (t h) -> p t h", t=NT)
        cq_sq = page(7)[:, 272:656]
        w_ukT, pool_d = blocks(half(16), 4), blocks(half(17), 2)
        pool_s = [arena[:, i * 1024:i * 1024 + 2 * (S + 16)].rearrange("p (c t) -> p c t", c=2) for i in (9, 10, 11)]
        q2T, q_abs = blocks(page(12), 4), blocks(page(13, 2), 8)
        score, work = blocks(half(30), NT), blocks(half(31), NT)
        rel = blocks(page(16, 2), 8)
        bias2 = blocks(half(36), NT)
        prob2, probT2 = blocks(page(19, 2), 8), page(21).rearrange("p (b k q) -> p b k q", b=4, k=2)
        ctxT = blocks(page(22, 2), 8)
        yT = hT3
        diag = blocks(page(16, 2), 16)
        g1_row, g2_row = page(25), page(26)
        scaled = half(48)

        gate_all = blocks(page(0, 8), N_EXP)
        exp_act, exp_silu = blocks(page(8), EC), blocks(page(9), EC)
        gT = arena[0:N_EXP, 10 * 1024:10 * 1024 + S]

        ssq, ssq2, rstd, flags = tiny(NT), tiny(NT), tiny(NT), tiny(24)
        lb_d, lb_e, lb, lb_c = tiny(12), tiny(12), tiny(4), tiny(4)
        hg_ss, rw_mu, rw_ss = tiny(8), tiny(16), tiny(16)
        c_mid, c_end, s_scale = tiny(8), tiny(8), tiny(4)
        head_ss = tiny(16)
        nmax, rsum, rinv = tiny(16), tiny(16), tiny(16)
        cond, modc = tiny(8), tiny(48)
        sc1, sc2 = tiny(8), tiny(8)
        cs = tiny(4)
        top8 = tiny(8)
        lg = tiny(72).rearrange("p (t n) -> p t n", t=NT)
        rt = [tiny(64) for _ in range(4)]
        gates = tiny(64).rearrange("p (t n) -> p t n", t=NT)

        units = weight_units(a)
        unit_of = {name: i for i, (name, _) in enumerate(units)}
        landed_value, slot_total = {}, [0] * SLOTS
        for i, (name, parts) in enumerate(units):
            slot_total[i % SLOTS] += 16 * len(parts)
            landed_value[name] = slot_total[i % SLOTS]
        landed = [sem(f"slot_landed{i}") for i in range(SLOTS)]
        unit_read = {}

        def slot(name):
            s = unit_of[name] % SLOTS
            return ring[:, s * UNIT:(s + 1) * UNIT]

        def weights(pe, *name):
            pe.wait_ge(landed[unit_of[name] % SLOTS], landed_value[name])
            return slot(name)

        def read_by(bank, *name):
            unit_read[name] = (bank.full, bank.use + 1)

        block = ctx.enter_context(nc.Block())

        @block.tensor
        def _(pe):
            mm = nc.tensor.matmul

            def transposes(pairs_, bank):
                for dst, src in pairs_:
                    last = nc.tensor.transpose(dst, src, ident[0:src.shape[0], 0:src.shape[0]])
                last.then_inc(bank.full, 1)

            def norm_turn(tag, count, source=None):
                src = xn3 if source is None else source
                for c in range(KC // 2):
                    bank = banks.take(pe, tag, c)
                    if c == 0 and count:
                        pe.wait_ge(sem("normed"), NT * count)
                    transposes([(bank.ap[:, i * S + t * P:i * S + (t + 1) * P],
                                 src[:, t, (2 * c + i) * P:(2 * c + i + 1) * P])
                                for i in range(2) for t in range(NT)], bank)

            def turned(tag):
                for c in range(KC // 2):
                    banks.wait_read(pe, tag, c)

            def to_features(tag, w, act, kcs, cols):
                for c in range(0, len(cols), 2):
                    bank = banks.take(pe, *tag, c // 2)
                    for i, m in enumerate(cols[c:c + 2]):
                        for k in range(kcs):
                            last = mm(bank.ap[:, i * S:(i + 1) * S], w[:, k, m:m + P], act[:, k, :],
                                      start=(k == 0), stop=(k == kcs - 1))
                    last.then_inc(bank.full, 1)
                return bank

            def to_tokens(tag, w, act, kcs, n):
                for t in range(NT):
                    bank = banks.take(pe, *tag, t)
                    for k in range(kcs):
                        last = mm(bank.ap[:, 0:n], act[:, k, t * P:(t + 1) * P], w[:, k, 0:n],
                                  start=(k == 0), stop=(k == kcs - 1))
                    last.then_inc(bank.full, 1)
                return bank

            def token_units(tag, count, act):
                for c in range(count):
                    w = blocks(weights(pe, *tag, c), KC)
                    read_by(to_tokens((*tag, c), w, act, KC, 512), *tag, c)

            four = [i * P for i in range(4)]

            pe.wait_ge(sem("const_landed"), 16)
            pe.wait_ge(sem("vec_zero"), 1)
            pe.wait_ge(sem("vecs_landed"), 16 * (len(VECS1) + len(VECS2)))
            bank = banks.take(pe, "vec")
            transposes([(bank.ap[:, i * P:(i + 1) * P], vec_rows[:, i * P:(i + 1) * P]) for i in range(2)], bank)
            norm_turn("h_mix", 1)
            turned("h_mix")
            for c in range(8):
                w = weights(pe, "w_in", c)
                if c == 2:
                    bank = to_tokens(("hi",), blocks(w, KC), hT3, KC, 512)
                elif c < 7:
                    bank = to_features(("in", c), blocks(w, KC), hT3, KC, four)
                else:
                    bank = to_features(("in", c), blocks(w[:, 0:KC * 256], KC), hT3, KC, four[:2])
                read_by(bank, "w_in", c)

            if stop < 1:
                return
            lora = weights(pe, "lora")
            pe.wait_ge(sem("low_ready"), 1)
            for tag, p0, col, b in (("lw", 0, 0, 0), ("la", 64, 0, 0), ("lg", 0, 512, 1)):
                p1 = P if tag != "lw" else 64
                for c in range(2):
                    bank = banks.take(pe, tag, c)
                    for i in range(2):
                        m = col + (2 * c + i) * P
                        last = mm(bank.ap[:, i * S:(i + 1) * S], lora[p0:p1, m:m + P], low[p0:p1, b, :],
                                  start=True, stop=True)
                    last.then_inc(bank.full, 1)
            read_by(bank, "lora")

            for i, m in enumerate([0] + LEVELS):
                pe.wait_ge(sem("hgrn_scaled"), i + 1)
                for t in range(NT):
                    bank = banks.take(pe, "hs", m, t)
                    for h in range(HG_HEADS):
                        last = mm(bank.ap[:, h * P:(h + 1) * P], hk[:, h, t * P:(t + 1) * P],
                                  hq[:, h, t * P:(t + 1) * P], start=True, stop=True)
                    last.then_inc(bank.full, 1)
            pe.wait_ge(sem("hgrn_scaled"), len(LEVELS) + 2)
            bank = banks.take(pe, "hs", P)
            for h in range(HG_HEADS):
                last = mm(bank.ap[:, h * P:(h + 1) * P], hk[:, h, 0:P], hq[:, h, P:S], start=True, stop=True)
            last.then_inc(bank.full, 1)
            for t in range(NT):
                banks.wait_read(pe, "hi", t)
            banks.wait_read(pe, "hs", LEVELS[-1], 0)
            banks.wait_read(pe, "hs", LEVELS[-1], 1)
            banks.wait_read(pe, "hs", P)
            for t in range(NT):
                bank = banks.take(pe, "ho", t)
                for h in range(HG_HEADS):
                    col = slice(h * P, (h + 1) * P)
                    last = mm(bank.ap[:, col], st[:, t, h, :], hv[:, t, col], start=True, stop=(t == 0))
                    if t:
                        last = mm(bank.ap[:, col], sx[:, h, :], hv[:, 0, col], start=False, stop=True)
                last.then_inc(bank.full, 1)
            pe.wait_ge(sem("hgrn_normed"), 1)
            for c in range(2):
                bank = banks.take(pe, "ha", c)
                transposes([(bank.ap[:, i * S + t * P:i * S + (t + 1) * P], o_a[:, t, (2 * c + i) * P:(2 * c + i + 1) * P])
                            for i in range(2) for t in range(NT)], bank)

            if stop < 2:
                return
            pe.wait_ge(sem("kk_sq"), 1)
            for c in range(2):
                bank = banks.take(pe, "kk", c)
                mm(bank.ap[:, :], pairs, page(21)[:, c * 512:(c + 1) * 512], start=True, stop=True).then_inc(bank.full, 1)
            for t in range(NT):
                bank = banks.take(pe, "vt", t)
                transposes([(bank.ap[:, j * P:(j + 1) * P], v_mix[:, j, t * P:(t + 1) * P]) for j in range(4)], bank)
            pe.wait_ge(sem("rk_prod"), 1)
            for c in range(2):
                bank = banks.take(pe, "bonus", c)
                mm(bank.ap[:, :], pairs, page(22)[:, c * 512:(c + 1) * 512], start=True, stop=True).then_inc(bank.full, 1)
            pe.wait_ge(sem("tilded"), 1)
            for b, src in enumerate((b_til, k_til)):
                bank = banks.take(pe, "bk", b)
                transposes([(bank.ap[:, j * P:(j + 1) * P], src[:, j, 0:P]) for j in range(4)], bank)
            for i in range(16):
                t, h = i // 8, i % 8
                j, rows_ = h // 2, slice(64 * (h % 2), 64 * (h % 2) + 64)
                bank = banks.take(pe, "pairs", i)
                for b, src in enumerate((b_til, k_til)):
                    last = mm(bank.ap[:, b * S:(b + 1) * S], src[rows_, j, t * P:(t + 1) * P],
                              ar[rows_, j, t, :, :], start=True, stop=True)
                last.then_inc(bank.full, 1)
            pe.wait_ge(sem("inv_first"), 1)
            for g in range(4):
                bank = banks.take(pe, "x", 1, g)
                transposes([(bank.ap[:, i * P:(i + 1) * P], invT[:, 4 * g + i, :]) for i in range(4)], bank)
            for n, m in enumerate(LEVELS[1:]):
                for g in range(4):
                    banks.wait_read(pe, "x", LEVELS[n], g)
                    bank = banks.take(pe, "ax", m, g)
                    for i in range(4):
                        last = mm(bank.ap[:, i * P:(i + 1) * P], ab[:, 4 * g + i, 0, :], inv[:, 4 * g + i, :],
                                  start=True, stop=True)
                    last.then_inc(bank.full, 1)
                for g in range(4):
                    banks.wait_read(pe, "ax", m, g)
                    bank = banks.take(pe, "xax", m, g)
                    for i in range(4):
                        last = mm(bank.ap[:, i * P:(i + 1) * P], a_inv[:, 4 * g + i, :], invT[:, 4 * g + i, :],
                                  start=True, stop=True)
                    last.then_inc(bank.full, 1)
                if m != LEVELS[-1]:
                    for g in range(4):
                        banks.wait_read(pe, "xax", m, g)
                        bank = banks.take(pe, "x", m, g)
                        transposes([(bank.ap[:, i * P:(i + 1) * P], invT[:, 4 * g + i, :]) for i in range(4)], bank)
            for g in range(4):
                banks.wait_read(pe, "xax", LEVELS[-1], g)
            for t in range(NT):
                for half_ in range(2):
                    rows_ = slice(64 * half_, 64 * half_ + 64)
                    bank = banks.take(pe, "w", t, half_)
                    for j in range(RW_PAIRS):
                        col, h = slice(j * 64, (j + 1) * 64), 2 * j + half_
                        last = mm(bank.ap[:, col], ak[:, 8 * t + h, 0, :], v_tok[:, t, h * 64:(h + 1) * 64],
                                  start=True, stop=(t == 0))
                        if t:
                            last = mm(bank.ap[:, col], ar[rows_, j, t, 0, :], s1[rows_, j, :], start=False, stop=True)
                    last.then_inc(bank.full, 1)
                for half_ in range(2):
                    banks.wait_read(pe, "w", t, half_)
                bank = banks.take(pe, "sa", t)
                for h in range(RW_HEADS):
                    col = slice(h * 64, (h + 1) * 64)
                    last = mm(bank.ap[:, col], invT[:, 8 * t + h, :], w_sb[:, col], start=True, stop=True)
                last.then_inc(bank.full, 1)
                banks.wait_read(pe, "sa", t)
                if t == 0:
                    bank = banks.take(pe, "state")
                    for j in range(4):
                        col = slice(j * P, (j + 1) * P)
                        mm(bank.ap[:, col], bk_tok[:, 0, j, :], sa_sb[:, col], start=True, stop=False)
                        last = mm(bank.ap[:, col], bk_tok[:, 1, j, :], v_tok[:, 0, col], start=False, stop=True)
                    last.then_inc(bank.full, 1)
                for half_ in range(2):
                    rows_ = slice(64 * half_, 64 * half_ + 64)
                    bank = banks.take(pe, "y", t, half_)
                    for j in range(RW_PAIRS):
                        col, h = slice(j * 64, (j + 1) * 64), 2 * j + half_
                        own = slice(h * 64, (h + 1) * 64)
                        mm(bank.ap[:, col], ab[:, 8 * t + h, 1, :], sa_sb[:, own], start=True, stop=False)
                        last = mm(bank.ap[:, col], ak[:, 8 * t + h, 1, :], v_tok[:, t, own],
                                  start=False, stop=(t == 0))
                        if t:
                            last = mm(bank.ap[:, col], ar[rows_, j, t, 1, :], s1[rows_, j, :], start=False, stop=True)
                    last.then_inc(bank.full, 1)
                if t == 0:
                    pe.wait_ge(sem("state_ready"), 1)
                    banks.wait_read(pe, "state")
            pe.wait_ge(sem("rwkv_normed"), 1)
            for c in range(2):
                bank = banks.take(pe, "yb", c)
                transposes([(bank.ap[:, i * S + t * P:i * S + (t + 1) * P], y_tok[:, t, (2 * c + i) * P:(2 * c + i + 1) * P])
                            for i in range(2) for t in range(NT)], bank)

            if stop < 3:
                return
            pe.wait_ge(sem("cond_ready"), 1)
            bank = banks.take(pe, "mod")
            for c in range(12):
                w = blocks(weights(pe, "mod", c), KC)
                for i in range(4):
                    for k in range(KC):
                        last = mm(bank.ap[:, 4 * c + i:4 * c + i + 1], w[:, k, i * P:(i + 1) * P], cond[:, k:k + 1],
                                  start=(k == 0), stop=(k == KC - 1))
                if c < 11:
                    last.then_inc(sem("mod_read"), 1)
                    unit_read[("mod", c)] = (sem("mod_read"), c + 1)
            last.then_inc(bank.full, 1)
            read_by(bank, "mod", 11)

            pe.wait_ge(sem("mixed_ready"), 1)
            token_units(("w_out",), 2, hT3)

            def feed_forward(l):
                norm_turn(("h_mlp", l), 2 if l == 0 else 4)
                turned(("h_mlp", l))
                for c in range(8):
                    w = blocks(weights(pe, "up", l, c), KC)
                    read_by(to_features(("up", l, c), w, hT3, KC, four), "up", l, c)
                pe.wait_ge(sem("act_ready"), 16 * (l + 1))
                for n in range(2):
                    pair = [banks.take(pe, "down", l, n, t) for t in range(NT)]
                    for kb in range(4):
                        w = blocks(weights(pe, "down", l, n, kb), KC)
                        for t in range(NT):
                            for k in range(KC):
                                last = mm(pair[t].ap[:, :], actT[:, kb * KC + k, t * P:(t + 1) * P], w[:, k, :],
                                          start=(kb == 0 and k == 0), stop=(kb == 3 and k == KC - 1))
                            if kb == 3:
                                last.then_inc(pair[t].full, 1)
                        if kb < 3:
                            last.then_inc(sem("down_read"), 1)
                            unit_read[("down", l, n, kb)] = (sem("down_read"), 6 * l + 3 * n + kb + 1)
                        else:
                            read_by(pair[1], "down", l, n, kb)
                pe.wait_ge(sem("p_landed"), 16 * (l + 1))
                bank = banks.take(pe, "pT", l)
                transposes([(bank.ap[:, k * S + t * P:k * S + (t + 1) * P], p_tok[:, t, k * P:(k + 1) * P])
                            for k in range(2) for t in range(NT)], bank)
                banks.wait_read(pe, "pT", l)
                w = blocks(weights(pe, "ple", l)[:, 0:2 * D], 2)
                for n in range(2):
                    bank = to_tokens(("ple", l, n), w[:, :, n * 512:(n + 1) * 512], pT, 2, 512)
                read_by(bank, "ple", l)
                for n in range(2):
                    for t in range(NT):
                        banks.wait_read(pe, "down", l, n, t)
                norm_turn(("x_gate", l), 0, x3)
                turned(("x_gate", l))
                token_units(("gate", l), 2, hT3)

            def attend(tag, items_q, items_k, value, landed_sem, probs, probsT):
                n = 2 * HEADS
                for i in range(n + LAG):
                    if i < n:
                        h, t = i // 2, i % 2
                        bank = banks.take(pe, tag, "s", i)
                        mm(bank.ap[:, 0:(t + 1) * P], items_q(h)[:, t * P:(t + 1) * P], items_k(h)[:, 0:(t + 1) * P],
                           start=True, stop=True).then_inc(bank.full, 1)
                    if i >= LAG:
                        i2 = i - LAG
                        h, t = i2 // 2, i2 % 2
                        bank = banks.take(pe, tag, "pT", i2)
                        pe.wait_ge(sem(landed_sem), i2 + 1)
                        transposes([(bank.ap[:, k * P:(k + 1) * P], probs[:, i2 % 8, k * P:(k + 1) * P])
                                    for k in range(t + 1)], bank)
                        if t == 1 and h >= 1:
                            out_of(tag, h - 1, value, probsT)
                out_of(tag, HEADS - 1, value, probsT)

            open_bank = {}

            def out_of(tag, h, value, probsT):
                if h % 2 == 0:
                    open_bank[tag] = banks.take(pe, tag, "o", h // 2)
                bank = open_bank[tag]
                for t in range(NT):
                    banks.wait_read(pe, tag, "pT", 2 * h + t)
                    for k in range(t + 1):
                        last = mm(bank.ap[:, (h % 2) * S + t * P:(h % 2) * S + (t + 1) * P], value(h, k),
                                  probsT[:, (2 * h + t) % 4, k, :], start=(k == 0), stop=(k == t))
                if h % 2:
                    last.then_inc(bank.full, 1)
                else:
                    last.then_inc(sem(tag + "_even_read"), 1)

            feed_forward(0)
            if stop < 4:
                return
            norm_turn("h_att", 3)
            turned("h_att")
            token_units(("qkv",), 6, hT3)
            pe.wait_ge(sem("rotated"), 2)
            for tag, src in (("qT", q_tok), ("kT", k_tok)):
                for c in range(4):
                    bank = banks.take(pe, tag, c)
                    transposes([(bank.ap[:, i * S + t * P:i * S + (t + 1) * P], src[:, t, (2 * c + i) * P:(2 * c + i + 1) * P])
                                for i in range(2) for t in range(NT)], bank)
            for tag in ("qT", "kT"):
                for c in range(4):
                    banks.wait_read(pe, tag, c)
            attend("att", lambda h: qT[:, h, :], lambda h: kT[:, h, :],
                   lambda h, k: v_att[:, k, h * P:(h + 1) * P], "att_prob", prob, probT)
            for c in range(4):
                banks.wait_read(pe, "att", "o", c)
            token_units(("w_o",), 2, hT3)
            feed_forward(1)
            if stop < 5:
                return

            norm_turn("h_in2", 5)
            pe.wait_ge(sem("diag_ready"), 1)
            for c in range(4):
                bank = banks.take(pe, "grow", c)
                for i in range(4):
                    last = mm(bank.ap[:, i * P:(i + 1) * P], ones, diag[:, 4 * c + i, :], start=True, stop=True)
                last.then_inc(bank.full, 1)
            turned("h_in2")
            w = blocks(weights(pe, "in2", 0), KC)
            read_by(to_features(("av",), w, hT3, KC, four), "in2", 0)
            w = blocks(weights(pe, "in2", 1)[:, 0:KC * 384], KC)
            read_by(to_tokens(("cq",), w, hT3, KC, 384), "in2", 1)
            w = blocks(weights(pe, "in2", 2), KC)
            read_by(to_features(("qi",), w, hT3, KC, four), "in2", 2)
            w = weights(pe, "in2", 3)
            to_features(("ki",), blocks(w[:, 0:KC * P], KC), hT3, KC, [0])
            to_features(("pool",), blocks(w[:, KC * P:KC * 384], KC), hT3, KC, [0, P])
            wiw = blocks(w[:, KC * 384:KC * 392], KC)
            bank = banks.take(pe, "wi")
            for t in range(NT):
                for k in range(KC):
                    last = mm(bank.ap[:, t * 8:(t + 1) * 8], hT3[:, k, t * P:(t + 1) * P], wiw[:, k, :],
                              start=(k == 0), stop=(k == KC - 1))
            last.then_inc(bank.full, 1)
            read_by(bank, "in2", 3)
            w = weights(pe, "dsa")
            bank = banks.take(pe, "convk")
            transposes([(bank.ap[:, c * TAPS:(c + 1) * TAPS], w[0:TAPS, 2176 + c * P:2176 + (c + 1) * P])
                        for c in range(2)], bank)
            bank = banks.take(pe, "ukT")
            transposes([(bank.ap[:, j * P:(j + 1) * P], w[:, 1024 + j * P:1024 + (j + 1) * P]) for j in range(4)], bank)
            pe.wait_ge(sem("latents_normed"), 1)
            bank = banks.take(pe, "cqT")
            transposes([(bank.ap[:, k * S + t * P:k * S + (t + 1) * P], cq_tok[:, t, k * P:(k + 1) * P])
                        for k in range(2) for t in range(NT)], bank)
            bank = banks.take(pe, "ckvT")
            transposes([(bank.ap[:, t * P:(t + 1) * P], ckv_tok[:, t, :]) for t in range(NT)], bank)
            banks.wait_read(pe, "qi", 0)
            banks.wait_read(pe, "qi", 1)
            banks.wait_read(pe, "ki", 0)
            for t in range(NT):
                for g in range(4):
                    bank = banks.take(pe, "idx", t, g)
                    rows_ = slice(64 * (g // 2), 64 * (g // 2) + 64)
                    for i in range(2):
                        j = 2 * (g % 2) + i
                        last = mm(bank.ap[:, i * S:(i + 1) * S], qiT[rows_, j, t * P:(t + 1) * P], kiT[rows_, :],
                                  start=True, stop=True)
                    last.then_inc(bank.full, 1)
            banks.wait_read(pe, "cqT")
            to_features(("q2",), blocks(w[:, 0:1024], 2), cqT, 2, four)
            banks.wait_read(pe, "ukT")
            banks.wait_read(pe, "q2", 0)
            banks.wait_read(pe, "q2", 1)
            for g in range(4):
                bank = banks.take(pe, "qabs", g)
                rows_ = slice(64 * (g // 2), 64 * (g // 2) + 64)
                for i in range(2):
                    j = 2 * (g % 2) + i
                    last = mm(bank.ap[:, i * S:(i + 1) * S], w_ukT[rows_, j, :], q2T[rows_, j, :], start=True, stop=True)
                last.then_inc(bank.full, 1)
            pe.wait_ge(sem("conv_done"), 1)
            bank = banks.take(pe, "cmean")
            for c in range(2):
                last = mm(bank.ap[:, 0:S], ones, conv_acc[:, c, :], start=(c == 0), stop=(c == 1))
            last.then_inc(bank.full, 1)
            pe.wait_ge(sem("conv_centred"), 1)
            bank = banks.take(pe, "cvar")
            for c in range(2):
                last = mm(bank.ap[:, 0:S], ones, conv_sq[:, c, :], start=(c == 0), stop=(c == 1))
            last.then_inc(bank.full, 1)
            pe.wait_ge(sem("pool_ready"), 1)
            for g in range(2):
                rows_ = slice(64 * g, 64 * g + 64)
                bank = banks.take(pe, "poolo", g)
                for c in range(2):
                    last = mm(bank.ap[rows_, c * S:(c + 1) * S], w[rows_, 2048 + c * 64:2048 + (c + 1) * 64],
                              pool_d[rows_, c, :], start=True, stop=True)
                last.then_inc(bank.full, 1)
            for g in range(4):
                banks.wait_read(pe, "qabs", g)
            banks.wait_read(pe, "ckvT")
            attend("dsa", lambda h: q_abs[:, h, :], lambda h: ckvT, lambda h, k: ckv_tok[:, k, :],
                   "dsa_prob", prob2, probT2)
            for c in range(4):
                banks.wait_read(pe, "dsa", "o", c)
            for g in range(2):
                rows_ = slice(64 * g, 64 * g + 64)
                for c in range(2):
                    bank = banks.take(pe, "yatt", g, c)
                    for i in range(2):
                        h = 2 * (2 * c + i) + g
                        last = mm(bank.ap[rows_, i * S:(i + 1) * S], w[:, 1536 + h * 64:1536 + (h + 1) * 64],
                                  ctxT[:, h, :], start=True, stop=True)
                    last.then_inc(bank.full, 1)
            read_by(bank, "dsa")
            pe.wait_ge(sem("conv_out"), 2)
            for g in range(2):
                banks.wait_read(pe, "poolo", g)
                for c in range(2):
                    banks.wait_read(pe, "yatt", g, c)
            token_units(("w_out2",), 2, hT3)
            if stop < 6:
                return

            norm_turn("h_moe", 6)
            turned("h_moe")
            pe.wait_ge(sem("router_landed"), 32)
            bank = banks.take(pe, "router")
            rw = blocks(router[:, :], KC)
            for t in range(NT):
                for k in range(KC):
                    last = mm(bank.ap[:, t * 36:(t + 1) * 36], hT3[:, k, t * P:(t + 1) * P], rw[:, k, :],
                              start=(k == 0), stop=(k == KC - 1))
            last.then_inc(bank.full, 1)
            pe.wait_ge(sem("gates_ready"), 1)
            bank = banks.take(pe, "gT")
            transposes([(bank.ap[0:N_EXP, t * P:(t + 1) * P], gates[:, t, :]) for t in range(NT)], bank)
            for b in range(8):
                if banks.n > b:
                    pe.wait_ge(banks.freed[b], (banks.n - 1 - b) // 8 + 1)
            y_bank = [[bank_aps[2 * t + n] for n in range(2)] for t in range(NT)]
            for t in range(NT):
                for n in range(2):
                    last = mm(y_bank[t][n], zeros, const[:, 0:512], start=True, stop=False, skip_group_check=True)
            last.then_inc(sem("moe_down"), 1)
            w1 = [blocks(ring[:, ((len(units) + i) % SLOTS) * UNIT:((len(units) + i) % SLOTS + 1) * UNIT],
                         KC if i < 2 else EC) for i in range(3)]
            with pe.Fori(0, N_EXP) as e:
                for m in range(EC):
                    if m == 0:
                        for i in range(2):
                            s = (len(units) + i) % SLOTS
                            pe.wait_ge(landed[s], e * 16 + (slot_total[s] + 16))
                    pe.wait_ge(sem("moe_hidden_read"), e * EC + (m + 1))
                    for i in range(2):
                        for k in range(KC):
                            last = mm(bank_aps[4 + m][:, i * S:(i + 1) * S], w1[i][:, k, m * P:(m + 1) * P],
                                      hT3[:, k, :], start=(k == 0), stop=(k == KC - 1), skip_group_check=True)
                    last.then_inc(sem("moe_hidden"), 1)
                s = (len(units) + 2) % SLOTS
                pe.wait_ge(landed[s], e * 16 + (slot_total[s] + 16))
                for m in range(EC):
                    pe.wait_ge(sem("moe_act"), e * EC + (m + 1))
                    for t in range(NT):
                        for n in range(2):
                            last = mm(y_bank[t][n], exp_act[:, m, t * P:(t + 1) * P],
                                      w1[2][:, m, n * 512:(n + 1) * 512], start=False, stop=False,
                                      skip_group_check=True)
                last.then_inc(sem("moe_down"), 1)
            for t in range(NT):
                for n in range(2):
                    last = mm(y_bank[t][n], zeros, const[:, 0:512], start=False, stop=True, skip_group_check=True)
            last.then_inc(sem("moe_sum"), 1)

        @block.vector
        def _(dve):
            v = nc.vector
            flag = iter([flags[:, i:i + 1] for i in range(24)])
            step = Chain(dve, sem("dve_step"))

            def evacuate(dst, *name):
                bank = banks.read(dve, *name)
                v.tensor_copy(dst, bank.ap).then_inc(bank.freed, 1)

            def norm(k):
                dve.wait_ge(sem("rms_root"), k)
                step(v.reciprocal(rstd, rstd))
                for t in range(NT):
                    v.tensor_scalar(xn3[:, t, :], x3[:, t, :], rstd[:, t:t + 1], None, ALU.mult)\
                        .then_inc(sem("normed"), 1)

            def add_to_x(tag, *key):
                for n in range(2):
                    for t in range(NT):
                        bank = banks.read(dve, tag, *key, n, t)
                        part = x3[:, t, n * 512:(n + 1) * 512]
                        v.tensor_tensor(part, part, bank.ap, ALU.add).then_inc(bank.freed, 1)

            v.memset(vec_rows, 0.0).then_inc(sem("vec_zero"), 1)
            v.memset(raw[:, :, 0:1], 0.0).then_inc(sem("dve_step"), 1)
            step.n += 1
            step(v.memset(st, 0.0))
            bank = banks.read(dve, "vec")
            v.tensor_copy(vec[:, :], bank.ap[:, 0:2 * P]).then_inc(bank.freed, 1)
            norm(1)
            banks.wait_read(dve, "vec")
            l3 = v1("hgrn_lb", 0, 12)
            step(v.tensor_tensor(lb, l3[:, 0:4], l3[:, 4:8], ALU.max))
            step(v.tensor_tensor(lb, lb, l3[:, 8:12], ALU.max))
            v.tensor_tensor(blocks(lb_d, 3), blocks(l3, 3), mid(lb, 3), ALU.subtract).then_inc(sem("lb_shifted"), 1)
            dve.wait_ge(sem("lb_exp"), 1)
            step(v.tensor_tensor(lb, lb_e[:, 0:4], lb_e[:, 4:8], ALU.add))
            step(v.tensor_tensor(lb, lb, lb_e[:, 8:12], ALU.add))
            step(v.reciprocal(lb, lb))
            step(v.tensor_tensor(lb, lb, lb_e[:, 0:4], ALU.mult))
            step(v.tensor_scalar(lb_c, lb, -1.0, 1.0, ALU.mult, ALU.add))
            for c in range(4, 8):
                for i in range(2 if c < 7 else 1):
                    b = 4 * (c - 4) + 2 * i
                    bank = banks.read(dve, "in", c, i)
                    v.tensor_copy(raw[:, b:b + 2, 1:S + 1], blocks(bank.ap, 2)).then_inc(bank.freed, 1)
            for c in range(4, 8):
                for i in range(2 if c < 7 else 1):
                    banks.wait_read(dve, "in", c, i)
            if stop < 1:
                return

            def shift_mix(dst, b0, n):
                step(v.tensor_tensor(dst, raw[:, b0:b0 + n, 0:S], raw[:, b0:b0 + n, 1:S + 1], ALU.subtract))
                for i in range(n):
                    last = v.scalar_tensor_tensor(dst[:, i, :], dst[:, i, :], v1("rwkv_mu", b0 + i),
                                                  raw[:, b0 + i, 1:S + 1], ALU.mult, ALU.add)
                    last.then_inc(sem("dve_step"), 1)
                    step.n += 1
                dve.wait_ge(sem("dve_step"), step.n)

            shift_mix(low, 12, 2)
            v.memset(next(flag), 0.0).then_inc(sem("low_mixed"), 1)

            for i in range(2):
                banks.wait_read(dve, "in", 0, i)
                banks.wait_read(dve, "in", 1, i)
            for j in range(4):
                step(v.tensor_scalar(hf[:, j, :], hf[:, j, :], lb_c[:, j:j + 1], lb[:, j:j + 1], ALU.mult, ALU.add))
            v.tensor_scalar(hk, hf, -1.0, 1.0, ALU.mult, ALU.add).then_inc(sem("hgrn_scaled"), 1)

            def take_scores(m):
                for t in range(NT):
                    bank = banks.read(dve, "hs", m, t)
                    mask = mid(level_mask(m) if m else ident, HG_HEADS).bitcast(I32)
                    v.copy_predicated(st[:, t], mask, blocks(bank.ap, HG_HEADS)).then_inc(bank.freed, 1)

            take_scores(0)
            v.tensor_tensor(hq, hq, hf, ALU.mult).then_inc(sem("hgrn_scaled"), 1)
            take_scores(1)
            ends = page(15)
            for i, m in enumerate(LEVELS):
                n = 4 * S // (2 * m)
                e2 = ends[:, 0:2 * n].rearrange("p (b a) -> p b a", a=2)
                q4 = page(13).rearrange("p (b a s) -> p b a s", a=2, s=m)
                k4 = page(14).rearrange("p (b a s) -> p b a s", a=2, s=m)
                dve.wait_ge(sem("hgrn_scaled"), i + 2)
                step(v.tensor_tensor(q4[:, :, 1, :], q4[:, :, 1, :], tail(e2[:, :, 0], m), ALU.mult))
                if m < LEVELS[-1]:
                    step(v.tensor_tensor(h_end[i % 2][:, 0:n], e2[:, :, 0], e2[:, :, 1], ALU.mult))
                v.tensor_tensor(k4[:, :, 0, :], k4[:, :, 0, :], tail(e2[:, :, 1], m), ALU.mult)\
                    .then_inc(sem("hgrn_scaled"), 1)
                ends = h_end[i % 2]
                if m < LEVELS[-1]:
                    take_scores(2 * m)
            bank = banks.read(dve, "hs", P)
            v.tensor_copy(sx, blocks(bank.ap, HG_HEADS)).then_inc(bank.freed, 1)
            for t in range(NT):
                evacuate(o_a[:, t, :], "ho", t)
            for t in range(NT):
                banks.wait_read(dve, "ho", t)
            o8 = blocks(page(21), 8)
            step(v.tensor_tensor(page(23), page(21), page(21), ALU.mult))
            step(v.tensor_reduce(hg_ss, blocks(page(23), 8), AX.X, ALU.add))
            v.tensor_scalar(hg_ss, hg_ss, 1.0 / P, EPS, ALU.mult, ALU.add).then_inc(sem("hgrn_sq"), 1)
            dve.wait_ge(sem("hgrn_root"), 1)
            step(v.reciprocal(hg_ss, hg_ss))
            v.tensor_tensor(o8, o8, tail(hg_ss, P), ALU.mult).then_inc(sem("hgrn_normed"), 1)
            for c in range(2):
                bank = banks.read(dve, "ha", c)
                for i in range(2):
                    h = 2 * c + i
                    last = v.scalar_tensor_tensor(hT3[:, h, :], bank.ap[:, i * S:(i + 1) * S], v1("hgrn_onorm", h),
                                                  hgT[:, h, :], ALU.mult, ALU.mult)
                last.then_inc(bank.freed, 1)
            for c in range(2):
                banks.wait_read(dve, "ha", c)
            if stop < 2:
                return

            shift_mix(page(4, 2).rearrange("p (b t) -> p b t", b=8), 0, 8)
            shift_mix(v_mix, 8, 4)
            for c in range(2):
                banks.wait_read(dve, "lw", c)
                banks.wait_read(dve, "la", c)
                banks.wait_read(dve, "lg", c)
            v.tensor_scalar(logdec, logdec, DECAY_SCALE, None, ALU.mult).then_inc(sem("dve_step"), 1)
            step.n += 1
            for j in range(4):
                step(v.tensor_scalar(kk[:, j, :], k_mix[:, j, :], v1("rwkv_kk", j), None, ALU.mult))
            v.tensor_tensor(page(21), page(7), page(7), ALU.mult).then_inc(sem("kk_sq"), 1)
            for j in range(4):
                step(v.tensor_scalar(k_adj[:, j, :], a_gate[:, j, :], -1.0, v1("rwkv_ka", j), ALU.add, ALU.mult))
            step(v.scalar_tensor_tensor(page(13), page(13), 1.0, page(5), ALU.add, ALU.mult))
            for j in range(4):
                last = v.scalar_tensor_tensor(blocks(page(22), 4)[:, j, :], r_mix[:, j, :], v1("rwkv_rk", j),
                                              k_adj[:, j, :], ALU.mult, ALU.mult)
                if j < 3:
                    step(last)
            last.then_inc(sem("rk_prod"), 1)
            cum8, log8 = blocks(page(12), 8), blocks(page(6), 8)
            for i in range(8):
                step(v.tensor_tensor_scan(cum8[:, i, :], ones, log8[:, i, :], 0.0, ALU.mult, ALU.add))
            for c in range(2):
                bank = banks.read(dve, "kk", c)
                v.tensor_scalar(page(21)[:, c * 512:(c + 1) * 512], bank.ap, 1e-24, None, ALU.max).then_inc(bank.freed, 1)
            for t in range(NT):
                evacuate(v_tok[:, t, :], "vt", t)
            for c in range(2):
                bank = banks.read(dve, "bonus", c)
                v.tensor_tensor(page(18)[:, c * 512:(c + 1) * 512], bank.ap, page(8)[:, c * 512:(c + 1) * 512],
                                ALU.mult).then_inc(bank.freed, 1)
            dve.wait_ge(sem("kk_root"), 1)
            step(v.reciprocal(page(21), page(21)))
            step(v.tensor_tensor(page(7), page(7), page(21), ALU.mult))
            step(v.tensor_copy(c_mid, cum8[:, :, 63]))
            step(v.tensor_tensor(cum8, cum8, tail(c_mid, P), ALU.subtract))
            step(v.tensor_tensor(s_scale, cum8[:, 0:8:2, P - 1], c_mid[:, 1:8:2], ALU.add))
            v.tensor_tensor(page(21), page(12), page(6), ALU.subtract).then_inc(sem("cum_ready"), 1)
            step(v.tensor_tensor(page(16), page(7), page(10), ALU.mult))
            dve.wait_ge(sem("decays_exp"), 1)
            ar8 = page(14, 2).rearrange("p (i a s) -> p i a s", i=8, a=2)
            step(v.scalar_tensor_tensor(ar8[:, :, 0, :], blocks(page(7), 8), -1.0, blocks(page(21), 8), ALU.mult, ALU.mult))
            step(v.tensor_tensor(ar8[:, :, 1, :], blocks(page(4), 8), blocks(page(22), 8), ALU.mult))
            step(v.tensor_tensor(page(16), page(16), page(12), ALU.mult))
            v.tensor_tensor(page(17), page(13), page(12), ALU.mult).then_inc(sem("tilded"), 1)
            dve.wait_ge(sem("tilded"), 1)
            step(v.tensor_copy(invT, mid(ident, 16)))
            both = const[:, cols_at["strict"][0]:cols_at["upto"][1]]
            for i in range(16):
                bank = banks.read(dve, "pairs", i)
                v.tensor_tensor(ab[:, i].rearrange("p a s -> p (a s)"), bank.ap[:, 0:S], both, ALU.mult)
                v.tensor_tensor(ak[:, i].rearrange("p a s -> p (a s)"), bank.ap[:, S:2 * S], both, ALU.mult)\
                    .then_inc(bank.freed, 1)
            for i in range(8, 16):
                banks.wait_read(dve, "pairs", i)
            v.copy_predicated(invT, mid(level_mask(1), 16).bitcast(I32), ab[:, :, 0, :]).then_inc(sem("inv_first"), 1)
            dve.wait_ge(sem("inv_first"), 1)
            for m in LEVELS[1:]:
                for g in range(4):
                    bank = banks.read(dve, "xax", m, g)
                    v.copy_predicated(invT[:, 4 * g:4 * g + 4, :], mid(level_mask(m), 4).bitcast(I32),
                                      blocks(bank.ap, 4)).then_inc(bank.freed, 1)
            def take_halves(dst, tag, t):
                for half_ in range(2):
                    bank = banks.read(dve, tag, t, half_)
                    v.tensor_copy(dst.rearrange("p (j a v) -> p j a v", a=2, v=64)[:, :, half_, :],
                                  blocks(bank.ap[:, 0:S], 4)).then_inc(bank.freed, 1)

            dve.wait_ge(sem("scale_exp"), 1)
            for t in range(NT):
                take_halves(w_sb, "w", t)
                evacuate(sa_sb, "sa", t)
                if t == 0:
                    bank = banks.read(dve, "state")
                    b4 = blocks(bank.ap, 4)
                    v.tensor_tensor(s1[0:64], b4[0:64, :, 0:64], tail(s_scale[0:64, :], 64), ALU.mult)\
                        .then_inc(sem("state_ready"), 1)
                    v.tensor_tensor(s1[64:P], b4[64:P, :, 64:P], tail(s_scale[64:P, :], 64), ALU.mult)\
                        .then_inc(bank.freed, 1)
                take_halves(y_tok[:, t, :], "y", t)
            for t in range(NT):
                for half_ in range(2):
                    banks.wait_read(dve, "y", t, half_)
            y16 = blocks(page(21), 16)
            step(v.tensor_reduce(rw_mu, y16, AX.X, ALU.add))
            step(v.tensor_scalar(rw_mu, rw_mu, 1.0 / 64, None, ALU.mult))
            step(v.tensor_tensor(y16, y16, tail(rw_mu, 64), ALU.subtract))
            step(v.tensor_tensor(page(13), page(21), page(21), ALU.mult))
            step(v.tensor_reduce(rw_ss, blocks(page(13), 16), AX.X, ALU.add))
            v.tensor_scalar(rw_ss, rw_ss, 1.0 / 64, LN_EPS, ALU.mult, ALU.add).then_inc(sem("rwkv_sq"), 1)
            dve.wait_ge(sem("rwkv_root"), 1)
            step(v.reciprocal(rw_ss, rw_ss))
            v.tensor_tensor(y16, y16, tail(rw_ss, 64), ALU.mult).then_inc(sem("rwkv_normed"), 1)
            for c in range(2):
                bank = banks.read(dve, "yb", c)
                for i in range(2):
                    j = 2 * c + i
                    last = v.tensor_scalar(hT3[:, 4 + j, :], bank.ap[:, i * S:(i + 1) * S], v1("rwkv_ln_w", j),
                                           v1("rwkv_ln_b", j), ALU.mult, ALU.add)
                    if i == 0:
                        step(last)
                last.then_inc(bank.freed, 1)
                banks.wait_read(dve, "yb", c)
            out4 = hT[:, 4 * S:8 * S]
            step(v.tensor_tensor(out4, out4, page(18), ALU.add))
            v.tensor_tensor(out4, out4, page(11), ALU.mult).then_inc(sem("mixed_ready"), 1)
            if stop < 3:
                return

            bank = banks.read(dve, "mod")
            v.tensor_tensor(modc, bank.ap[:, 0:48], v2("mod_b_2", 0, 48), ALU.add).then_inc(bank.freed, 1)
            banks.wait_read(dve, "mod")
            step(v.scalar_tensor_tensor(sc1, modc[:, 8:16], 1.0, v2("norm1_g_2", 0, 8), ALU.add, ALU.mult))
            step(v.scalar_tensor_tensor(sc2, modc[:, 32:40], 1.0, v2("norm2_g_2", 0, 8), ALU.add, ALU.mult))
            for n in range(2):
                for t in range(NT):
                    bank = banks.read(dve, "w_out", n, t)
                    part = x3[:, t, n * 512:(n + 1) * 512]
                    v.tensor_tensor(part, part, bank.ap, ALU.add).then_inc(bank.freed, 1)

            def feed_forward(l):
                for n in range(2):
                    for t in range(NT):
                        banks.wait_read(dve, "w_out" if l == 0 else "w_o", n, t)
                norm(2 if l == 0 else 4)
                for c in range(8):
                    for i in range(2):
                        banks.wait_read(dve, "up", l, c, i)
                        buf = relu[:, (2 * c + i) % 4, :]
                        v.tensor_tensor(actT[:, 4 * c + 2 * i:4 * c + 2 * i + 2, :], blocks(buf, 2), blocks(buf, 2),
                                        ALU.mult).then_inc(sem("act_ready"), 1)
                add_to_x("down", l)
                dve.wait_ge(sem("ple_root"), l + 1)
                step(v.reciprocal(ssq, ssq))
                dve.wait_ge(sem("big_row_landed"), 16 * (l + 1))
                for t in range(NT):
                    step(v.scalar_tensor_tensor(ple_raw[:, t, :], ple_raw[:, t, :], ssq[:, t:t + 1], big_row,
                                                ALU.mult, ALU.mult))
                for n in range(2):
                    for t in range(NT):
                        banks.wait_read(dve, "gate", l, n, t)
                step(v.tensor_tensor(page(21, 2), page(21, 2), page(23, 2), ALU.mult))
                v.tensor_tensor(x[:, :], x[:, :], page(21, 2), ALU.add).then_inc(sem("ple_added"), 1)
                dve.wait_ge(sem("ple_added"), l + 1)

            def head_norm(tok, gain):
                flat = tok.rearrange("p t n -> p (t n)")
                t16 = blocks(flat, 16)
                step(v.tensor_tensor(sq, flat, flat, ALU.mult))
                step(v.tensor_reduce(head_ss, blocks(sq, 16), AX.X, ALU.add))

            def head_norm2(tok, gain, k):
                flat = tok.rearrange("p t n -> p (t n)")
                t16 = blocks(flat, 16)
                head_norm(tok, gain)
                v.tensor_scalar(head_ss, head_ss, 1.0 / P, EPS, ALU.mult, ALU.add).then_inc(sem("head_sq"), 1)
                dve.wait_ge(sem("head_root"), k)
                step(v.reciprocal(head_ss, head_ss))
                step(v.tensor_tensor(t16, t16, tail(head_ss, P), ALU.mult))
                step(v.tensor_tensor(t16, t16, mid(gain, 16), ALU.mult))
                s4 = sq.rearrange("p (t h d) -> p t h d", t=NT, h=HEADS)
                f4 = flat.rearrange("p (t h d) -> p t h d", t=NT, h=HEADS)
                for t in range(NT):
                    cos = mid(c_("cos", t * 64, (t + 1) * 64), HEADS)
                    sin = mid(c_("sin", t * 64, (t + 1) * 64), HEADS)
                    lo, hi = f4[:, t, :, 0:64], f4[:, t, :, 64:P]
                    step(v.tensor_tensor(s4[:, t, :, 0:64], lo, sin, ALU.mult))
                    step(v.tensor_tensor(s4[:, t, :, 64:P], hi, sin, ALU.mult))
                    step(v.tensor_tensor(lo, lo, cos, ALU.mult))
                    step(v.tensor_tensor(hi, hi, cos, ALU.mult))
                    step(v.tensor_tensor(lo, lo, s4[:, t, :, 64:P], ALU.subtract))
                    last = v.tensor_tensor(hi, hi, s4[:, t, :, 0:64], ALU.add)
                    if t < NT - 1:
                        step(last)
                last.then_inc(sem("rotated"), 1)
                dve.wait_ge(sem("rotated"), k)

            def attend(tag, scale, mask, probs, extra=None):
                n = 2 * HEADS
                for i in range(n + 2):
                    if i < n:
                        t = i % 2
                        bank = banks.read(dve, tag, "s", i)
                        if i >= 8:
                            banks.read(dve, tag, "pT", i - 8)
                        part = probs[:, i % 8, 0:(t + 1) * P]
                        v.scalar_tensor_tensor(part, bank.ap[:, 0:(t + 1) * P], scale, mask(t), ALU.mult, ALU.add)\
                            .then_inc(bank.freed, 1)
                        banks.wait_read(dve, tag, "s", i)
                        v.tensor_reduce(nmax[:, i:i + 1], part, AX.X, ALU.max, negate=True).then_inc(sem(tag + "_max"), 1)
                    if i >= 2:
                        i2 = i - 2
                        t = i2 % 2
                        dve.wait_ge(sem(tag + "_exp"), i2 + 1)
                        step(v.reciprocal(rinv[:, i2:i2 + 1], rsum[:, i2:i2 + 1]))
                        part = probs[:, i2 % 8, 0:(t + 1) * P]
                        v.tensor_scalar(part, part, rinv[:, i2:i2 + 1], None, ALU.mult).then_inc(sem(tag + "_prob"), 1)

            feed_forward(0)
            if stop < 4:
                return
            norm(3)
            for c in range(4):
                for t in range(NT):
                    banks.wait_read(dve, "qkv", c, t)
            dve.wait_ge(sem("rows_landed"), 16 * len(ROWS))
            head_norm2(q_tok, row("q_norm"), 1)
            head_norm2(k_tok, row("k_norm"), 2)
            causal = c_("causal")
            attend("att", float(P) ** -0.5, lambda t: causal[:, (1 - t) * P:S], prob)
            for n in range(2):
                for t in range(NT):
                    bank = banks.read(dve, "w_o", n, t)
                    part = x3[:, t, n * 512:(n + 1) * 512]
                    v.tensor_tensor(part, part, bank.ap, ALU.add).then_inc(bank.freed, 1)
            feed_forward(1)
            if stop < 5:
                return

            norm(5)
            for i in range(16):
                col = modc[:, 16 + i:17 + i] if i < 8 else modc[:, 32 + i:33 + i]
                last = v.tensor_scalar(diag[:, i, :], ident, col, None, ALU.mult)
                if i < 15:
                    last.then_inc(sem("dve_step"), 1)
                    step.n += 1
            dve.wait_ge(sem("dve_step"), step.n)
            last.then_inc(sem("diag_ready"), 1)
            v.memset(arena[:, 0:2 * (S + TAPS - 1)], 0.0).then_inc(sem("dve_step"), 1)
            step.n += 1
            for i in range(3):
                v.memset(arena[:, (9 + i) * 1024:(9 + i) * 1024 + 2 * (S + 16)], 0.0).then_inc(sem("dve_step"), 1)
                step.n += 1
            dve.wait_ge(sem("dve_step"), step.n)
            v.memset(next(flag), 0.0).then_inc(sem("pool_zero"), 1)
            for c in range(4):
                evacuate((g1_row if c < 2 else g2_row)[:, (c % 2) * 512:(c % 2 + 1) * 512], "grow", c)
            banks.wait_read(dve, "av", 1)
            bank = banks.read(dve, "av", 0)
            v.tensor_tensor(u_pad[:, :, TAPS - 1:], blocks(bank.ap, 2), sig_gate, ALU.mult).then_inc(bank.freed, 1)
            banks.wait_read(dve, "av", 0)
            for t in range(NT):
                bank = banks.read(dve, "cq", t)
                v.tensor_copy(cq_tok[:, t, :], bank.ap[:, 0:384]).then_inc(bank.freed, 1)
                banks.wait_read(dve, "cq", t)
                step(v.tensor_tensor(cq_sq, cq_tok[:, t, :], cq_tok[:, t, :], ALU.mult))
                step(v.tensor_reduce(cs[:, 2 * t:2 * t + 1], cq_sq[:, 0:256], AX.X, ALU.add))
                step(v.tensor_reduce(cs[:, 2 * t + 1:2 * t + 2], cq_sq[:, 256:384], AX.X, ALU.add))
                step(v.tensor_scalar(cs[:, 2 * t:2 * t + 1], cs[:, 2 * t:2 * t + 1], 1.0 / 256, EPS, ALU.mult, ALU.add))
                step(v.tensor_scalar(cs[:, 2 * t + 1:2 * t + 2], cs[:, 2 * t + 1:2 * t + 2], 1.0 / P, EPS, ALU.mult,
                                     ALU.add))
            v.memset(next(flag), 0.0).then_inc(sem("latent_sq"), 1)
            dve.wait_ge(sem("latent_root"), 1)
            step(v.reciprocal(cs, cs))
            for t in range(NT):
                step(v.tensor_scalar(cq_tok[:, t, 0:256], cq_tok[:, t, 0:256], cs[:, 2 * t:2 * t + 1], None, ALU.mult))
                step(v.scalar_tensor_tensor(ckv_tok[:, t, :], cq_tok[:, t, 256:384], cs[:, 2 * t + 1:2 * t + 2],
                                            row("kv_norm_g_2"), ALU.mult, ALU.mult))
            v.memset(next(flag), 0.0).then_inc(sem("latents_normed"), 1)
            bank = banks.read(dve, "convk")
            v.tensor_copy(half(5)[:, 0:2 * TAPS], bank.ap[:, 0:2 * TAPS]).then_inc(bank.freed, 1)
            banks.wait_read(dve, "convk")
            banks.wait_read(dve, "wi")
            for t in range(NT):
                for g in range(4):
                    banks.wait_read(dve, "idx", t, g)
                    for i in range(2):
                        h = 2 * (2 * (g % 2) + i) + g // 2
                        buf = rel[:, (4 * t + g) % 4 * 2 + i, :]
                        if g == 0 and i == 0:
                            last = v.tensor_scalar(score[:, t, :], buf, wi[:, t, h:h + 1], None, ALU.mult)
                        else:
                            last = v.scalar_tensor_tensor(score[:, t, :], buf, wi[:, t, h:h + 1], score[:, t, :],
                                                          ALU.mult, ALU.add)
                        if i == 0:
                            step(last)
                    last.then_inc(sem("rel_used"), 1)
                    dve.wait_ge(sem("rel_used"), 4 * t + g + 1)
            for t in range(NT):
                step(v.scalar_tensor_tensor(work[:, t, :], score[:, t, :], float(512) ** -0.5,
                                            c_("allowed", t * S, (t + 1) * S), ALU.mult, ALU.add))
                for r in range(8):
                    step(v.max(top8, work[:, t, :]))
                    step(v.match_replace(work[:, t, :], top8, work[:, t, :], -3e38))
                step(v.tensor_scalar(bias2[:, t, :], work[:, t, :], -2e38, NEG, ALU.is_gt, ALU.mult))
            for k in range(TAPS):
                for c in range(2):
                    src = u_pad[:, c, k:k + S]
                    if k == 0:
                        last = v.tensor_scalar(conv_acc[:, c, :], src, conv_col[:, c, 0:1], v2("conv_b_2", c),
                                               ALU.mult, ALU.add)
                    else:
                        last = v.scalar_tensor_tensor(conv_acc[:, c, :], src, conv_col[:, c, k:k + 1],
                                                      conv_acc[:, c, :], ALU.mult, ALU.add)
                    last.then_inc(sem("dve_step"), 1)
                    step.n += 1
                dve.wait_ge(sem("dve_step"), step.n)
            v.memset(next(flag), 0.0).then_inc(sem("conv_done"), 1)
            bank = banks.read(dve, "cmean")
            v.tensor_scalar(conv_m[:, 0, :], bank.ap[:, 0:S], 1.0 / 256, None, ALU.mult).then_inc(bank.freed, 1)
            banks.wait_read(dve, "cmean")
            step(v.tensor_tensor(conv_acc, conv_acc, mid(conv_m[:, 0, :], 2), ALU.subtract))
            v.tensor_tensor(conv_sq, conv_acc, conv_acc, ALU.mult).then_inc(sem("conv_centred"), 1)
            banks.wait_read(dve, "pool", 0)
            u = pool_s[0]
            src, spare = pool_s[0], [pool_s[1], pool_s[2]]
            inv_n = blocks(c_("pool_inv"), 2)
            for n, w_ in enumerate((1, 2, 4, 8)):
                dst = spare[n % 2]
                step(v.tensor_tensor(dst[:, :, 16:], src[:, :, 16:], src[:, :, 16 - w_:16 - w_ + S], ALU.add))
                c, g = n // 2, slice(64 * (n % 2), 64 * (n % 2) + 64)
                step(v.tensor_tensor(pool_d[g, c, :], dst[g, c, 16:], inv_n[g, c, :], ALU.mult))
                src = dst
            v.tensor_tensor(pool_d, pool_d, u[:, :, 16:], ALU.subtract).then_inc(sem("pool_ready"), 1)
            bank = banks.read(dve, "cvar")
            v.tensor_scalar(conv_m[:, 0, :], bank.ap[:, 0:S], 1.0 / 256, EPS, ALU.mult, ALU.add).then_inc(bank.freed, 1)
            dve.wait_ge(sem("conv_root"), 1)
            step(v.reciprocal(conv_m[:, 0, :], conv_m[:, 0, :]))
            v.tensor_tensor(conv_acc, conv_acc, mid(conv_m[:, 0, :], 2), ALU.mult).then_inc(sem("conv_normed"), 1)
            for g in range(2):
                rows_ = slice(64 * g, 64 * g + 64)
                bank = banks.read(dve, "poolo", g)
                for c in range(2):
                    last = v.tensor_scalar(yT[rows_, 6 + c, :], bank.ap[rows_, c * S:(c + 1) * S],
                                           v2("pool_scale_2", c)[rows_, :], None, ALU.mult)
                last.then_inc(bank.freed, 1)
            attend("dsa", 64.0 ** -0.5, lambda t: bias2[:, t, 0:(t + 1) * P], prob2)
            for n in range(2):
                for t in range(NT):
                    bank = banks.read(dve, "w_out2", n, t)
                    part = x3[:, t, n * 512:(n + 1) * 512]
                    v.tensor_tensor(scaled, bank.ap, g1_row[:, n * 512:(n + 1) * 512], ALU.mult)\
                        .then_inc(bank.freed, 1)
                    banks.wait_read(dve, "w_out2", n, t)
                    step(v.tensor_tensor(part, part, scaled, ALU.add))
            v.memset(next(flag), 0.0).then_inc(sem("mix2_added"), 1)
            if stop < 6:
                return

            norm(6)
            bank = banks.read(dve, "router")
            bias_row = rows[:, rows_at["router_g_b_2"][0]:rows_at["router_e_b_2"][1]]
            v.tensor_tensor(lg, bank.ap[:, 0:72].rearrange("p (t n) -> p t n", t=NT), mid(bias_row, NT), ALU.add)\
                .then_inc(bank.freed, 1)
            banks.wait_read(dve, "router")
            first = c_("first")

            def one_hot(dst, logits, best, spare_):
                n = logits.shape[1]
                step(v.tensor_reduce(best, logits, AX.X, ALU.max))
                step(v.scalar_tensor_tensor(dst, logits, best, first[:, 0:n], ALU.is_equal, ALU.mult))
                step(v.tensor_reduce(spare_, dst, AX.X, ALU.max))
                step(v.tensor_scalar(dst, dst, spare_, None, ALU.is_equal))

            for t in range(NT):
                r = rt[t]
                group, e_sel, h1, h2 = r[:, 0:4], r[:, 4:12], r[:, 12:20], r[:, 20:28]
                g_max, g_sum, e1, e2, tmp, diff, expd = (r[:, 28 + i:29 + i] for i in range(7))
                shifted = r[:, 36:40]
                one_hot(group, lg[:, t, 0:4], g_max, tmp)
                v.tensor_scalar(shifted, lg[:, t, 0:4], g_max, None, ALU.subtract).then_inc(sem("group_shifted"), 1)
                step(v.tensor_scalar(e_sel, lg[:, t, 4:12], group[:, 0:1], None, ALU.mult))
                for g in range(1, 4):
                    step(v.scalar_tensor_tensor(e_sel, lg[:, t, 4 + 8 * g:12 + 8 * g], group[:, g:g + 1], e_sel,
                                                ALU.mult, ALU.add))
                one_hot(h1, e_sel, e1, tmp)
                step(v.scalar_tensor_tensor(e_sel, h1, NEG, e_sel, ALU.mult, ALU.add))
                one_hot(h2, e_sel, e2, tmp)
                v.tensor_tensor(diff, e2, e1, ALU.subtract).then_inc(sem("expert_diff"), 1)
                dve.wait_ge(sem("route_exp"), 2 * (t + 1))
                step(v.tensor_reduce(g_sum, shifted, AX.X, ALU.add))
                step(v.tensor_scalar(tmp, expd, 1.0, g_sum, ALU.add, ALU.mult))
                step(v.reciprocal(tmp, tmp))
                step(v.scalar_tensor_tensor(h1, h2, expd, h1, ALU.mult, ALU.add))
                step(v.tensor_scalar(h1, h1, tmp, None, ALU.mult))
                for g in range(4):
                    step(v.tensor_scalar(gates[:, t, 8 * g:8 * g + 8], h1, group[:, g:g + 1], None, ALU.mult))
            v.memset(next(flag), 0.0).then_inc(sem("gates_ready"), 1)
            bank = banks.read(dve, "gT")
            v.tensor_copy(gT, bank.ap[0:N_EXP, 0:S]).then_inc(bank.freed, 1)
            dve.wait_ge(sem("gates_back"), 16)
            for m in range(EC):
                v.memset(next(flag), 0.0).then_inc(sem("moe_hidden_read"), 1)
            with dve.Fori(0, N_EXP) as e:
                dve.wait_ge(sem("moe_down"), e + 1)
                for m in range(EC):
                    dve.wait_ge(sem("moe_silu"), e * EC + (m + 1))
                    v.tensor_tensor(exp_act[:, m, :], exp_silu[:, m, :], bank_aps[4 + m][:, S:2 * S], ALU.mult)\
                        .then_inc(sem("moe_hidden_read"), 1)
                    dve.wait_ge(sem("moe_hidden_read"), e * EC + (EC + m + 1))
                    v.tensor_tensor(exp_act[:, m, :], exp_act[:, m, :], gate_all[:, e, :], ALU.mult)\
                        .then_inc(sem("moe_act"), 1)
            dve.wait_ge(sem("moe_sum"), 1)
            for t in range(NT):
                for n in range(2):
                    part = x3[:, t, n * 512:(n + 1) * 512]
                    step(v.tensor_tensor(scaled, bank_aps[2 * t + n], g2_row[:, n * 512:(n + 1) * 512], ALU.mult))
                    step(v.tensor_tensor(part, part, scaled, ALU.add))
            v.memset(next(flag), 0.0).then_inc(sem("moe_added"), 1)
            dve.wait_ge(sem("rms_root"), 7)
            step(v.reciprocal(rstd, rstd))
            dve.wait_ge(sem("big_row_landed"), 48)
            for t in range(NT):
                v.scalar_tensor_tensor(xn3[:, t, :], x3[:, t, :], rstd[:, t:t + 1], big_row, ALU.mult, ALU.mult)\
                    .then_inc(sem("final_ready"), 1)

        @block.scalar
        def _(act):
            s = nc.scalar
            step = Chain(act, sem("act_step"))
            eps_col, ln_col = c_("eps"), c_("ln_eps")

            def evacuate(dst, func, *name, scale=1.0, width=512, bias=None):
                bank = banks.read(act, *name)
                src = bank.ap[:, 0:width]
                if len(dst.shape) == 3:
                    src = blocks(src, dst.shape[1])
                s.activation(dst, src, func, scale=scale).then_inc(bank.freed, 1)

            def norm(k):
                for t in range(NT):
                    step(s.activation(xn3[:, t, :], x3[:, t, :], ACT.Square, accum_out=ssq2[:, t:t + 1]))
                s.activation(rstd, ssq2, ACT.Sqrt, scale=1.0 / D, bias=eps_col).then_inc(sem("rms_root"), 1)

            def take_turned(tag, scale, bias=None):
                for c in range(KC // 2):
                    bank = banks.read(act, tag, c)
                    for i in range(2):
                        k = 2 * c + i
                        kw = {} if bias is None else {"bias": bias(k)}
                        if scale is None:
                            last = s.activation(hT3[:, k, :], bank.ap[:, i * S:(i + 1) * S], ACT.Copy)
                        else:
                            last = s.activation(hT3[:, k, :], bank.ap[:, i * S:(i + 1) * S], ACT.Identity,
                                                scale=scale(k), **kw)
                    last.then_inc(bank.freed, 1)

            act.wait_ge(sem("const_landed"), 16)
            act.wait_ge(sem("x_landed"), 16)
            norm(1)
            act.wait_ge(sem("lb_shifted"), 1)
            s.activation(lb_e, lb_d, ACT.Exp).then_inc(sem("lb_exp"), 1)
            banks.wait_read(act, "vec")
            s.activation(cond, v2("c_2", 0, 8), ACT.Silu).then_inc(sem("cond_ready"), 1)
            take_turned("h_mix", lambda k: v1("attn_norm", k))
            for i in range(2):
                evacuate(hq[:, 2 * i:2 * i + 2, :], ACT.Silu, "in", 0, i)
            for i in range(2):
                evacuate(hf[:, 2 * i:2 * i + 2, :], ACT.Sigmoid, "in", 1, i)
            for t in range(NT):
                evacuate(hv[:, t, :], ACT.Copy, "hi", t)
            for i in range(2):
                evacuate(hgT[:, 2 * i:2 * i + 2, :], ACT.Silu, "in", 3, i)
            if stop < 1:
                return
            act.wait_ge(sem("low_mixed"), 1)
            step(s.activation(low[0:64, 0, :], low[0:64, 0, :], ACT.Tanh))
            s.activation(low[:, 1, :], low[:, 1, :], ACT.Sigmoid).then_inc(sem("low_ready"), 1)
            for tag, dst, col in (("lw", logdec, "rwkv_w0"), ("la", a_gate, "rwkv_a0")):
                for c in range(2):
                    bank = banks.read(act, tag, c)
                    for i in range(2):
                        j = 2 * c + i
                        last = s.activation(dst[:, j, :], bank.ap[:, i * S:(i + 1) * S], ACT.Sigmoid, bias=v1(col, j))
                    last.then_inc(bank.freed, 1)
            for c in range(2):
                evacuate(g_out[:, 2 * c:2 * c + 2, :], ACT.Copy, "lg", c)
            act.wait_ge(sem("hgrn_sq"), 1)
            s.activation(hg_ss, hg_ss, ACT.Sqrt).then_inc(sem("hgrn_root"), 1)
            if stop < 2:
                return
            for c in range(2):
                banks.wait_read(act, "kk", c)
            s.activation(page(21), page(21), ACT.Sqrt).then_inc(sem("kk_root"), 1)
            act.wait_ge(sem("cum_ready"), 1)
            step(s.activation(page(21), page(21), ACT.Exp))
            step(s.activation(page(22), page(12), ACT.Exp))
            s.activation(page(12), page(12), ACT.Exp, scale=-1.0).then_inc(sem("decays_exp"), 1)
            s.activation(s_scale, s_scale, ACT.Exp).then_inc(sem("scale_exp"), 1)
            for b in range(2):
                evacuate(bk_tok[:, b], ACT.Copy, "bk", b)
            for g in range(4):
                evacuate(inv[:, 4 * g:4 * g + 4, :], ACT.Copy, "x", 1, g)
            for m in LEVELS[1:]:
                for g in range(4):
                    evacuate(a_inv[:, 4 * g:4 * g + 4, :], ACT.Copy, "ax", m, g)
                if m != LEVELS[-1]:
                    for g in range(4):
                        evacuate(inv[:, 4 * g:4 * g + 4, :], ACT.Copy, "x", m, g)
            act.wait_ge(sem("rwkv_sq"), 1)
            s.activation(rw_ss, rw_ss, ACT.Sqrt).then_inc(sem("rwkv_root"), 1)
            if stop < 3:
                return

            def feed_forward(l):
                for n in range(2):
                    for t in range(NT):
                        banks.wait_read(act, "w_out" if l == 0 else "w_o", n, t)
                norm(2 if l == 0 else 4)
                take_turned(("h_mlp", l), lambda k: v1("mlp_norm", 8 * l + k))
                for c in range(8):
                    for i in range(2):
                        n = 2 * c + i
                        if n >= 4 or l:
                            act.wait_ge(sem("act_ready"), 16 * l + n - 3)
                        evacuate(relu[:, n % 4, :], ACT.Relu, "up", l, c, i)
                evacuate(pT, ACT.Copy, "pT", l)
                for n in range(2):
                    for t in range(NT):
                        evacuate(ple_raw[:, t, n * 512:(n + 1) * 512], ACT.Copy, "ple", l, n, t)
                for n in range(2):
                    for t in range(NT):
                        banks.wait_read(act, "ple", l, n, t)
                for t in range(NT):
                    step(s.activation(xn3[:, t, :], ple_raw[:, t, :], ACT.Square, accum_out=ssq2[:, t:t + 1]))
                s.activation(ssq, ssq2, ACT.Sqrt, scale=1.0 / D, bias=eps_col).then_inc(sem("ple_root"), 1)
                take_turned(("x_gate", l), None)
                for n in range(2):
                    for t in range(NT):
                        evacuate(gate_s[:, t, n * 512:(n + 1) * 512], ACT.Sigmoid, "gate", l, n, t)

            def attend(tag, probs, probsT, dst):
                n = 2 * HEADS
                for i in range(n + LAG):
                    if i < n:
                        t = i % 2
                        part = probs[:, i % 8, 0:(t + 1) * P]
                        act.wait_ge(sem(tag + "_max"), i + 1)
                        s.activation(part, part, ACT.Exp, bias=nmax[:, i:i + 1], accum_out=rsum[:, i:i + 1])\
                            .then_inc(sem(tag + "_exp"), 1)
                    if i >= LAG:
                        i2 = i - LAG
                        h, t = i2 // 2, i2 % 2
                        if i2 >= 4:
                            last_head = (i2 - 4) // 2
                            if last_head % 2:
                                banks.read(act, tag, "o", last_head // 2)
                            else:
                                act.wait_ge(sem(tag + "_even_read"), last_head // 2 + 1)
                        bank = banks.read(act, tag, "pT", i2)
                        s.activation(probsT[:, i2 % 4, 0:t + 1, :], blocks(bank.ap[:, 0:(t + 1) * P], t + 1), ACT.Copy)\
                            .then_inc(bank.freed, 1)
                        if i2 >= 5 and (i2 - 5) % 4 == 0:
                            c = (i2 - 5) // 4
                            evacuate(dst[:, 2 * c:2 * c + 2, :], ACT.Copy, tag, "o", c)
                evacuate(dst[:, 6:8, :], ACT.Copy, tag, "o", 3)

            feed_forward(0)
            if stop < 4:
                return
            act.wait_ge(sem("ple_added"), 1)
            norm(3)
            take_turned("h_att", lambda k: v1("attn_norm", 8 + k))
            for u, dst in enumerate((q_tok, q_tok, k_tok, k_tok, v_att, v_att)):
                for t in range(NT):
                    evacuate(dst[:, t, (u % 2) * 512:(u % 2 + 1) * 512], ACT.Copy, "qkv", u, t)
            for k in range(2):
                act.wait_ge(sem("head_sq"), k + 1)
                s.activation(head_ss, head_ss, ACT.Sqrt).then_inc(sem("head_root"), 1)
            for tag, dst in (("qT", qT), ("kT", kT)):
                for c in range(4):
                    evacuate(dst[:, 2 * c:2 * c + 2, :], ACT.Copy, tag, c)
            attend("att", prob, probT, hT3)
            feed_forward(1)
            if stop < 5:
                return
            act.wait_ge(sem("ple_added"), 2)
            norm(5)
            take_turned("h_in2", lambda k: sc1[:, k:k + 1], lambda k: modc[:, k:k + 1])
            evacuate(sig_gate, ACT.Sigmoid, "av", 1)
            for i in range(2):
                evacuate(qiT[:, 2 * i:2 * i + 2, :], ACT.Copy, "qi", i)
            evacuate(kiT, ACT.Copy, "ki", 0, width=S)
            act.wait_ge(sem("pool_zero"), 1)
            bank = banks.read(act, "pool", 0)
            s.activation(pool_s[0][:, :, 16:], blocks(bank.ap, 2), ACT.Copy).then_inc(bank.freed, 1)
            evacuate(wi.rearrange("p t h -> p (t h)"), ACT.Copy, "wi", width=16)
            evacuate(w_ukT, ACT.Copy, "ukT")
            act.wait_ge(sem("latent_sq"), 1)
            s.activation(cs, cs, ACT.Sqrt).then_inc(sem("latent_root"), 1)
            bank = banks.read(act, "cqT")
            for k in range(2):
                last = s.activation(cqT[:, k, :], bank.ap[:, k * S:(k + 1) * S], ACT.Identity, scale=v2("q_norm_g_2", k))
            last.then_inc(bank.freed, 1)
            evacuate(ckvT, ACT.Copy, "ckvT", width=S)
            for t in range(NT):
                for g in range(4):
                    n = 4 * t + g
                    if n >= 4:
                        act.wait_ge(sem("rel_used"), n - 3)
                    if n == 0:
                        for c in range(4):
                            banks.wait_read(act, "grow", c)
                    evacuate(rel[:, (n % 4) * 2:(n % 4) * 2 + 2, :], ACT.Relu, "idx", t, g)
            for i in range(2):
                evacuate(q2T[:, 2 * i:2 * i + 2, :], ACT.Copy, "q2", i)
            for g in range(4):
                bank = banks.read(act, "qabs", g)
                h0 = 4 * (g % 2) + g // 2
                s.activation(q_abs[:, h0:h0 + 3:2, :], blocks(bank.ap, 2), ACT.Copy).then_inc(bank.freed, 1)
            banks.wait_read(act, "cvar")
            s.activation(conv_m[:, 0, :], conv_m[:, 0, :], ACT.Sqrt).then_inc(sem("conv_root"), 1)
            act.wait_ge(sem("conv_normed"), 1)
            for c in range(2):
                s.activation(yT[:, c, :], conv_acc[:, c, :], ACT.Silu, scale=v2("conv_ln_g_2", c),
                             bias=v2("conv_ln_b_2", c)).then_inc(sem("conv_out"), 1)
            attend("dsa", prob2, probT2, ctxT)
            for g in range(2):
                rows_ = slice(64 * g, 64 * g + 64)
                for c in range(2):
                    bank = banks.read(act, "yatt", g, c)
                    s.activation(yT[rows_, 2 + 2 * c:4 + 2 * c, :], blocks(bank.ap, 2)[rows_], ACT.Copy)\
                        .then_inc(bank.freed, 1)
            if stop < 6:
                return
            act.wait_ge(sem("mix2_added"), 1)
            norm(6)
            take_turned("h_moe", lambda k: sc2[:, k:k + 1], lambda k: modc[:, 24 + k:25 + k])
            for t in range(NT):
                r = rt[t]
                act.wait_ge(sem("group_shifted"), t + 1)
                s.activation(r[:, 36:40], r[:, 36:40], ACT.Exp).then_inc(sem("route_exp"), 1)
                act.wait_ge(sem("expert_diff"), t + 1)
                s.activation(r[:, 34:35], r[:, 33:34], ACT.Exp).then_inc(sem("route_exp"), 1)
            with act.Fori(0, N_EXP) as e:
                for m in range(EC):
                    act.wait_ge(sem("moe_hidden"), e * EC + (m + 1))
                    act.wait_ge(sem("moe_hidden_read"), e * EC + (m + 1))
                    s.activation(exp_silu[:, m, :], bank_aps[4 + m][:, 0:S], ACT.Silu).then_inc(sem("moe_silu"), 1)
            act.wait_ge(sem("moe_added"), 1)
            norm(7)

        @block.sync
        def _(sp):
            sp.dma_start(x3, a["x"][0].rearrange("(t p) n -> p t n", p=P)).then_inc(sem("x_landed"), 16)
            for i, (name, parts) in enumerate(units):
                if i >= SLOTS and units[i - SLOTS][0] not in unit_read:
                    return
                if i >= SLOTS:
                    sp.wait_ge(*unit_read[units[i - SLOTS][0]])
                for dst, src in parts:
                    sp.dma_start(dst(slot(name)), src).then_inc(landed[i % SLOTS], 16)
            if stop < 6:
                return
            for i in range(3):
                sp.wait_ge(*unit_read[units[len(units) - SLOTS + i][0]])
            sources = [a["exp_w1_2"][0], a["exp_w3_2"][0], a["exp_w2_2"][0]]

            def load_expert(e, i):
                n = (len(units) + i) % SLOTS
                sp.dma_start(blocks(ring[:, n * UNIT:(n + 1) * UNIT], KC if i < 2 else EC), kcn(sources[i][e]))\
                    .then_inc(landed[n], 16)

            for i in range(3):
                load_expert(0, i)
            with sp.Fori(0, N_EXP - 1) as e:
                sp.wait_ge(sem("moe_hidden"), e * EC + EC)
                load_expert(e + 1, 0)
                load_expert(e + 1, 1)
                sp.wait_ge(sem("moe_down"), e + 2)
                load_expert(e + 1, 2)
            sp.wait_ge(sem("final_ready"), 2)
            sp.dma_start(out[0].rearrange("(t p) n -> p t n", p=P), xn3).then_inc(sem("out_written"), 16)
            sp.wait_ge(sem("out_written"), 16)

        @block.gpsimd
        def _(pool):
            pool.dma_start(const[:, :], a["constants"]).then_inc(sem("const_landed"), 16)
            pool.wait_ge(sem("vec_zero"), 1)
            at = 0
            for base, table in ((0, VECS1), (P, VECS2)):
                at = 0
                for name, n in table:
                    src = a[name]
                    flat = src.rearrange("a b -> (a b)") if len(src.shape) == 2 else src
                    pool.dma_start(vec_rows[at:at + n, base:base + P], flat.rearrange("(r c) -> r c", c=P))\
                        .then_inc(sem("vecs_landed"), 16)
                    at += n
            for name, n in ROWS:
                src = a[name]
                flat = src.rearrange("a b c -> (a b c)") if len(src.shape) == 3 else src.rearrange("a b -> (a b)")
                pool.dma_start(row(name), flat.partition_broadcast(P)).then_inc(sem("rows_landed"), 16)
            pool.dma_start(blocks(router[:, :], KC)[:, :, 0:4], kcn(a["router_g_w_2"][0]))\
                .then_inc(sem("router_landed"), 16)
            pool.dma_start(blocks(router[:, :], KC)[:, :, 4:36],
                           a["router_e_w_2"][0].rearrange("(k p) g e -> p k (g e)", p=P)).then_inc(sem("router_landed"), 16)
            pool.dma_start(big_row, a["ple_norm"][0].partition_broadcast(P)).then_inc(sem("big_row_landed"), 16)
            if stop < 3:
                return
            pool.wait_ge(sem("mixed_ready"), 1)
            for l in range(2):
                if l:
                    pool.wait_ge(sem("ple_added"), 1)
                pool.dma_start(p_tok, a["p"][l, 0].rearrange("(t p) n -> p t n", p=P)).then_inc(sem("p_landed"), 16)
                if l:
                    pool.dma_start(big_row, a["ple_norm"][1].partition_broadcast(P)).then_inc(sem("big_row_landed"), 16)
                if stop < 5:
                    return
            pool.wait_ge(sem("ple_added"), 2)
            pool.dma_start(big_row, a["final_g_2"].partition_broadcast(P)).then_inc(sem("big_row_landed"), 16)
            if stop < 6:
                return
            banks.wait_read(pool, "gT")
            pool.dma_start(gates_dram, gT).then_inc(sem("gates_out"), 16)
            pool.wait_ge(sem("gates_out"), 16)
            pool.dma_start(page(0, 8), gates_dram.rearrange("e t -> (e t)").partition_broadcast(P))\
                .then_inc(sem("gates_back"), 16)


INPUTS = [
    "x", "p", "attn_norm", "mlp_norm", "w_in_ar", "w_out_ar", "hgrn_lb", "hgrn_onorm", "rwkv_mu", "rwkv_w0",
    "rwkv_w2", "rwkv_a0", "rwkv_a2", "rwkv_g2", "rwkv_kk", "rwkv_ka", "rwkv_rk", "rwkv_ln_w", "rwkv_ln_b", "w_qkv",
    "w_o_attn", "q_norm", "k_norm", "w_up", "w_down", "ple_proj", "ple_norm", "ple_gate", "c_2", "mod_w_2", "mod_b_2",
    "norm1_g_2", "w_in_2", "conv_k_2", "conv_b_2", "conv_ln_g_2", "conv_ln_b_2", "q_norm_g_2", "kv_norm_g_2",
    "w_uq_2", "w_uk_2", "w_uv_2", "pool_w_2", "pool_scale_2", "w_out_2", "norm2_g_2", "router_g_w_2",
    "router_g_b_2", "router_e_w_2", "router_e_b_2", "exp_w1_2", "exp_w3_2", "exp_w2_2", "final_g_2",
]


def kernel(**inputs):
    import concourse.bacc as bacc
    from concourse.bass_utils import run_bass_kernel_spmd

    nc = bacc.Bacc("TRN2", target_bir_lowering=False, num_devices=1)
    arrays, args = {}, {}
    for name in INPUTS:
        a = np.ascontiguousarray(inputs[name])
        arrays[f"in_{name}"] = a
        args[name] = nc.dram_tensor(f"in_{name}", a.shape, mybir.dt.from_np(a.dtype), kind="ExternalInput").ap()
    table = constants()
    arrays["constants"] = table
    args["constants"] = nc.dram_tensor("constants", table.shape, F32, kind="ExternalInput").ap()
    out = nc.dram_tensor("out", (1, S, D), F32, kind="ExternalOutput").ap()
    build(nc, args, out)
    r = run_bass_kernel_spmd(nc, [arrays], core_ids=[0])
    return r.results[0]["out"]
```

```python
from contextlib import ExitStack

import numpy as np

import concourse.bass as bass
from concourse import mybir

P = 128
ALU = mybir.AluOpType
ACT = mybir.ActivationFunctionType
F32 = mybir.dt.float32
I32 = mybir.dt.int32
AX = mybir.AxisListType

D = 1024
S = 256
NT = S // P
KC = D // P
D_FF = 4 * D
FC = D_FF // P
HG_HEADS = 4
RW_HEADS = 8
RW_PAIRS = RW_HEADS // 2
HEADS = 8
PLE = 256
N_EXP = 32
D_EXP = 512
EC = D_EXP // P
EPS = 1e-6
LN_EPS = 64e-5
NEG = -1e30
TAPS = 31
DECAY_SCALE = -float(np.exp(-0.5))
UNIT = 4096
SLOTS = 3
LEVELS = [1, 2, 4, 8, 16, 32, 64]
MOD_COLUMNS = [(c, m) for c in (0, 1, 2, 3, 6, 7, 8, 9) for m in range(4)]
MOD_ROWS = [4, 5, 10, 11]
SLOTS_OF = 64
PAIRS = N_EXP // 2
MOE_SLOTS = 6
LAG = 4

CONST_WIDTHS = [
    ("ident", P), ("level", P * len(LEVELS)), ("strict", P), ("upto", P), ("ones", P), ("pairs", P),
    ("cos", NT * 64), ("sin", NT * 64), ("causal", S), ("allowed", NT * S), ("pool_inv", 2 * S),
    ("first", 8), ("iota", SLOTS_OF), ("eps", 1), ("ln_eps", 1), ("zero", P),
]

VECS1 = [
    ("attn_norm", 16), ("mlp_norm", 16), ("hgrn_lb", 12), ("hgrn_onorm", 4), ("rwkv_mu", 14), ("rwkv_w0", 4),
    ("rwkv_a0", 4), ("rwkv_kk", 4), ("rwkv_ka", 4), ("rwkv_rk", 4), ("rwkv_ln_w", 4), ("rwkv_ln_b", 4),
]
VECS2 = [
    ("mod_b_2", 48), ("norm1_g_2", 8), ("norm2_g_2", 8), ("conv_b_2", 2), ("conv_ln_g_2", 2), ("conv_ln_b_2", 2),
    ("q_norm_g_2", 2), ("pool_scale_2", 2), ("c_2", 8),
]
ROWS = [("q_norm", 128), ("k_norm", 128), ("kv_norm_g_2", 128), ("router_g_b_2", 4), ("router_e_b_2", 32)]


CONV_ROW = 96


def offsets(table):
    at, out = 0, {}
    for name, width in table:
        out[name] = (at, at + width)
        at += width
    return out, at


def constants():
    at, n = offsets(CONST_WIDTHS)
    c = np.zeros((P, n), np.float32)

    def put(name, value):
        s, e = at[name]
        c[:, s:e] = value

    s_, t_ = np.arange(P)[:, None], np.arange(P)[None, :]
    put("ident", np.eye(P))
    put("level", np.concatenate(
        [(s_ // (2 * m) == t_ // (2 * m)) & (s_ // m % 2 == 0) & (t_ // m % 2 == 1) for m in LEVELS], axis=1))
    put("strict", s_ < t_)
    put("upto", s_ <= t_)
    put("ones", 1.0)
    put("pairs", s_ // 64 == t_ // 64)
    half = 64
    inv = np.power(np.float32(10000.0), -np.arange(half, dtype=np.float32) / half).astype(np.float32)
    ang = np.arange(S, dtype=np.float32)[:, None] * inv[None, :]
    put("cos", np.cos(ang).reshape(NT, P, half).transpose(1, 0, 2).reshape(P, -1))
    put("sin", np.sin(ang).reshape(NT, P, half).transpose(1, 0, 2).reshape(P, -1))
    put("causal", np.concatenate([np.zeros((P, P)), np.where(t_ <= s_, 0.0, NEG)], axis=1))
    q = np.arange(S).reshape(NT, P)
    ok = np.arange(S)[None, None, :] // 64 <= q[:, :, None] // 64
    put("allowed", np.where(ok, 0.0, NEG).transpose(1, 0, 2).reshape(P, -1))
    windows = np.array([[2, 8], [4, 16]])[(np.arange(P) // 64)]
    put("pool_inv", (1.0 / np.minimum(np.arange(1, S + 1)[None, None, :], windows[:, :, None])).reshape(P, -1))
    put("first", 8.0 - np.arange(8))
    put("iota", np.arange(SLOTS_OF))
    put("eps", EPS)
    put("ln_eps", LN_EPS)
    return c


class Bank:

    def __init__(self, ap, full, freed, use):
        self.ap, self.full, self.freed, self.use = ap, full, freed, use


class Banks:

    def __init__(self, aps, full, freed):
        self.aps, self.full, self.freed, self.n, self.uses = aps, full, freed, 0, {}

    def take(self, pe, *name):
        b = self.n % len(self.aps)
        use = self.n // len(self.aps)
        self.n += 1
        assert name not in self.uses, name
        self.uses[name] = Bank(self.aps[b], self.full[b], self.freed[b], use)
        if use:
            pe.wait_ge(self.freed[b], use)
        return self.uses[name]

    def read(self, eng, *name):
        bank = self.uses[name]
        eng.wait_ge(bank.full, bank.use + 1)
        return bank

    def wait_read(self, eng, *name):
        bank = self.uses[name]
        eng.wait_ge(bank.freed, bank.use + 1)


class Chain:

    def __init__(self, eng, sem):
        self.eng, self.sem, self.n = eng, sem, 0

    def __call__(self, ins):
        ins.then_inc(self.sem, 1)
        self.n += 1
        self.eng.wait_ge(self.sem, self.n)


def kcn(w):
    return w.rearrange("(k p) n -> p k n", p=P)


def weight_units(a):
    units = []

    def grid(lo, k, n):
        return lambda s: s[:, lo:lo + k * n].rearrange("p (k n) -> p k n", k=k)

    def whole(name, w, n, width=512):
        for c in range(n):
            units.append(((*name, c), [(grid(0, KC, width), kcn(w[:, c * width:(c + 1) * width]))]))

    whole(("w_in",), a["w_in_ar"][0], 7)
    units.append((("w_in", 7), [(grid(0, KC, 256), kcn(a["w_in_ar"][0][:, 3584:3840]))]))
    units.append((("lora",), [(lambda s: s[0:64, 0:512], a["rwkv_w2"][0]),
                              (lambda s: s[64:128, 0:512], a["rwkv_a2"][0]),
                              (lambda s: s[:, 512:1024], a["rwkv_g2"][0])]))
    whole(("w_out",), a["w_out_ar"][0], 2)
    mods = [(("mod", c), [(grid(0, KC, 512), kcn(a["mod_w_2"][0][:, c * 512:(c + 1) * 512]))]) for c in range(12)]

    def mlp(l):
        for c in range(8):
            units.append((("up", l, c), [(grid(0, KC, 512), kcn(a["w_up"][l][:, c * 512:(c + 1) * 512]))]))
            if l == 0:
                units.append(mods[c])
        for n in range(2):
            for k in range(4):
                part = kcn(a["w_down"][l][k * D:(k + 1) * D, n * 512:(n + 1) * 512])
                units.append((("down", l, n, k), [(grid(0, KC, 512), part)]))
                if l == 0 and n == 0:
                    units.append(mods[8 + k])
        units.append((("ple", l), [(grid(0, 2, D), kcn(a["ple_proj"][l]))]))
        whole(("gate", l), a["ple_gate"][l], 2)

    mlp(0)
    whole(("qkv",), a["w_qkv"][0], 6)
    whole(("w_o",), a["w_o_attn"][0], 2)
    mlp(1)
    w = kcn(a["w_in_2"][0])
    units.append((("in2", 0), [(grid(0, KC, 512), w[:, :, 0:512])]))
    units.append((("in2", 1), [(grid(0, KC, 384), w[:, :, 512:896])]))
    units.append((("in2", 2), [(grid(0, KC, 512), w[:, :, 896:1408])]))
    twice = lambda d: lambda s: s[:, 0:KC * P].rearrange("p (k d n) -> p k d n", k=KC, d=2)[:, :, d, :]
    units.append((("in2", 3), [(twice(0), w[:, :, 1408:1472]), (twice(1), w[:, :, 1408:1472]),
                               (grid(KC * P, KC, 256), w[:, :, 1480:1736]),
                               (grid(KC * 384, KC, 8), w[:, :, 1472:1480])]))
    units.append((("dsa",), [
        (grid(0, 2, 512), a["w_uq_2"][0].rearrange("(k p) h d -> p k (h d)", p=P)),
        (lambda s: s[:, 1024:1536], a["w_uk_2"][0].rearrange("p h d -> p (h d)")),
        (lambda s: s[:, 1536:2048], a["w_uv_2"][0].rearrange("p h d -> p (h d)")),
        (grid(2048, 2, 64), a["pool_w_2"][0].rearrange("(c g) i o -> (g i) c o", c=2)),
    ]))
    whole(("w_out2",), a["w_out_2"][0], 2)
    return units


def build(nc, a, out):
    ctx = ExitStack()
    with ctx:
        def sb(name, cols, dt=F32):
            return ctx.enter_context(nc.sbuf_tensor(name, [P, cols], dt))

        cols_at, n_const = offsets(CONST_WIDTHS)
        v1_at, n_v1 = offsets(VECS1)
        v2_at, n_v2 = offsets(VECS2)
        rows_at, n_rows = offsets(ROWS)

        const = sb("const", n_const)
        rows = sb("rows", n_rows)
        vec = sb("vec", 2 * P)
        x = sb("x", NT * D)
        xn = sb("xn", NT * D)
        hT = sb("hT", KC * S)
        ring = sb("ring", SLOTS * UNIT)
        arena = sb("arena", 27 * 1024)
        big_row_t = sb("big_row", D)
        small = sb("small", 896)
        router = sb("router", KC * 36)
        most_int = sb("most_int", 1, I32)
        big_row = big_row_t[:, :]
        gates_dram = nc.dram_tensor("gates_scratch", [N_EXP, S], F32, kind="Internal").ap()

        sems = {}

        def sem(name):
            if name not in sems:
                sems[name] = ctx.enter_context(nc.semaphore(name))
            return sems[name]

        banks_mem = [ctx.enter_context(nc.psum_tensor(f"bank{i}", [P, 512], F32)) for i in range(8)]
        bank_aps = [b[:, :] for b in banks_mem]
        banks = Banks(bank_aps, [sem(f"bank_full{i}") for i in range(8)], [sem(f"bank_freed{i}") for i in range(8)])

        def c_(name, lo=0, hi=None):
            s, e = cols_at[name]
            return const[:, s + lo:(e if hi is None else s + hi)]

        ident, ones, pairs = c_("ident"), c_("ones"), c_("pairs")
        zeros = c_("zero")

        def level_mask(m):
            i = LEVELS.index(m)
            return c_("level", i * P, (i + 1) * P)

        def v1(name, i, n=1):
            s = v1_at[name][0] + i
            return vec[:, s:s + n]

        def v2(name, i, n=1):
            s = P + v2_at[name][0] + i
            return vec[:, s:s + n]

        def row(name, lo=0, hi=None):
            s, e = rows_at[name]
            return rows[:, s + lo:(e if hi is None else s + hi)]

        small_used = [0]

        def tiny(n):
            at = small_used[0]
            small_used[0] += n
            assert small_used[0] <= 896
            return small[:, at:at + n]

        def page(i, n=1):
            return arena[:, i * 1024:(i + n) * 1024]

        def half(i, n=1):
            return arena[:, i * 512:(i + n) * 512]

        def blocks(ap, j):
            return ap.rearrange("p (j t) -> p j t", j=j)

        def mid(ap, n):
            return ap.unsqueeze(1).to_broadcast([ap.shape[0], n, ap.shape[1]])

        def tail(ap, w):
            return ap.unsqueeze(2).to_broadcast([ap.shape[0], ap.shape[1], w])

        x3, xn3, hT3 = blocks(x[:, :], NT), blocks(xn[:, :], NT), blocks(hT[:, :], KC)
        vec_rows = page(26)[:, 0:2 * P]

        raw = arena[:, 0:14 * 257].rearrange("p (b t) -> p b t", b=14)
        mixed = page(4, 4)
        r_mix, k_mix, logdec, kk = (blocks(page(i), 4) for i in (4, 5, 6, 7))
        v_mix, low = blocks(page(8), 4), blocks(half(18), 2)
        a_gate, g_out, cum, k_adj = (blocks(page(i), 4) for i in (10, 11, 12, 13))
        ar = page(14, 2).rearrange("p (j t a s) -> p j t a s", j=4, t=NT, a=2)
        b_til, k_til, bonus = (blocks(page(i), 4) for i in (16, 17, 18))
        v_tok = blocks(page(19), NT)
        bk_tok = page(20).rearrange("p (b j s) -> p b j s", b=2, j=4)
        y_tok = blocks(page(21), NT)
        w_sb, sa_sb = half(44), half(45)
        ab = page(23, 4).rearrange("p (i a s) -> p i a s", i=16, a=2)
        ak = page(4, 4).rearrange("p (i a s) -> p i a s", i=16, a=2)
        inv, invT = blocks(page(0, 2), 16), blocks(page(2, 2), 16)
        a_inv = blocks(xn[:, :], 16)
        s1 = arena[:, 19 * 512:19 * 512 + 256].rearrange("p (j v) -> p j v", j=4)
        hq, hk, hf, hgT = (blocks(page(i), 4) for i in (13, 14, 15, 16))
        hv = blocks(page(17), NT)
        h_end = [page(18), page(22)]
        st = page(19).rearrange("p (t h s) -> p t h s", t=NT, h=4)
        sx = blocks(half(40), 4)
        o_a, o_sq = blocks(page(21), NT), blocks(page(23), NT)

        q_tok, k_tok, v_att = (blocks(page(i, 2), NT) for i in (0, 2, 4))
        qT, kT = blocks(page(6, 2), HEADS), blocks(page(8, 2), HEADS)
        rot, sq = page(10, 2), page(12, 2)
        prob, probT = blocks(page(14, 2), 8), page(16).rearrange("p (b k q) -> p b k q", b=4, k=2)

        actT = blocks(page(0, 8), FC)
        relu = blocks(page(8, 2), 4)
        p_tok, pT = blocks(half(40), NT), blocks(half(41), 2)
        ple_raw, gate_s = blocks(page(21, 2), NT), blocks(page(23, 2), NT)

        mod_acc = blocks(page(11, 6), 12)

        u_pad = arena[:, 0:2 * (S + TAPS - 1)].rearrange("p (c t) -> p c t", c=2)
        conv_acc, conv_sq, sig_gate = blocks(half(2), 2), blocks(half(3), 2), blocks(half(4), 2)
        conv_col = vec[:, :].rearrange("p (c r) -> p c r", c=2)[:, :, CONV_ROW:CONV_ROW + TAPS]
        conv_m = blocks(half(6), 2)
        cq_tok = page(4)[:, 0:768].rearrange("p (t n) -> p t n", t=NT)
        cqT = blocks(half(10), 2)
        ckvT, ckv_tok = page(5)[:, 512:768], blocks(page(5)[:, 768:1024], NT)
        qiT = blocks(page(6), 4)
        kiT, wi = page(7)[:, 0:256], page(7)[:, 256:272].rearrange("p (t h) -> p t h", t=NT)
        cq_sq = page(7)[:, 272:656]
        w_ukT, pool_d = blocks(half(16), 4), blocks(half(17), 2)
        pool_s = [arena[:, i * 1024:i * 1024 + 2 * (S + 16)].rearrange("p (c t) -> p c t", c=2) for i in (9, 10, 11)]
        q2T, q_abs = blocks(page(12), 4), blocks(page(13, 2), 8)
        score, work = blocks(half(30), NT), blocks(half(31), NT)
        rel = blocks(page(16, 2), 8)
        bias2 = blocks(half(36), NT)
        prob2, probT2 = blocks(page(19, 2), 8), page(21).rearrange("p (b k q) -> p b k q", b=4, k=2)
        ctxT = blocks(page(22, 2), 8)
        yT = hT3
        g1_row, g2_row = page(25), page(26)
        scaled = half(48)

        gate_all = blocks(page(0, 8), N_EXP)
        exp_act, exp_silu = blocks(page(8), EC), blocks(page(9), EC)
        gT = arena[0:N_EXP, 10 * 1024:10 * 1024 + S]

        gathered = blocks(page(0), KC)
        select = [blocks(arena[:, 1024 + i * S:1024 + (i + 1) * S], NT) for i in range(2)]
        spread = [arena[:, 1024 + (2 + i) * S:1024 + (3 + i) * S] for i in range(2)]
        pair_act, pair_silu = half(4), half(5)
        pair_actT, pair_y = blocks(half(6), EC), page(4)
        moe_slot = [ring[:, i * UNIT:(i + 1) * UNIT] for i in range(SLOTS)] + \
                   [page(12 + 4 * i, 4) for i in range(MOE_SLOTS - SLOTS)]
        slot_gate = [tiny(1), tiny(1)]

        ssq, ssq2, rstd, flags = tiny(NT), tiny(NT), tiny(NT), tiny(24)
        lb_d, lb_e, lb, lb_c = tiny(12), tiny(12), tiny(4), tiny(4)
        hg_ss, rw_mu, rw_ss = tiny(8), tiny(16), tiny(16)
        c_mid, c_end, s_scale = tiny(8), tiny(8), tiny(4)
        head_ss = tiny(16)
        nmax, rsum, rinv = tiny(16), tiny(16), tiny(16)
        cond, modc = tiny(8), tiny(48)
        sc1, sc2 = tiny(8), tiny(8)
        cs = tiny(4)
        top8 = tiny(8)
        lg = tiny(72).rearrange("p (t n) -> p t n", t=NT)
        rt = [tiny(64) for _ in range(4)]
        gates = tiny(NT * (N_EXP + 2)).rearrange("p (t n) -> p t n", t=NT)
        rank = tiny(NT * (N_EXP + 4)).rearrange("p (t n) -> p t n", t=NT)
        chosen = tiny(NT * N_EXP).rearrange("p (t n) -> p t n", t=NT)
        most = tiny(1)

        units = weight_units(a)
        unit_of = {name: i for i, (name, _) in enumerate(units)}
        landed_value, slot_total = {}, [0] * SLOTS
        for i, (name, parts) in enumerate(units):
            slot_total[i % SLOTS] += 16 * len(parts)
            landed_value[name] = slot_total[i % SLOTS]
        landed = [sem(f"slot_landed{i}") for i in range(SLOTS)]
        unit_read = {("mod", c): (sem("mod_used"), c + 1) for c in range(12)}

        def slot(name):
            s = unit_of[name] % SLOTS
            return ring[:, s * UNIT:(s + 1) * UNIT]

        def weights(pe, *name):
            pe.wait_ge(landed[unit_of[name] % SLOTS], landed_value[name])
            return slot(name)

        def read_by(bank, *name):
            unit_read[name] = (bank.full, bank.use + 1)


        moe_full = [sem(f"moe_full{b}") for b in range(4)]
        moe_freed = [sem(f"moe_freed{b}") for b in range(4)]
        mb = bank_aps[4:8]
        moe_landed = landed + [sem(f"slot_landed{i}") for i in range(SLOTS, MOE_SLOTS)]
        landed_before = slot_total + [0] * (MOE_SLOTS - SLOTS)
        HIDDEN, MIDDLE, DOWN = 0, 1, 2

        def filled(p6, q, phase):
            return p6 + (3 * q + phase + 2)

        def dense_pe(pe, y_bank):
            mm = nc.tensor.matmul
            w = [blocks(ring[:, i * UNIT:(i + 1) * UNIT], KC if i < 2 else EC) for i in range(3)]
            with pe.Fori(0, N_EXP) as e:
                for m in range(EC):
                    if m == 0:
                        for i in range(2):
                            pe.wait_ge(landed[i], e * 16 + (slot_total[i] + 32))
                    pe.wait_ge(sem("moe_hidden_read"), e * EC + (m + 1))
                    for i in range(2):
                        for k in range(KC):
                            last = mm(bank_aps[4 + m][:, i * S:(i + 1) * S], w[i][:, k, m * P:(m + 1) * P],
                                      hT3[:, k, :], start=(k == 0), stop=(k == KC - 1), skip_group_check=True)
                    last.then_inc(sem("moe_hidden"), 1)
                pe.wait_ge(landed[2], e * 16 + (slot_total[2] + 32))
                for m in range(EC):
                    pe.wait_ge(sem("moe_act"), e * EC + (m + 1))
                    for t in range(NT):
                        for n in range(2):
                            last = mm(y_bank[t][n], exp_act[:, m, t * P:(t + 1) * P],
                                      w[2][:, m, n * 512:(n + 1) * 512], start=False, stop=False,
                                      skip_group_check=True)
                last.then_inc(sem("moe_down"), 1)

        def sparse_pe(pe, y_bank):
            mm = nc.tensor.matmul

            def gather(side, first):
                for k in range(KC):
                    dst = mb[k // 4][:, (k % 4) * P:(k % 4 + 1) * P]
                    for t in range(NT):
                        last = mm(dst, xn3[:, t, k * P:(k + 1) * P], select[side][:, t, :], start=(t == 0),
                                  stop=(t == NT - 1), skip_group_check=True)
                    if k % 4 == 3:
                        last.then_inc(moe_full[k // 4], 1)
                for t in range(NT):
                    nc.tensor.transpose(mb[2][:, t * P:(t + 1) * P], select[side][:, t, :], ident)
                for t in range(NT):
                    last = mm(mb[2][:, S:S + 2], select[side][:, t, :], gates[:, t, bass.ds(first, 2)],
                              start=(t == 0), stop=(t == NT - 1), skip_group_check=True)
                last.then_inc(moe_full[2], 1)

            def scatter(side):
                for t in range(NT):
                    for n in range(2):
                        mm(y_bank[t][n], spread[side][:, t * P:(t + 1) * P], pair_y[:, n * 512:(n + 1) * 512],
                           start=False, stop=False, skip_group_check=True)

            pe.wait_ge(sem("selected"), 1)
            gather(0, 0)
            for b in range(3):
                pe.wait_ge(moe_freed[b], 1)
            with pe.Fori(0, PAIRS // 2) as pp:
                p6 = pp * 6
                for q in range(2):
                    for b in range(4):
                        i = b if b < 4 else None
                        pe.wait_ge(moe_freed[b], filled(p6, q, HIDDEN) - 1)
                    for b in range(4):
                        pe.wait_ge(moe_landed[b], pp * 32 + (landed_before[b] + 16 * (q + 1)))
                        w = blocks(moe_slot[b], KC)
                        for k in range(KC):
                            last = mm(mb[b], gathered[:, k, :], w[:, k, :], start=(k == 0), stop=(k == KC - 1),
                                      skip_group_check=True)
                        last.then_inc(moe_full[b], 1)
                    scatter(1 - q)
                    pe.wait_ge(sem("selected"), pp * 2 + (q + 2))
                    for b in range(3):
                        pe.wait_ge(moe_freed[b], filled(p6, q, MIDDLE) - 1)
                    gather(1 - q, pp * 4 + (2 * q + 2))
                    pe.wait_ge(moe_freed[3], filled(p6, q, MIDDLE) - 1)
                    for m in range(EC):
                        last = nc.tensor.transpose(mb[3][:, m * P:(m + 1) * P], pair_act[:, m * P:(m + 1) * P], ident)
                    last.then_inc(moe_full[3], 1)
                    for b in range(4):
                        pe.wait_ge(moe_freed[b], filled(p6, q, DOWN) - 1)
                    for i in range(2):
                        b = 4 + i
                        pe.wait_ge(moe_landed[b], pp * 32 + (landed_before[b] + 16 * (q + 1)))
                        w = blocks(moe_slot[b], EC)
                        for n in range(2):
                            for m in range(EC):
                                last = mm(mb[2 * i + n], pair_actT[:, m, :], w[:, m, n * 512:(n + 1) * 512],
                                          start=(m == 0), stop=(m == EC - 1), skip_group_check=True)
                            last.then_inc(moe_full[2 * i + n], 1)
            for b in range(4):
                pe.wait_ge(moe_freed[b], 3 * PAIRS + 1)
            scatter(1)

        def dense_dve(dve):
            v = nc.vector
            dve.wait_ge(sem("gates_back"), 16)
            flag = iter([flags[:, 20 + i:21 + i] for i in range(EC)])
            for m in range(EC):
                v.memset(next(flag), 0.0).then_inc(sem("moe_hidden_read"), 1)
            with dve.Fori(0, N_EXP) as e:
                dve.wait_ge(sem("moe_down"), e + 1)
                for m in range(EC):
                    dve.wait_ge(sem("moe_silu"), e * EC + (m + 1))
                    v.tensor_tensor(exp_act[:, m, :], exp_silu[:, m, :], bank_aps[4 + m][:, S:2 * S], ALU.mult)\
                        .then_inc(sem("moe_hidden_read"), 1)
                    dve.wait_ge(sem("moe_hidden_read"), e * EC + (EC + m + 1))
                    v.tensor_tensor(exp_act[:, m, :], exp_act[:, m, :], gate_all[:, e, :], ALU.mult)\
                        .then_inc(sem("moe_act"), 1)

        def sparse_dve(dve):
            v = nc.vector
            iota = c_("iota")

            def choose(side, first):
                for t in range(NT):
                    for i in range(2):
                        last = v.tensor_scalar(select[side][:, t, i * SLOTS_OF:(i + 1) * SLOTS_OF], iota,
                                               rank[:, t, bass.ds(first + i, 1)], None, ALU.is_equal)
                last.then_inc(sem("selected"), 1)

            def keep_gathered(side, value):
                for b in range(2):
                    dve.wait_ge(moe_full[b], value)
                    for k in range(4 * b, 4 * b + 4):
                        last = v.tensor_scalar(gathered[:, k, :], mb[b][:, (k % 4) * P:(k % 4 + 1) * P],
                                               sc2[:, k:k + 1], modc[:, 24 + k:25 + k], ALU.mult, ALU.add)
                    last.then_inc(moe_freed[b], 1)
                dve.wait_ge(moe_full[2], value)
                v.tensor_copy(spread[side], mb[2][:, 0:S])
                v.tensor_copy(slot_gate[side][0:64, :], mb[2][0:64, S:S + 1])
                v.tensor_copy(slot_gate[side][64:P, :], mb[2][64:P, S + 1:S + 2]).then_inc(moe_freed[2], 1)

            v.memset(pair_y, 0.0).then_inc(sem("dve_moe"), 1)
            v.memset(spread[1], 0.0).then_inc(sem("dve_moe"), 1)
            v.memset(flags[:, 20:21], 0.0).then_inc(moe_freed[3], 1)
            choose(0, 0)
            keep_gathered(0, 1)
            choose(1, 2)
            with dve.Fori(0, PAIRS // 2) as pp:
                p6 = pp * 6
                for q in range(2):
                    for i in range(2):
                        rows_ = slice(64 * i, 64 * i + 64)
                        dve.wait_ge(moe_freed[2 * i], filled(p6, q, HIDDEN))
                        dve.wait_ge(moe_full[2 * i + 1], filled(p6, q, HIDDEN) - i)
                        v.tensor_tensor(pair_act[rows_, :], pair_silu[rows_, :], mb[2 * i + 1][rows_, :], ALU.mult)\
                            .then_inc(moe_freed[2 * i + 1], 1)
                    keep_gathered(1 - q, filled(p6, q, MIDDLE))
                    choose(q, pp * 4 + (2 * q + 4))
                    for n in range(2):
                        dve.wait_ge(moe_full[2 + n], filled(p6, q, DOWN) - n)
                        v.tensor_scalar(pair_y[64:P, n * 512:(n + 1) * 512], mb[2 + n][64:P, :],
                                        slot_gate[q][64:P, :], None, ALU.mult).then_inc(moe_freed[2 + n], 1)

        def dense_act(act):
            with act.Fori(0, N_EXP) as e:
                for m in range(EC):
                    act.wait_ge(sem("moe_hidden"), e * EC + (m + 1))
                    act.wait_ge(sem("moe_hidden_read"), e * EC + (m + 1))
                    nc.scalar.activation(exp_silu[:, m, :], bank_aps[4 + m][:, 0:S], ACT.Silu)\
                        .then_inc(sem("moe_silu"), 1)

        def sparse_act(act):
            s = nc.scalar
            act.wait_ge(sem("dve_moe"), 2)
            with act.Fori(0, PAIRS // 2) as pp:
                p6 = pp * 6
                for q in range(2):
                    for i in range(2):
                        rows_ = slice(64 * i, 64 * i + 64)
                        act.wait_ge(moe_full[2 * i], filled(p6, q, HIDDEN))
                        s.activation(pair_silu[rows_, :], mb[2 * i][rows_, :], ACT.Silu).then_inc(moe_freed[2 * i], 1)
                    act.wait_ge(moe_full[3], filled(p6, q, MIDDLE) - 1)
                    s.activation(pair_actT, blocks(mb[3], EC), ACT.Copy).then_inc(moe_freed[3], 1)
                    for n in range(2):
                        act.wait_ge(moe_full[n], filled(p6, q, DOWN))
                        s.activation(pair_y[0:64, n * 512:(n + 1) * 512], mb[n][0:64, :], ACT.Copy,
                                     scale=slot_gate[q][0:64, :]).then_inc(moe_freed[n], 1)

        def load_vectors(eng, base, table, half_):
            eng.wait_ge(sem("vec_zero"), 1)
            at = 0
            for name, n in table:
                src = a[name]
                flat = src.rearrange("a b -> (a b)") if len(src.shape) == 2 else src
                eng.dma_start(vec_rows[at:at + n, base:base + P], flat.rearrange("(r c) -> r c", c=P))\
                    .then_inc(sem(f"vecs_landed{half_}"), 16)
                at += n
            assert at <= CONV_ROW
            eng.dma_start(vec_rows[CONV_ROW:CONV_ROW + TAPS, base:base + P], a["conv_k_2"][0, :, base:base + P])\
                .then_inc(sem(f"vecs_landed{half_}"), 16)

        block = ctx.enter_context(nc.Block())

        @block.tensor
        def _(pe):
            mm = nc.tensor.matmul

            def transposes(pairs_, bank):
                for dst, src in pairs_:
                    last = nc.tensor.transpose(dst, src, ident[0:src.shape[0], 0:src.shape[0]])
                last.then_inc(bank.full, 1)

            def norm_turn(tag, count, source=None):
                src = xn3 if source is None else source
                for c in range(KC // 2):
                    bank = banks.take(pe, tag, c)
                    if c == 0 and count:
                        pe.wait_ge(sem("normed"), NT * count)
                    transposes([(bank.ap[:, i * S + t * P:i * S + (t + 1) * P],
                                 src[:, t, (2 * c + i) * P:(2 * c + i + 1) * P])
                                for i in range(2) for t in range(NT)], bank)

            def turned(tag):
                for c in range(KC // 2):
                    banks.wait_read(pe, tag, c)

            def to_features(tag, w, act, kcs, cols):
                for c in range(0, len(cols), 2):
                    bank = banks.take(pe, *tag, c // 2)
                    for i, m in enumerate(cols[c:c + 2]):
                        for k in range(kcs):
                            last = mm(bank.ap[:, i * S:(i + 1) * S], w[:, k, m:m + P], act[:, k, :],
                                      start=(k == 0), stop=(k == kcs - 1))
                    last.then_inc(bank.full, 1)
                return bank

            def to_tokens(tag, w, act, kcs, n):
                for t in range(NT):
                    bank = banks.take(pe, *tag, t)
                    for k in range(kcs):
                        last = mm(bank.ap[:, 0:n], act[:, k, t * P:(t + 1) * P], w[:, k, 0:n],
                                  start=(k == 0), stop=(k == kcs - 1))
                    last.then_inc(bank.full, 1)
                return bank

            def token_units(tag, count, act):
                for c in range(count):
                    w = blocks(weights(pe, *tag, c), KC)
                    read_by(to_tokens((*tag, c), w, act, KC, 512), *tag, c)

            four = [i * P for i in range(4)]

            pe.wait_ge(sem("const_landed"), 16)
            pe.wait_ge(sem("vec_zero"), 1)
            def vector_columns(i, table):
                pe.wait_ge(sem(f"vecs_landed{i}"), 16 * (len(table) + 1))
                bank = banks.take(pe, "vec", i)
                transposes([(bank.ap[:, 0:P], vec_rows[:, i * P:(i + 1) * P])], bank)

            vector_columns(0, VECS1)
            norm_turn("h_mix", 1)
            turned("h_mix")
            for c in range(8):
                w = weights(pe, "w_in", c)
                if c == 2:
                    bank = to_tokens(("hi",), blocks(w, KC), hT3, KC, 512)
                elif c < 7:
                    bank = to_features(("in", c), blocks(w, KC), hT3, KC, four)
                else:
                    bank = to_features(("in", c), blocks(w[:, 0:KC * 256], KC), hT3, KC, four[:2])
                read_by(bank, "w_in", c)
                if c == 3:
                    vector_columns(1, VECS2)

            lora = weights(pe, "lora")
            pe.wait_ge(sem("low_ready"), 1)
            for tag, p0, col, b in (("lw", 0, 0, 0), ("la", 64, 0, 0), ("lg", 0, 512, 1)):
                p1 = P if tag != "lw" else 64
                for c in range(2):
                    bank = banks.take(pe, tag, c)
                    for i in range(2):
                        m = col + (2 * c + i) * P
                        last = mm(bank.ap[:, i * S:(i + 1) * S], lora[p0:p1, m:m + P], low[p0:p1, b, :],
                                  start=True, stop=True)
                    last.then_inc(bank.full, 1)
            read_by(bank, "lora")

            for i, m in enumerate([0] + LEVELS):
                pe.wait_ge(sem("hgrn_scaled"), i + 1)
                for t in range(NT):
                    bank = banks.take(pe, "hs", m, t)
                    for h in range(HG_HEADS):
                        last = mm(bank.ap[:, h * P:(h + 1) * P], hk[:, h, t * P:(t + 1) * P],
                                  hq[:, h, t * P:(t + 1) * P], start=True, stop=True)
                    last.then_inc(bank.full, 1)
            pe.wait_ge(sem("hgrn_scaled"), len(LEVELS) + 2)
            bank = banks.take(pe, "hs", P)
            for h in range(HG_HEADS):
                last = mm(bank.ap[:, h * P:(h + 1) * P], hk[:, h, 0:P], hq[:, h, P:S], start=True, stop=True)
            last.then_inc(bank.full, 1)
            for t in range(NT):
                banks.wait_read(pe, "hi", t)
            banks.wait_read(pe, "hs", LEVELS[-1], 0)
            banks.wait_read(pe, "hs", LEVELS[-1], 1)
            banks.wait_read(pe, "hs", P)
            for t in range(NT):
                bank = banks.take(pe, "ho", t)
                for h in range(HG_HEADS):
                    col = slice(h * P, (h + 1) * P)
                    last = mm(bank.ap[:, col], st[:, t, h, :], hv[:, t, col], start=True, stop=(t == 0))
                    if t:
                        last = mm(bank.ap[:, col], sx[:, h, :], hv[:, 0, col], start=False, stop=True)
                last.then_inc(bank.full, 1)
            pe.wait_ge(sem("hgrn_normed"), 1)
            for c in range(2):
                bank = banks.take(pe, "ha", c)
                transposes([(bank.ap[:, i * S + t * P:i * S + (t + 1) * P], o_a[:, t, (2 * c + i) * P:(2 * c + i + 1) * P])
                            for i in range(2) for t in range(NT)], bank)

            pe.wait_ge(sem("kk_sq"), 1)
            for c in range(2):
                bank = banks.take(pe, "kk", c)
                mm(bank.ap[:, :], pairs, page(21)[:, c * 512:(c + 1) * 512], start=True, stop=True).then_inc(bank.full, 1)
            for t in range(NT):
                bank = banks.take(pe, "vt", t)
                transposes([(bank.ap[:, j * P:(j + 1) * P], v_mix[:, j, t * P:(t + 1) * P]) for j in range(4)], bank)
            pe.wait_ge(sem("rk_prod"), 1)
            for c in range(2):
                bank = banks.take(pe, "bonus", c)
                mm(bank.ap[:, :], pairs, page(22)[:, c * 512:(c + 1) * 512], start=True, stop=True).then_inc(bank.full, 1)
            pe.wait_ge(sem("tilded"), 1)
            for b, src in enumerate((b_til, k_til)):
                bank = banks.take(pe, "bk", b)
                transposes([(bank.ap[:, j * P:(j + 1) * P], src[:, j, 0:P]) for j in range(4)], bank)
            for i in range(16):
                t, h = i // 8, i % 8
                j, rows_ = h // 2, slice(64 * (h % 2), 64 * (h % 2) + 64)
                bank = banks.take(pe, "pairs", i)
                for b, src in enumerate((b_til, k_til)):
                    last = mm(bank.ap[:, b * S:(b + 1) * S], src[rows_, j, t * P:(t + 1) * P],
                              ar[rows_, j, t, :, :], start=True, stop=True)
                last.then_inc(bank.full, 1)
            pe.wait_ge(sem("inv_first"), 1)
            for g in range(4):
                bank = banks.take(pe, "x", 1, g)
                transposes([(bank.ap[:, i * P:(i + 1) * P], invT[:, 4 * g + i, :]) for i in range(4)], bank)
            for n, m in enumerate(LEVELS[1:]):
                for g in range(4):
                    banks.wait_read(pe, "x", LEVELS[n], g)
                    bank = banks.take(pe, "ax", m, g)
                    for i in range(4):
                        last = mm(bank.ap[:, i * P:(i + 1) * P], ab[:, 4 * g + i, 0, :], inv[:, 4 * g + i, :],
                                  start=True, stop=True)
                    last.then_inc(bank.full, 1)
                for g in range(4):
                    banks.wait_read(pe, "ax", m, g)
                    bank = banks.take(pe, "xax", m, g)
                    for i in range(4):
                        last = mm(bank.ap[:, i * P:(i + 1) * P], a_inv[:, 4 * g + i, :], invT[:, 4 * g + i, :],
                                  start=True, stop=True)
                    last.then_inc(bank.full, 1)
                if m != LEVELS[-1]:
                    for g in range(4):
                        banks.wait_read(pe, "xax", m, g)
                        bank = banks.take(pe, "x", m, g)
                        transposes([(bank.ap[:, i * P:(i + 1) * P], invT[:, 4 * g + i, :]) for i in range(4)], bank)
            for g in range(4):
                banks.wait_read(pe, "xax", LEVELS[-1], g)
            for t in range(NT):
                for half_ in range(2):
                    rows_ = slice(64 * half_, 64 * half_ + 64)
                    bank = banks.take(pe, "w", t, half_)
                    for j in range(RW_PAIRS):
                        col, h = slice(j * 64, (j + 1) * 64), 2 * j + half_
                        last = mm(bank.ap[:, col], ak[:, 8 * t + h, 0, :], v_tok[:, t, h * 64:(h + 1) * 64],
                                  start=True, stop=(t == 0))
                        if t:
                            last = mm(bank.ap[:, col], ar[rows_, j, t, 0, :], s1[rows_, j, :], start=False, stop=True)
                    last.then_inc(bank.full, 1)
                for half_ in range(2):
                    banks.wait_read(pe, "w", t, half_)
                bank = banks.take(pe, "sa", t)
                for h in range(RW_HEADS):
                    col = slice(h * 64, (h + 1) * 64)
                    last = mm(bank.ap[:, col], invT[:, 8 * t + h, :], w_sb[:, col], start=True, stop=True)
                last.then_inc(bank.full, 1)
                banks.wait_read(pe, "sa", t)
                if t == 0:
                    bank = banks.take(pe, "state")
                    for j in range(4):
                        col = slice(j * P, (j + 1) * P)
                        mm(bank.ap[:, col], bk_tok[:, 0, j, :], sa_sb[:, col], start=True, stop=False)
                        last = mm(bank.ap[:, col], bk_tok[:, 1, j, :], v_tok[:, 0, col], start=False, stop=True)
                    last.then_inc(bank.full, 1)
                for half_ in range(2):
                    rows_ = slice(64 * half_, 64 * half_ + 64)
                    bank = banks.take(pe, "y", t, half_)
                    for j in range(RW_PAIRS):
                        col, h = slice(j * 64, (j + 1) * 64), 2 * j + half_
                        own = slice(h * 64, (h + 1) * 64)
                        mm(bank.ap[:, col], ab[:, 8 * t + h, 1, :], sa_sb[:, own], start=True, stop=False)
                        last = mm(bank.ap[:, col], ak[:, 8 * t + h, 1, :], v_tok[:, t, own],
                                  start=False, stop=(t == 0))
                        if t:
                            last = mm(bank.ap[:, col], ar[rows_, j, t, 1, :], s1[rows_, j, :], start=False, stop=True)
                    last.then_inc(bank.full, 1)
                if t == 0:
                    pe.wait_ge(sem("state_ready"), 1)
                    banks.wait_read(pe, "state")
            pe.wait_ge(sem("rwkv_normed"), 1)
            for c in range(2):
                bank = banks.take(pe, "yb", c)
                transposes([(bank.ap[:, i * S + t * P:i * S + (t + 1) * P], y_tok[:, t, (2 * c + i) * P:(2 * c + i + 1) * P])
                            for i in range(2) for t in range(NT)], bank)

            pe.wait_ge(sem("mixed_ready"), 1)
            token_units(("w_out",), 2, hT3)

            def feed_forward(l):
                norm_turn(("h_mlp", l), 2 if l == 0 else 4)
                turned(("h_mlp", l))
                for c in range(8):
                    w = blocks(weights(pe, "up", l, c), KC)
                    read_by(to_features(("up", l, c), w, hT3, KC, four), "up", l, c)
                pe.wait_ge(sem("act_ready"), 16 * (l + 1))
                for n in range(2):
                    pair = [banks.take(pe, "down", l, n, t) for t in range(NT)]
                    for kb in range(4):
                        w = blocks(weights(pe, "down", l, n, kb), KC)
                        for t in range(NT):
                            for k in range(KC):
                                last = mm(pair[t].ap[:, :], actT[:, kb * KC + k, t * P:(t + 1) * P], w[:, k, :],
                                          start=(kb == 0 and k == 0), stop=(kb == 3 and k == KC - 1))
                            if kb == 3:
                                last.then_inc(pair[t].full, 1)
                        if kb < 3:
                            last.then_inc(sem("down_read"), 1)
                            unit_read[("down", l, n, kb)] = (sem("down_read"), 6 * l + 3 * n + kb + 1)
                        else:
                            read_by(pair[1], "down", l, n, kb)
                if l == 0:
                    pe.wait_ge(sem("mod_used"), 12)
                    bank = banks.take(pe, "mod_columns")
                    for i, (c, m) in enumerate(MOD_COLUMNS):
                        last = mm(bank.ap[:, i:i + P], mod_acc[:, c, m * P:(m + 1) * P], ones, start=True, stop=True)
                    last.then_inc(bank.full, 1)
                    for i, c in enumerate(MOD_ROWS):
                        bank = banks.take(pe, "mod_row", i)
                        mm(bank.ap[:, :], ones, mod_acc[:, c, :], start=True, stop=True).then_inc(bank.full, 1)
                pe.wait_ge(sem("p_landed"), 16 * (l + 1))
                bank = banks.take(pe, "pT", l)
                transposes([(bank.ap[:, k * S + t * P:k * S + (t + 1) * P], p_tok[:, t, k * P:(k + 1) * P])
                            for k in range(2) for t in range(NT)], bank)
                banks.wait_read(pe, "pT", l)
                w = blocks(weights(pe, "ple", l)[:, 0:2 * D], 2)
                for n in range(2):
                    bank = to_tokens(("ple", l, n), w[:, :, n * 512:(n + 1) * 512], pT, 2, 512)
                read_by(bank, "ple", l)
                for n in range(2):
                    for t in range(NT):
                        banks.wait_read(pe, "down", l, n, t)
                norm_turn(("x_gate", l), 0, x3)
                turned(("x_gate", l))
                token_units(("gate", l), 2, hT3)

            def attend(tag, items_q, items_k, value, landed_sem, probs, probsT):
                n = 2 * HEADS
                for i in range(n + LAG):
                    if i < n:
                        h, t = i // 2, i % 2
                        bank = banks.take(pe, tag, "s", i)
                        mm(bank.ap[:, 0:(t + 1) * P], items_q(h)[:, t * P:(t + 1) * P], items_k(h)[:, 0:(t + 1) * P],
                           start=True, stop=True).then_inc(bank.full, 1)
                    if i >= LAG:
                        i2 = i - LAG
                        h, t = i2 // 2, i2 % 2
                        bank = banks.take(pe, tag, "pT", i2)
                        pe.wait_ge(sem(landed_sem), i2 + 1)
                        transposes([(bank.ap[:, k * P:(k + 1) * P], probs[:, i2 % 8, k * P:(k + 1) * P])
                                    for k in range(t + 1)], bank)
                        if t == 1 and h >= 1:
                            out_of(tag, h - 1, value, probsT)
                out_of(tag, HEADS - 1, value, probsT)

            open_bank = {}

            def out_of(tag, h, value, probsT):
                if h % 2 == 0:
                    open_bank[tag] = banks.take(pe, tag, "o", h // 2)
                bank = open_bank[tag]
                for t in range(NT):
                    banks.wait_read(pe, tag, "pT", 2 * h + t)
                    for k in range(t + 1):
                        last = mm(bank.ap[:, (h % 2) * S + t * P:(h % 2) * S + (t + 1) * P], value(h, k),
                                  probsT[:, (2 * h + t) % 4, k, :], start=(k == 0), stop=(k == t))
                if h % 2:
                    last.then_inc(bank.full, 1)
                else:
                    last.then_inc(sem(tag + "_even_read"), 1)

            feed_forward(0)
            norm_turn("h_att", 3)
            turned("h_att")
            token_units(("qkv",), 6, hT3)
            pe.wait_ge(sem("rotated"), 2)
            for tag, src in (("qT", q_tok), ("kT", k_tok)):
                for c in range(4):
                    bank = banks.take(pe, tag, c)
                    transposes([(bank.ap[:, i * S + t * P:i * S + (t + 1) * P], src[:, t, (2 * c + i) * P:(2 * c + i + 1) * P])
                                for i in range(2) for t in range(NT)], bank)
            for tag in ("qT", "kT"):
                for c in range(4):
                    banks.wait_read(pe, tag, c)
            attend("att", lambda h: qT[:, h, :], lambda h: kT[:, h, :],
                   lambda h, k: v_att[:, k, h * P:(h + 1) * P], "att_prob", prob, probT)
            for c in range(4):
                banks.wait_read(pe, "att", "o", c)
            token_units(("w_o",), 2, hT3)
            feed_forward(1)

            norm_turn("h_in2", 5)
            turned("h_in2")
            w = blocks(weights(pe, "in2", 0), KC)
            read_by(to_features(("av",), w, hT3, KC, four), "in2", 0)
            w = blocks(weights(pe, "in2", 1)[:, 0:KC * 384], KC)
            read_by(to_tokens(("cq",), w, hT3, KC, 384), "in2", 1)
            w = blocks(weights(pe, "in2", 2), KC)
            read_by(to_features(("qi",), w, hT3, KC, four), "in2", 2)
            w = weights(pe, "in2", 3)
            to_features(("ki",), blocks(w[:, 0:KC * P], KC), hT3, KC, [0])
            to_features(("pool",), blocks(w[:, KC * P:KC * 384], KC), hT3, KC, [0, P])
            wiw = blocks(w[:, KC * 384:KC * 392], KC)
            bank = banks.take(pe, "wi")
            for t in range(NT):
                for k in range(KC):
                    last = mm(bank.ap[:, t * 8:(t + 1) * 8], hT3[:, k, t * P:(t + 1) * P], wiw[:, k, :],
                              start=(k == 0), stop=(k == KC - 1))
            last.then_inc(bank.full, 1)
            read_by(bank, "in2", 3)
            w = weights(pe, "dsa")
            bank = banks.take(pe, "ukT")
            transposes([(bank.ap[:, j * P:(j + 1) * P], w[:, 1024 + j * P:1024 + (j + 1) * P]) for j in range(4)], bank)
            pe.wait_ge(sem("latents_normed"), 1)
            bank = banks.take(pe, "cqT")
            transposes([(bank.ap[:, k * S + t * P:k * S + (t + 1) * P], cq_tok[:, t, k * P:(k + 1) * P])
                        for k in range(2) for t in range(NT)], bank)
            bank = banks.take(pe, "ckvT")
            transposes([(bank.ap[:, t * P:(t + 1) * P], ckv_tok[:, t, :]) for t in range(NT)], bank)
            banks.wait_read(pe, "qi", 0)
            banks.wait_read(pe, "qi", 1)
            banks.wait_read(pe, "ki", 0)
            for t in range(NT):
                for g in range(4):
                    bank = banks.take(pe, "idx", t, g)
                    rows_ = slice(64 * (g // 2), 64 * (g // 2) + 64)
                    for i in range(2):
                        j = 2 * (g % 2) + i
                        last = mm(bank.ap[:, i * S:(i + 1) * S], qiT[rows_, j, t * P:(t + 1) * P], kiT[rows_, :],
                                  start=True, stop=True)
                    last.then_inc(bank.full, 1)
            banks.wait_read(pe, "cqT")
            to_features(("q2",), blocks(w[:, 0:1024], 2), cqT, 2, four)
            banks.wait_read(pe, "ukT")
            banks.wait_read(pe, "q2", 0)
            banks.wait_read(pe, "q2", 1)
            for g in range(4):
                bank = banks.take(pe, "qabs", g)
                rows_ = slice(64 * (g // 2), 64 * (g // 2) + 64)
                for i in range(2):
                    j = 2 * (g % 2) + i
                    last = mm(bank.ap[:, i * S:(i + 1) * S], w_ukT[rows_, j, :], q2T[rows_, j, :], start=True, stop=True)
                last.then_inc(bank.full, 1)
            pe.wait_ge(sem("conv_done"), 1)
            bank = banks.take(pe, "cmean")
            for c in range(2):
                last = mm(bank.ap[:, 0:S], ones, conv_acc[:, c, :], start=(c == 0), stop=(c == 1))
            last.then_inc(bank.full, 1)
            pe.wait_ge(sem("conv_centred"), 1)
            bank = banks.take(pe, "cvar")
            for c in range(2):
                last = mm(bank.ap[:, 0:S], ones, conv_sq[:, c, :], start=(c == 0), stop=(c == 1))
            last.then_inc(bank.full, 1)
            pe.wait_ge(sem("pool_ready"), 1)
            for g in range(2):
                rows_ = slice(64 * g, 64 * g + 64)
                bank = banks.take(pe, "poolo", g)
                for c in range(2):
                    last = mm(bank.ap[rows_, c * S:(c + 1) * S], w[rows_, 2048 + c * 64:2048 + (c + 1) * 64],
                              pool_d[rows_, c, :], start=True, stop=True)
                last.then_inc(bank.full, 1)
            for g in range(4):
                banks.wait_read(pe, "qabs", g)
            banks.wait_read(pe, "ckvT")
            attend("dsa", lambda h: q_abs[:, h, :], lambda h: ckvT, lambda h, k: ckv_tok[:, k, :],
                   "dsa_prob", prob2, probT2)
            for c in range(4):
                banks.wait_read(pe, "dsa", "o", c)
            for g in range(2):
                rows_ = slice(64 * g, 64 * g + 64)
                for c in range(2):
                    bank = banks.take(pe, "yatt", g, c)
                    for i in range(2):
                        h = 2 * (2 * c + i) + g
                        last = mm(bank.ap[rows_, i * S:(i + 1) * S], w[:, 1536 + h * 64:1536 + (h + 1) * 64],
                                  ctxT[:, h, :], start=True, stop=True)
                    last.then_inc(bank.full, 1)
            read_by(bank, "dsa")
            pe.wait_ge(sem("conv_out"), 2)
            for g in range(2):
                banks.wait_read(pe, "poolo", g)
                for c in range(2):
                    banks.wait_read(pe, "yatt", g, c)
            token_units(("w_out2",), 2, hT3)

            norm_turn("h_moe", 6)
            turned("h_moe")
            pe.wait_ge(sem("router_landed"), 32)
            bank = banks.take(pe, "router")
            rw = blocks(router[:, :], KC)
            for t in range(NT):
                for k in range(KC):
                    last = mm(bank.ap[:, t * 36:(t + 1) * 36], hT3[:, k, t * P:(t + 1) * P], rw[:, k, :],
                              start=(k == 0), stop=(k == KC - 1))
            last.then_inc(bank.full, 1)
            pe.wait_ge(sem("chosen_ready"), 1)
            bank = banks.take(pe, "rank")
            strict = c_("strict")
            for t in range(NT):
                last = mm(bank.ap[:, t * N_EXP:(t + 1) * N_EXP], strict, chosen[:, t, :], start=True, stop=(t == 0))
            mm(bank.ap[:, N_EXP:2 * N_EXP], ones, chosen[:, 0, :], start=False, stop=True)
            for t in range(NT):
                last = mm(bank.ap[:, 2 * N_EXP:3 * N_EXP], ones, chosen[:, t, :], start=(t == 0), stop=(t == 1))
            last.then_inc(bank.full, 1)
            for b in range(8):
                pe.wait_ge(banks.freed[b], (banks.n - 1 - b) // 8 + 1)
            y_bank = [[bank_aps[2 * t + n] for n in range(2)] for t in range(NT)]
            for t in range(NT):
                for n in range(2):
                    last = mm(y_bank[t][n], zeros, const[:, 0:512], start=True, stop=False, skip_group_check=True)
            last.then_inc(sem("moe_down"), 1)
            pe.wait_ge(sem("most_ready"), 1)
            crowded = pe.value_load(most_int[0:1, 0:1], min_val=0, max_val=S)
            with pe.If(crowded > SLOTS_OF):
                dense_pe(pe, y_bank)
            with pe.Else():
                sparse_pe(pe, y_bank)
            for t in range(NT):
                for n in range(2):
                    last = mm(y_bank[t][n], zeros, const[:, 0:512], start=False, stop=True, skip_group_check=True)
            last.then_inc(sem("moe_sum"), 1)

        @block.vector
        def _(dve):
            v = nc.vector
            flag = iter([flags[:, i:i + 1] for i in range(24)])
            step = Chain(dve, sem("dve_step"))

            def evacuate(dst, *name):
                bank = banks.read(dve, *name)
                v.tensor_copy(dst, bank.ap).then_inc(bank.freed, 1)

            def norm(k):
                dve.wait_ge(sem("rms_root"), k)
                step(v.reciprocal(rstd, rstd))
                for t in range(NT):
                    v.tensor_scalar(xn3[:, t, :], x3[:, t, :], rstd[:, t:t + 1], None, ALU.mult)\
                        .then_inc(sem("normed"), 1)

            def add_to_x(tag, *key):
                for n in range(2):
                    for t in range(NT):
                        bank = banks.read(dve, tag, *key, n, t)
                        part = x3[:, t, n * 512:(n + 1) * 512]
                        v.tensor_tensor(part, part, bank.ap, ALU.add).then_inc(bank.freed, 1)

            v.memset(vec_rows, 0.0).then_inc(sem("vec_zero"), 1)
            v.memset(raw[:, :, 0:1], 0.0).then_inc(sem("dve_step"), 1)
            step.n += 1
            step(v.memset(st, 0.0))
            bank = banks.read(dve, "vec", 0)
            v.tensor_copy(vec[:, 0:P], bank.ap[:, 0:P]).then_inc(bank.freed, 1)
            norm(1)
            banks.wait_read(dve, "vec", 0)
            l3 = v1("hgrn_lb", 0, 12)
            step(v.tensor_tensor(lb, l3[:, 0:4], l3[:, 4:8], ALU.max))
            step(v.tensor_tensor(lb, lb, l3[:, 8:12], ALU.max))
            v.tensor_tensor(blocks(lb_d, 3), blocks(l3, 3), mid(lb, 3), ALU.subtract).then_inc(sem("lb_shifted"), 1)
            dve.wait_ge(sem("lb_exp"), 1)
            step(v.tensor_tensor(lb, lb_e[:, 0:4], lb_e[:, 4:8], ALU.add))
            step(v.tensor_tensor(lb, lb, lb_e[:, 8:12], ALU.add))
            step(v.reciprocal(lb, lb))
            step(v.tensor_tensor(lb, lb, lb_e[:, 0:4], ALU.mult))
            step(v.tensor_scalar(lb_c, lb, -1.0, 1.0, ALU.mult, ALU.add))
            bank = banks.read(dve, "vec", 1)
            v.tensor_copy(vec[:, P:2 * P], bank.ap[:, 0:P]).then_inc(bank.freed, 1)
            for c in range(4, 8):
                for i in range(2 if c < 7 else 1):
                    b = 4 * (c - 4) + 2 * i
                    bank = banks.read(dve, "in", c, i)
                    v.tensor_copy(raw[:, b:b + 2, 1:S + 1], blocks(bank.ap, 2)).then_inc(bank.freed, 1)
            for c in range(4, 8):
                for i in range(2 if c < 7 else 1):
                    banks.wait_read(dve, "in", c, i)

            def shift_mix(dst, b0, n):
                step(v.tensor_tensor(dst, raw[:, b0:b0 + n, 0:S], raw[:, b0:b0 + n, 1:S + 1], ALU.subtract))
                for i in range(n):
                    last = v.scalar_tensor_tensor(dst[:, i, :], dst[:, i, :], v1("rwkv_mu", b0 + i),
                                                  raw[:, b0 + i, 1:S + 1], ALU.mult, ALU.add)
                    last.then_inc(sem("dve_step"), 1)
                    step.n += 1
                dve.wait_ge(sem("dve_step"), step.n)

            shift_mix(low, 12, 2)
            v.memset(next(flag), 0.0).then_inc(sem("low_mixed"), 1)

            for i in range(2):
                banks.wait_read(dve, "in", 0, i)
                banks.wait_read(dve, "in", 1, i)
            for j in range(4):
                step(v.tensor_scalar(hf[:, j, :], hf[:, j, :], lb_c[:, j:j + 1], lb[:, j:j + 1], ALU.mult, ALU.add))
            v.tensor_scalar(hk, hf, -1.0, 1.0, ALU.mult, ALU.add).then_inc(sem("hgrn_scaled"), 1)

            def take_scores(m):
                for t in range(NT):
                    bank = banks.read(dve, "hs", m, t)
                    mask = mid(level_mask(m) if m else ident, HG_HEADS).bitcast(I32)
                    v.copy_predicated(st[:, t], mask, blocks(bank.ap, HG_HEADS)).then_inc(bank.freed, 1)

            take_scores(0)
            v.tensor_tensor(hq, hq, hf, ALU.mult).then_inc(sem("hgrn_scaled"), 1)
            take_scores(1)
            ends = page(15)
            for i, m in enumerate(LEVELS):
                n = 4 * S // (2 * m)
                e2 = ends[:, 0:2 * n].rearrange("p (b a) -> p b a", a=2)
                q4 = page(13).rearrange("p (b a s) -> p b a s", a=2, s=m)
                k4 = page(14).rearrange("p (b a s) -> p b a s", a=2, s=m)
                dve.wait_ge(sem("hgrn_scaled"), i + 2)
                step(v.tensor_tensor(q4[:, :, 1, :], q4[:, :, 1, :], tail(e2[:, :, 0], m), ALU.mult))
                if m < LEVELS[-1]:
                    step(v.tensor_tensor(h_end[i % 2][:, 0:n], e2[:, :, 0], e2[:, :, 1], ALU.mult))
                v.tensor_tensor(k4[:, :, 0, :], k4[:, :, 0, :], tail(e2[:, :, 1], m), ALU.mult)\
                    .then_inc(sem("hgrn_scaled"), 1)
                ends = h_end[i % 2]
                if m < LEVELS[-1]:
                    take_scores(2 * m)
            bank = banks.read(dve, "hs", P)
            v.tensor_copy(sx, blocks(bank.ap, HG_HEADS)).then_inc(bank.freed, 1)
            for t in range(NT):
                evacuate(o_a[:, t, :], "ho", t)
            for t in range(NT):
                banks.wait_read(dve, "ho", t)
            o8 = blocks(page(21), 8)
            step(v.tensor_tensor(page(23), page(21), page(21), ALU.mult))
            step(v.tensor_reduce(hg_ss, blocks(page(23), 8), AX.X, ALU.add))
            v.tensor_scalar(hg_ss, hg_ss, 1.0 / P, EPS, ALU.mult, ALU.add).then_inc(sem("hgrn_sq"), 1)
            dve.wait_ge(sem("hgrn_root"), 1)
            step(v.reciprocal(hg_ss, hg_ss))
            v.tensor_tensor(o8, o8, tail(hg_ss, P), ALU.mult).then_inc(sem("hgrn_normed"), 1)
            for c in range(2):
                bank = banks.read(dve, "ha", c)
                for i in range(2):
                    h = 2 * c + i
                    last = v.scalar_tensor_tensor(hT3[:, h, :], bank.ap[:, i * S:(i + 1) * S], v1("hgrn_onorm", h),
                                                  hgT[:, h, :], ALU.mult, ALU.mult)
                last.then_inc(bank.freed, 1)
            for c in range(2):
                banks.wait_read(dve, "ha", c)

            shift_mix(page(4, 2).rearrange("p (b t) -> p b t", b=8), 0, 8)
            shift_mix(v_mix, 8, 4)
            for c in range(2):
                banks.wait_read(dve, "lw", c)
                banks.wait_read(dve, "la", c)
                banks.wait_read(dve, "lg", c)
            v.tensor_scalar(logdec, logdec, DECAY_SCALE, None, ALU.mult).then_inc(sem("dve_step"), 1)
            step.n += 1
            for j in range(4):
                step(v.tensor_scalar(kk[:, j, :], k_mix[:, j, :], v1("rwkv_kk", j), None, ALU.mult))
            v.tensor_tensor(page(21), page(7), page(7), ALU.mult).then_inc(sem("kk_sq"), 1)
            for j in range(4):
                step(v.tensor_scalar(k_adj[:, j, :], a_gate[:, j, :], -1.0, v1("rwkv_ka", j), ALU.add, ALU.mult))
            step(v.scalar_tensor_tensor(page(13), page(13), 1.0, page(5), ALU.add, ALU.mult))
            for j in range(4):
                last = v.scalar_tensor_tensor(blocks(page(22), 4)[:, j, :], r_mix[:, j, :], v1("rwkv_rk", j),
                                              k_adj[:, j, :], ALU.mult, ALU.mult)
                if j < 3:
                    step(last)
            last.then_inc(sem("rk_prod"), 1)
            cum8, log8 = blocks(page(12), 8), blocks(page(6), 8)
            for i in range(8):
                step(v.tensor_tensor_scan(cum8[:, i, :], ones, log8[:, i, :], 0.0, ALU.mult, ALU.add))
            for c in range(2):
                bank = banks.read(dve, "kk", c)
                v.tensor_scalar(page(21)[:, c * 512:(c + 1) * 512], bank.ap, 1e-24, None, ALU.max).then_inc(bank.freed, 1)
            for t in range(NT):
                evacuate(v_tok[:, t, :], "vt", t)
            for c in range(2):
                bank = banks.read(dve, "bonus", c)
                v.tensor_tensor(page(18)[:, c * 512:(c + 1) * 512], bank.ap, page(8)[:, c * 512:(c + 1) * 512],
                                ALU.mult).then_inc(bank.freed, 1)
            dve.wait_ge(sem("kk_root"), 1)
            step(v.reciprocal(page(21), page(21)))
            step(v.tensor_tensor(page(7), page(7), page(21), ALU.mult))
            step(v.tensor_copy(c_mid, cum8[:, :, 63]))
            step(v.tensor_tensor(cum8, cum8, tail(c_mid, P), ALU.subtract))
            step(v.tensor_tensor(s_scale, cum8[:, 0:8:2, P - 1], c_mid[:, 1:8:2], ALU.add))
            v.tensor_tensor(page(21), page(12), page(6), ALU.subtract).then_inc(sem("cum_ready"), 1)
            step(v.tensor_tensor(page(16), page(7), page(10), ALU.mult))
            dve.wait_ge(sem("decays_exp"), 1)
            ar8 = page(14, 2).rearrange("p (i a s) -> p i a s", i=8, a=2)
            step(v.scalar_tensor_tensor(ar8[:, :, 0, :], blocks(page(7), 8), -1.0, blocks(page(21), 8), ALU.mult, ALU.mult))
            step(v.tensor_tensor(ar8[:, :, 1, :], blocks(page(4), 8), blocks(page(22), 8), ALU.mult))
            step(v.tensor_tensor(page(16), page(16), page(12), ALU.mult))
            v.tensor_tensor(page(17), page(13), page(12), ALU.mult).then_inc(sem("tilded"), 1)
            dve.wait_ge(sem("tilded"), 1)
            step(v.tensor_copy(invT, mid(ident, 16)))
            both = const[:, cols_at["strict"][0]:cols_at["upto"][1]]
            for i in range(16):
                bank = banks.read(dve, "pairs", i)
                v.tensor_tensor(ab[:, i].rearrange("p a s -> p (a s)"), bank.ap[:, 0:S], both, ALU.mult)
                v.tensor_tensor(ak[:, i].rearrange("p a s -> p (a s)"), bank.ap[:, S:2 * S], both, ALU.mult)\
                    .then_inc(bank.freed, 1)
            for i in range(8, 16):
                banks.wait_read(dve, "pairs", i)
            v.copy_predicated(invT, mid(level_mask(1), 16).bitcast(I32), ab[:, :, 0, :]).then_inc(sem("inv_first"), 1)
            dve.wait_ge(sem("inv_first"), 1)
            for m in LEVELS[1:]:
                for g in range(4):
                    bank = banks.read(dve, "xax", m, g)
                    v.copy_predicated(invT[:, 4 * g:4 * g + 4, :], mid(level_mask(m), 4).bitcast(I32),
                                      blocks(bank.ap, 4)).then_inc(bank.freed, 1)
            def take_halves(dst, tag, t):
                for half_ in range(2):
                    bank = banks.read(dve, tag, t, half_)
                    v.tensor_copy(dst.rearrange("p (j a v) -> p j a v", a=2, v=64)[:, :, half_, :],
                                  blocks(bank.ap[:, 0:S], 4)).then_inc(bank.freed, 1)

            dve.wait_ge(sem("scale_exp"), 1)
            for t in range(NT):
                take_halves(w_sb, "w", t)
                evacuate(sa_sb, "sa", t)
                if t == 0:
                    bank = banks.read(dve, "state")
                    b4 = blocks(bank.ap, 4)
                    v.tensor_tensor(s1[0:64], b4[0:64, :, 0:64], tail(s_scale[0:64, :], 64), ALU.mult)\
                        .then_inc(sem("state_ready"), 1)
                    v.tensor_tensor(s1[64:P], b4[64:P, :, 64:P], tail(s_scale[64:P, :], 64), ALU.mult)\
                        .then_inc(bank.freed, 1)
                take_halves(y_tok[:, t, :], "y", t)
            for t in range(NT):
                for half_ in range(2):
                    banks.wait_read(dve, "y", t, half_)
            y16 = blocks(page(21), 16)
            step(v.tensor_reduce(rw_mu, y16, AX.X, ALU.add))
            step(v.tensor_scalar(rw_mu, rw_mu, 1.0 / 64, None, ALU.mult))
            step(v.tensor_tensor(y16, y16, tail(rw_mu, 64), ALU.subtract))
            step(v.tensor_tensor(page(13), page(21), page(21), ALU.mult))
            step(v.tensor_reduce(rw_ss, blocks(page(13), 16), AX.X, ALU.add))
            v.tensor_scalar(rw_ss, rw_ss, 1.0 / 64, LN_EPS, ALU.mult, ALU.add).then_inc(sem("rwkv_sq"), 1)
            dve.wait_ge(sem("rwkv_root"), 1)
            step(v.reciprocal(rw_ss, rw_ss))
            v.tensor_tensor(y16, y16, tail(rw_ss, 64), ALU.mult).then_inc(sem("rwkv_normed"), 1)
            for c in range(2):
                bank = banks.read(dve, "yb", c)
                for i in range(2):
                    j = 2 * c + i
                    last = v.tensor_scalar(hT3[:, 4 + j, :], bank.ap[:, i * S:(i + 1) * S], v1("rwkv_ln_w", j),
                                           v1("rwkv_ln_b", j), ALU.mult, ALU.add)
                    if i == 0:
                        step(last)
                last.then_inc(bank.freed, 1)
                banks.wait_read(dve, "yb", c)
            out4 = hT[:, 4 * S:8 * S]
            step(v.tensor_tensor(out4, out4, page(18), ALU.add))
            v.tensor_tensor(out4, out4, page(11), ALU.mult).then_inc(sem("mixed_ready"), 1)

            for n in range(2):
                for t in range(NT):
                    bank = banks.read(dve, "w_out", n, t)
                    part = x3[:, t, n * 512:(n + 1) * 512]
                    v.tensor_tensor(part, part, bank.ap, ALU.add).then_inc(bank.freed, 1)

            def modulate(c):
                s = unit_of[("mod", c)] % SLOTS
                dve.wait_ge(landed[s], landed_value[("mod", c)])
                w = blocks(slot(("mod", c)), KC)
                dst = mod_acc[:, c, :]
                step(v.tensor_scalar(dst, w[:, 0, :], cond[:, 0:1], None, ALU.mult))
                for k in range(1, KC):
                    last = v.scalar_tensor_tensor(dst, w[:, k, :], cond[:, k:k + 1], dst, ALU.mult, ALU.add)
                    if k < KC - 1:
                        step(last)
                last.then_inc(sem("mod_used"), 1)

            dve.wait_ge(sem("cond_ready"), 1)

            def feed_forward(l):
                for n in range(2):
                    for t in range(NT):
                        banks.wait_read(dve, "w_out" if l == 0 else "w_o", n, t)
                norm(2 if l == 0 else 4)
                for c in range(8):
                    for i in range(2):
                        banks.wait_read(dve, "up", l, c, i)
                        buf = relu[:, (2 * c + i) % 4, :]
                        v.tensor_tensor(actT[:, 4 * c + 2 * i:4 * c + 2 * i + 2, :], blocks(buf, 2), blocks(buf, 2),
                                        ALU.mult).then_inc(sem("act_ready"), 1)
                    if l == 0:
                        modulate(c)
                if l == 0:
                    for c in range(8, 12):
                        modulate(c)
                add_to_x("down", l)
                if l == 0:
                    bank = banks.read(dve, "mod_columns")
                    v.tensor_tensor(modc[:, 0:16], bank.ap[:, 0:16], v2("mod_b_2", 0, 16), ALU.add)
                    v.tensor_tensor(modc[:, 24:40], bank.ap[:, 16:32], v2("mod_b_2", 24, 16), ALU.add)\
                        .then_inc(bank.freed, 1)
                    banks.wait_read(dve, "mod_columns")
                    step(v.scalar_tensor_tensor(sc1, modc[:, 8:16], 1.0, v2("norm1_g_2", 0, 8), ALU.add, ALU.mult))
                    step(v.scalar_tensor_tensor(sc2, modc[:, 32:40], 1.0, v2("norm2_g_2", 0, 8), ALU.add, ALU.mult))
                    dve.wait_ge(sem("gate_bias_landed"), 32)
                    for i in range(4):
                        bank = banks.read(dve, "mod_row", i)
                        part = (g1_row if i < 2 else g2_row)[:, (i % 2) * 512:(i % 2 + 1) * 512]
                        v.tensor_tensor(part, part, bank.ap, ALU.add).then_inc(bank.freed, 1)
                dve.wait_ge(sem("ple_root"), l + 1)
                step(v.reciprocal(ssq, ssq))
                dve.wait_ge(sem("big_row_landed"), 16 * (l + 1))
                for t in range(NT):
                    step(v.scalar_tensor_tensor(ple_raw[:, t, :], ple_raw[:, t, :], ssq[:, t:t + 1], big_row,
                                                ALU.mult, ALU.mult))
                for n in range(2):
                    for t in range(NT):
                        banks.wait_read(dve, "gate", l, n, t)
                step(v.tensor_tensor(page(21, 2), page(21, 2), page(23, 2), ALU.mult))
                v.tensor_tensor(x[:, :], x[:, :], page(21, 2), ALU.add).then_inc(sem("ple_added"), 1)
                dve.wait_ge(sem("ple_added"), l + 1)

            def head_norm(tok, gain):
                flat = tok.rearrange("p t n -> p (t n)")
                t16 = blocks(flat, 16)
                step(v.tensor_tensor(sq, flat, flat, ALU.mult))
                step(v.tensor_reduce(head_ss, blocks(sq, 16), AX.X, ALU.add))

            def head_norm2(tok, gain, k):
                flat = tok.rearrange("p t n -> p (t n)")
                t16 = blocks(flat, 16)
                head_norm(tok, gain)
                v.tensor_scalar(head_ss, head_ss, 1.0 / P, EPS, ALU.mult, ALU.add).then_inc(sem("head_sq"), 1)
                dve.wait_ge(sem("head_root"), k)
                step(v.reciprocal(head_ss, head_ss))
                step(v.tensor_tensor(t16, t16, tail(head_ss, P), ALU.mult))
                step(v.tensor_tensor(t16, t16, mid(gain, 16), ALU.mult))
                s4 = sq.rearrange("p (t h d) -> p t h d", t=NT, h=HEADS)
                f4 = flat.rearrange("p (t h d) -> p t h d", t=NT, h=HEADS)
                for t in range(NT):
                    cos = mid(c_("cos", t * 64, (t + 1) * 64), HEADS)
                    sin = mid(c_("sin", t * 64, (t + 1) * 64), HEADS)
                    lo, hi = f4[:, t, :, 0:64], f4[:, t, :, 64:P]
                    step(v.tensor_tensor(s4[:, t, :, 0:64], lo, sin, ALU.mult))
                    step(v.tensor_tensor(s4[:, t, :, 64:P], hi, sin, ALU.mult))
                    step(v.tensor_tensor(lo, lo, cos, ALU.mult))
                    step(v.tensor_tensor(hi, hi, cos, ALU.mult))
                    step(v.tensor_tensor(lo, lo, s4[:, t, :, 64:P], ALU.subtract))
                    last = v.tensor_tensor(hi, hi, s4[:, t, :, 0:64], ALU.add)
                    if t < NT - 1:
                        step(last)
                last.then_inc(sem("rotated"), 1)
                dve.wait_ge(sem("rotated"), k)

            def attend(tag, scale, mask, probs, extra=None):
                n = 2 * HEADS
                for i in range(n + 2):
                    if i < n:
                        t = i % 2
                        bank = banks.read(dve, tag, "s", i)
                        if i >= 8:
                            banks.read(dve, tag, "pT", i - 8)
                        part = probs[:, i % 8, 0:(t + 1) * P]
                        v.scalar_tensor_tensor(part, bank.ap[:, 0:(t + 1) * P], scale, mask(t), ALU.mult, ALU.add)\
                            .then_inc(bank.freed, 1)
                        banks.wait_read(dve, tag, "s", i)
                        v.tensor_reduce(nmax[:, i:i + 1], part, AX.X, ALU.max, negate=True).then_inc(sem(tag + "_max"), 1)
                    if i >= 2:
                        i2 = i - 2
                        t = i2 % 2
                        dve.wait_ge(sem(tag + "_exp"), i2 + 1)
                        step(v.reciprocal(rinv[:, i2:i2 + 1], rsum[:, i2:i2 + 1]))
                        part = probs[:, i2 % 8, 0:(t + 1) * P]
                        v.tensor_scalar(part, part, rinv[:, i2:i2 + 1], None, ALU.mult).then_inc(sem(tag + "_prob"), 1)

            feed_forward(0)
            norm(3)
            dve.wait_ge(sem("rows_landed"), 16 * len(ROWS))
            for c in range(2):
                for t in range(NT):
                    banks.wait_read(dve, "qkv", c, t)
            head_norm2(q_tok, row("q_norm"), 1)
            for c in range(2, 4):
                for t in range(NT):
                    banks.wait_read(dve, "qkv", c, t)
            head_norm2(k_tok, row("k_norm"), 2)
            causal = c_("causal")
            attend("att", float(P) ** -0.5, lambda t: causal[:, (1 - t) * P:S], prob)
            for n in range(2):
                for t in range(NT):
                    bank = banks.read(dve, "w_o", n, t)
                    part = x3[:, t, n * 512:(n + 1) * 512]
                    v.tensor_tensor(part, part, bank.ap, ALU.add).then_inc(bank.freed, 1)
            feed_forward(1)

            norm(5)
            v.memset(arena[:, 0:2 * (S + TAPS - 1)], 0.0).then_inc(sem("dve_step"), 1)
            step.n += 1
            for i in range(3):
                v.memset(arena[:, (9 + i) * 1024:(9 + i) * 1024 + 2 * (S + 16)], 0.0).then_inc(sem("dve_step"), 1)
                step.n += 1
            dve.wait_ge(sem("dve_step"), step.n)
            v.memset(next(flag), 0.0).then_inc(sem("pool_zero"), 1)
            banks.wait_read(dve, "av", 1)
            bank = banks.read(dve, "av", 0)
            v.tensor_tensor(u_pad[:, :, TAPS - 1:], blocks(bank.ap, 2), sig_gate, ALU.mult).then_inc(bank.freed, 1)
            banks.wait_read(dve, "av", 0)
            for k in range(TAPS):
                for c in range(2):
                    src = u_pad[:, c, k:k + S]
                    if k == 0:
                        last = v.tensor_scalar(conv_acc[:, c, :], src, conv_col[:, c, 0:1], v2("conv_b_2", c),
                                               ALU.mult, ALU.add)
                    else:
                        last = v.scalar_tensor_tensor(conv_acc[:, c, :], src, conv_col[:, c, k:k + 1],
                                                      conv_acc[:, c, :], ALU.mult, ALU.add)
                    last.then_inc(sem("dve_step"), 1)
                    step.n += 1
                dve.wait_ge(sem("dve_step"), step.n)
            v.memset(next(flag), 0.0).then_inc(sem("conv_done"), 1)
            for t in range(NT):
                bank = banks.read(dve, "cq", t)
                v.tensor_copy(cq_tok[:, t, :], bank.ap[:, 0:384]).then_inc(bank.freed, 1)
                banks.wait_read(dve, "cq", t)
                step(v.tensor_tensor(cq_sq, cq_tok[:, t, :], cq_tok[:, t, :], ALU.mult))
                step(v.tensor_reduce(cs[:, 2 * t:2 * t + 1], cq_sq[:, 0:256], AX.X, ALU.add))
                step(v.tensor_reduce(cs[:, 2 * t + 1:2 * t + 2], cq_sq[:, 256:384], AX.X, ALU.add))
                step(v.tensor_scalar(cs[:, 2 * t:2 * t + 1], cs[:, 2 * t:2 * t + 1], 1.0 / 256, EPS, ALU.mult, ALU.add))
                step(v.tensor_scalar(cs[:, 2 * t + 1:2 * t + 2], cs[:, 2 * t + 1:2 * t + 2], 1.0 / P, EPS, ALU.mult,
                                     ALU.add))
            v.memset(next(flag), 0.0).then_inc(sem("latent_sq"), 1)
            dve.wait_ge(sem("latent_root"), 1)
            step(v.reciprocal(cs, cs))
            for t in range(NT):
                step(v.tensor_scalar(cq_tok[:, t, 0:256], cq_tok[:, t, 0:256], cs[:, 2 * t:2 * t + 1], None, ALU.mult))
                step(v.scalar_tensor_tensor(ckv_tok[:, t, :], cq_tok[:, t, 256:384], cs[:, 2 * t + 1:2 * t + 2],
                                            row("kv_norm_g_2"), ALU.mult, ALU.mult))
            v.memset(next(flag), 0.0).then_inc(sem("latents_normed"), 1)
            banks.wait_read(dve, "wi")
            for t in range(NT):
                for g in range(4):
                    banks.wait_read(dve, "idx", t, g)
                    for i in range(2):
                        h = 2 * (2 * (g % 2) + i) + g // 2
                        buf = rel[:, (4 * t + g) % 4 * 2 + i, :]
                        if g == 0 and i == 0:
                            last = v.tensor_scalar(score[:, t, :], buf, wi[:, t, h:h + 1], None, ALU.mult)
                        else:
                            last = v.scalar_tensor_tensor(score[:, t, :], buf, wi[:, t, h:h + 1], score[:, t, :],
                                                          ALU.mult, ALU.add)
                        if i == 0:
                            step(last)
                    last.then_inc(sem("rel_used"), 1)
                    dve.wait_ge(sem("rel_used"), 4 * t + g + 1)
            for t in range(NT):
                step(v.scalar_tensor_tensor(work[:, t, :], score[:, t, :], float(512) ** -0.5,
                                            c_("allowed", t * S, (t + 1) * S), ALU.mult, ALU.add))
                for r in range(8):
                    step(v.max(top8, work[:, t, :]))
                    step(v.match_replace(work[:, t, :], top8, work[:, t, :], -3e38))
                step(v.tensor_scalar(bias2[:, t, :], work[:, t, :], -2e38, NEG, ALU.is_gt, ALU.mult))
            bank = banks.read(dve, "cmean")
            v.tensor_scalar(conv_m[:, 0, :], bank.ap[:, 0:S], 1.0 / 256, None, ALU.mult).then_inc(bank.freed, 1)
            banks.wait_read(dve, "cmean")
            step(v.tensor_tensor(conv_acc, conv_acc, mid(conv_m[:, 0, :], 2), ALU.subtract))
            v.tensor_tensor(conv_sq, conv_acc, conv_acc, ALU.mult).then_inc(sem("conv_centred"), 1)
            banks.wait_read(dve, "pool", 0)
            u = pool_s[0]
            src, spare = pool_s[0], [pool_s[1], pool_s[2]]
            inv_n = blocks(c_("pool_inv"), 2)
            for n, w_ in enumerate((1, 2, 4, 8)):
                dst = spare[n % 2]
                step(v.tensor_tensor(dst[:, :, 16:], src[:, :, 16:], src[:, :, 16 - w_:16 - w_ + S], ALU.add))
                c, g = n // 2, slice(64 * (n % 2), 64 * (n % 2) + 64)
                step(v.tensor_tensor(pool_d[g, c, :], dst[g, c, 16:], inv_n[g, c, :], ALU.mult))
                src = dst
            v.tensor_tensor(pool_d, pool_d, u[:, :, 16:], ALU.subtract).then_inc(sem("pool_ready"), 1)
            bank = banks.read(dve, "cvar")
            v.tensor_scalar(conv_m[:, 0, :], bank.ap[:, 0:S], 1.0 / 256, EPS, ALU.mult, ALU.add).then_inc(bank.freed, 1)
            dve.wait_ge(sem("conv_root"), 1)
            step(v.reciprocal(conv_m[:, 0, :], conv_m[:, 0, :]))
            v.tensor_tensor(conv_acc, conv_acc, mid(conv_m[:, 0, :], 2), ALU.mult).then_inc(sem("conv_normed"), 1)
            for g in range(2):
                rows_ = slice(64 * g, 64 * g + 64)
                bank = banks.read(dve, "poolo", g)
                for c in range(2):
                    last = v.tensor_scalar(yT[rows_, 6 + c, :], bank.ap[rows_, c * S:(c + 1) * S],
                                           v2("pool_scale_2", c)[rows_, :], None, ALU.mult)
                last.then_inc(bank.freed, 1)
            attend("dsa", 64.0 ** -0.5, lambda t: bias2[:, t, 0:(t + 1) * P], prob2)
            for n in range(2):
                for t in range(NT):
                    bank = banks.read(dve, "w_out2", n, t)
                    part = x3[:, t, n * 512:(n + 1) * 512]
                    v.tensor_tensor(scaled, bank.ap, g1_row[:, n * 512:(n + 1) * 512], ALU.mult)\
                        .then_inc(bank.freed, 1)
                    banks.wait_read(dve, "w_out2", n, t)
                    step(v.tensor_tensor(part, part, scaled, ALU.add))
            v.memset(next(flag), 0.0).then_inc(sem("mix2_added"), 1)

            norm(6)
            step(v.memset(gates[:, :, N_EXP:], 0.0))
            step(v.memset(rank[:, :, N_EXP:], -1.0))
            bank = banks.read(dve, "router")
            bias_row = rows[:, rows_at["router_g_b_2"][0]:rows_at["router_e_b_2"][1]]
            v.tensor_tensor(lg, bank.ap[:, 0:72].rearrange("p (t n) -> p t n", t=NT), mid(bias_row, NT), ALU.add)\
                .then_inc(bank.freed, 1)
            banks.wait_read(dve, "router")
            first = c_("first")

            def one_hot(dst, logits, best, spare_):
                n = logits.shape[1]
                step(v.tensor_reduce(best, logits, AX.X, ALU.max))
                step(v.scalar_tensor_tensor(dst, logits, best, first[:, 0:n], ALU.is_equal, ALU.mult))
                step(v.tensor_reduce(spare_, dst, AX.X, ALU.max))
                step(v.tensor_scalar(dst, dst, spare_, None, ALU.is_equal))

            for t in range(NT):
                r = rt[t]
                group, e_sel, h1, h2 = r[:, 0:4], r[:, 4:12], r[:, 12:20], r[:, 20:28]
                g_max, g_sum, e1, e2, tmp, diff, expd = (r[:, 28 + i:29 + i] for i in range(7))
                shifted, hit = r[:, 36:40], r[:, 40:48]
                one_hot(group, lg[:, t, 0:4], g_max, tmp)
                v.tensor_scalar(shifted, lg[:, t, 0:4], g_max, None, ALU.subtract).then_inc(sem("group_shifted"), 1)
                step(v.tensor_scalar(e_sel, lg[:, t, 4:12], group[:, 0:1], None, ALU.mult))
                for g in range(1, 4):
                    step(v.scalar_tensor_tensor(e_sel, lg[:, t, 4 + 8 * g:12 + 8 * g], group[:, g:g + 1], e_sel,
                                                ALU.mult, ALU.add))
                one_hot(h1, e_sel, e1, tmp)
                step(v.scalar_tensor_tensor(e_sel, h1, NEG, e_sel, ALU.mult, ALU.add))
                one_hot(h2, e_sel, e2, tmp)
                v.tensor_tensor(diff, e2, e1, ALU.subtract).then_inc(sem("expert_diff"), 1)
                dve.wait_ge(sem("route_exp"), 2 * (t + 1))
                step(v.tensor_reduce(g_sum, shifted, AX.X, ALU.add))
                step(v.tensor_scalar(tmp, expd, 1.0, g_sum, ALU.add, ALU.mult))
                step(v.reciprocal(tmp, tmp))
                step(v.tensor_tensor(hit, h1, h2, ALU.add))
                step(v.scalar_tensor_tensor(h1, h2, expd, h1, ALU.mult, ALU.add))
                step(v.tensor_scalar(h1, h1, tmp, None, ALU.mult))
                for g in range(4):
                    step(v.tensor_scalar(gates[:, t, 8 * g:8 * g + 8], h1, group[:, g:g + 1], None, ALU.mult))
                    step(v.tensor_scalar(chosen[:, t, 8 * g:8 * g + 8], hit, group[:, g:g + 1], None, ALU.mult))
            v.memset(next(flag), 0.0).then_inc(sem("chosen_ready"), 1)
            bank = banks.read(dve, "rank")
            step(v.tensor_scalar(chosen, chosen, -float(1 << 20), float(1 << 20), ALU.mult, ALU.add))
            step(v.tensor_reduce(most, bank.ap[:, 2 * N_EXP:3 * N_EXP], AX.X, ALU.max))
            v.tensor_tensor(rank[:, :, 0:N_EXP], bank.ap[:, 0:2 * N_EXP].rearrange("p (t n) -> p t n", t=NT), chosen,
                            ALU.add).then_inc(bank.freed, 1)
            banks.wait_read(dve, "rank")
            v.tensor_copy(most_int[:, :], most).then_inc(sem("most_ready"), 1)
            dve.wait_ge(sem("most_ready"), 1)
            crowded = dve.value_load(most_int[0:1, 0:1], min_val=0, max_val=S)
            with dve.If(crowded > SLOTS_OF):
                dense_dve(dve)
            with dve.Else():
                sparse_dve(dve)
            dve.wait_ge(sem("moe_sum"), 1)
            for t in range(NT):
                for n in range(2):
                    part = x3[:, t, n * 512:(n + 1) * 512]
                    step(v.tensor_tensor(scaled, bank_aps[2 * t + n], g2_row[:, n * 512:(n + 1) * 512], ALU.mult))
                    step(v.tensor_tensor(part, part, scaled, ALU.add))
            v.memset(next(flag), 0.0).then_inc(sem("moe_added"), 1)
            dve.wait_ge(sem("rms_root"), 7)
            step(v.reciprocal(rstd, rstd))
            dve.wait_ge(sem("big_row_landed"), 48)
            for t in range(NT):
                v.scalar_tensor_tensor(xn3[:, t, :], x3[:, t, :], rstd[:, t:t + 1], big_row, ALU.mult, ALU.mult)\
                    .then_inc(sem("final_ready"), 1)

        @block.scalar
        def _(act):
            s = nc.scalar
            step = Chain(act, sem("act_step"))
            eps_col, ln_col = c_("eps"), c_("ln_eps")

            def evacuate(dst, func, *name, scale=1.0, width=512, bias=None):
                bank = banks.read(act, *name)
                src = bank.ap[:, 0:width]
                if len(dst.shape) == 3:
                    src = blocks(src, dst.shape[1])
                s.activation(dst, src, func, scale=scale).then_inc(bank.freed, 1)

            def norm(k):
                for t in range(NT):
                    step(s.activation(xn3[:, t, :], x3[:, t, :], ACT.Square, accum_out=ssq2[:, t:t + 1]))
                s.activation(rstd, ssq2, ACT.Sqrt, scale=1.0 / D, bias=eps_col).then_inc(sem("rms_root"), 1)

            def take_turned(tag, scale, bias=None):
                for c in range(KC // 2):
                    bank = banks.read(act, tag, c)
                    for i in range(2):
                        k = 2 * c + i
                        kw = {} if bias is None else {"bias": bias(k)}
                        if scale is None:
                            last = s.activation(hT3[:, k, :], bank.ap[:, i * S:(i + 1) * S], ACT.Copy)
                        else:
                            last = s.activation(hT3[:, k, :], bank.ap[:, i * S:(i + 1) * S], ACT.Identity,
                                                scale=scale(k), **kw)
                    last.then_inc(bank.freed, 1)

            act.dma_start(const[:, :], a["constants"]).then_inc(sem("const_landed"), 16)
            load_vectors(act, 0, VECS1, 0)
            act.wait_ge(sem("const_landed"), 16)
            act.wait_ge(sem("x_landed"), 16)
            norm(1)
            act.wait_ge(sem("lb_shifted"), 1)
            s.activation(lb_e, lb_d, ACT.Exp).then_inc(sem("lb_exp"), 1)
            banks.wait_read(act, "vec", 0)
            take_turned("h_mix", lambda k: v1("attn_norm", k))
            for i in range(2):
                evacuate(hq[:, 2 * i:2 * i + 2, :], ACT.Silu, "in", 0, i)
            for i in range(2):
                evacuate(hf[:, 2 * i:2 * i + 2, :], ACT.Sigmoid, "in", 1, i)
            for t in range(NT):
                evacuate(hv[:, t, :], ACT.Copy, "hi", t)
            for i in range(2):
                evacuate(hgT[:, 2 * i:2 * i + 2, :], ACT.Silu, "in", 3, i)
            banks.wait_read(act, "vec", 1)
            s.activation(cond, v2("c_2", 0, 8), ACT.Silu).then_inc(sem("cond_ready"), 1)
            act.wait_ge(sem("low_mixed"), 1)
            step(s.activation(low[0:64, 0, :], low[0:64, 0, :], ACT.Tanh))
            s.activation(low[:, 1, :], low[:, 1, :], ACT.Sigmoid).then_inc(sem("low_ready"), 1)
            for tag, dst, col in (("lw", logdec, "rwkv_w0"), ("la", a_gate, "rwkv_a0")):
                for c in range(2):
                    bank = banks.read(act, tag, c)
                    for i in range(2):
                        j = 2 * c + i
                        last = s.activation(dst[:, j, :], bank.ap[:, i * S:(i + 1) * S], ACT.Sigmoid, bias=v1(col, j))
                    last.then_inc(bank.freed, 1)
            for c in range(2):
                evacuate(g_out[:, 2 * c:2 * c + 2, :], ACT.Copy, "lg", c)
            act.wait_ge(sem("hgrn_sq"), 1)
            s.activation(hg_ss, hg_ss, ACT.Sqrt).then_inc(sem("hgrn_root"), 1)
            for c in range(2):
                banks.wait_read(act, "kk", c)
            s.activation(page(21), page(21), ACT.Sqrt).then_inc(sem("kk_root"), 1)
            act.wait_ge(sem("cum_ready"), 1)
            step(s.activation(page(21), page(21), ACT.Exp))
            step(s.activation(page(22), page(12), ACT.Exp))
            s.activation(page(12), page(12), ACT.Exp, scale=-1.0).then_inc(sem("decays_exp"), 1)
            s.activation(s_scale, s_scale, ACT.Exp).then_inc(sem("scale_exp"), 1)
            for b in range(2):
                evacuate(bk_tok[:, b], ACT.Copy, "bk", b)
            for g in range(4):
                evacuate(inv[:, 4 * g:4 * g + 4, :], ACT.Copy, "x", 1, g)
            for m in LEVELS[1:]:
                for g in range(4):
                    evacuate(a_inv[:, 4 * g:4 * g + 4, :], ACT.Copy, "ax", m, g)
                if m != LEVELS[-1]:
                    for g in range(4):
                        evacuate(inv[:, 4 * g:4 * g + 4, :], ACT.Copy, "x", m, g)
            act.wait_ge(sem("rwkv_sq"), 1)
            s.activation(rw_ss, rw_ss, ACT.Sqrt).then_inc(sem("rwkv_root"), 1)

            def feed_forward(l):
                for n in range(2):
                    for t in range(NT):
                        banks.wait_read(act, "w_out" if l == 0 else "w_o", n, t)
                norm(2 if l == 0 else 4)
                take_turned(("h_mlp", l), lambda k: v1("mlp_norm", 8 * l + k))
                for c in range(8):
                    for i in range(2):
                        n = 2 * c + i
                        if n >= 4 or l:
                            act.wait_ge(sem("act_ready"), 16 * l + n - 3)
                        evacuate(relu[:, n % 4, :], ACT.Relu, "up", l, c, i)
                evacuate(pT, ACT.Copy, "pT", l)
                for n in range(2):
                    for t in range(NT):
                        evacuate(ple_raw[:, t, n * 512:(n + 1) * 512], ACT.Copy, "ple", l, n, t)
                for n in range(2):
                    for t in range(NT):
                        banks.wait_read(act, "ple", l, n, t)
                for t in range(NT):
                    step(s.activation(xn3[:, t, :], ple_raw[:, t, :], ACT.Square, accum_out=ssq2[:, t:t + 1]))
                s.activation(ssq, ssq2, ACT.Sqrt, scale=1.0 / D, bias=eps_col).then_inc(sem("ple_root"), 1)
                take_turned(("x_gate", l), None)
                for n in range(2):
                    for t in range(NT):
                        evacuate(gate_s[:, t, n * 512:(n + 1) * 512], ACT.Sigmoid, "gate", l, n, t)

            def attend(tag, probs, probsT, dst):
                n = 2 * HEADS
                for i in range(n + LAG):
                    if i < n:
                        t = i % 2
                        part = probs[:, i % 8, 0:(t + 1) * P]
                        act.wait_ge(sem(tag + "_max"), i + 1)
                        s.activation(part, part, ACT.Exp, bias=nmax[:, i:i + 1], accum_out=rsum[:, i:i + 1])\
                            .then_inc(sem(tag + "_exp"), 1)
                    if i >= LAG:
                        i2 = i - LAG
                        h, t = i2 // 2, i2 % 2
                        if i2 >= 4:
                            last_head = (i2 - 4) // 2
                            if last_head % 2:
                                banks.read(act, tag, "o", last_head // 2)
                            else:
                                act.wait_ge(sem(tag + "_even_read"), last_head // 2 + 1)
                        bank = banks.read(act, tag, "pT", i2)
                        s.activation(probsT[:, i2 % 4, 0:t + 1, :], blocks(bank.ap[:, 0:(t + 1) * P], t + 1), ACT.Copy)\
                            .then_inc(bank.freed, 1)
                        if i2 >= 5 and (i2 - 5) % 4 == 0:
                            c = (i2 - 5) // 4
                            evacuate(dst[:, 2 * c:2 * c + 2, :], ACT.Copy, tag, "o", c)
                evacuate(dst[:, 6:8, :], ACT.Copy, tag, "o", 3)

            feed_forward(0)
            act.wait_ge(sem("ple_added"), 1)
            norm(3)
            take_turned("h_att", lambda k: v1("attn_norm", 8 + k))
            for u, dst in enumerate((q_tok, q_tok, k_tok, k_tok, v_att, v_att)):
                for t in range(NT):
                    evacuate(dst[:, t, (u % 2) * 512:(u % 2 + 1) * 512], ACT.Copy, "qkv", u, t)
                if u in (2, 4):
                    k = u // 2 - 1
                    act.wait_ge(sem("head_sq"), k + 1)
                    s.activation(head_ss, head_ss, ACT.Sqrt).then_inc(sem("head_root"), 1)
            for tag, dst in (("qT", qT), ("kT", kT)):
                for c in range(4):
                    evacuate(dst[:, 2 * c:2 * c + 2, :], ACT.Copy, tag, c)
            attend("att", prob, probT, hT3)
            feed_forward(1)
            act.wait_ge(sem("ple_added"), 2)
            norm(5)
            take_turned("h_in2", lambda k: sc1[:, k:k + 1], lambda k: modc[:, k:k + 1])
            evacuate(sig_gate, ACT.Sigmoid, "av", 1)
            for i in range(2):
                evacuate(qiT[:, 2 * i:2 * i + 2, :], ACT.Copy, "qi", i)
            evacuate(kiT, ACT.Copy, "ki", 0, width=S)
            act.wait_ge(sem("pool_zero"), 1)
            bank = banks.read(act, "pool", 0)
            s.activation(pool_s[0][:, :, 16:], blocks(bank.ap, 2), ACT.Copy).then_inc(bank.freed, 1)
            evacuate(wi.rearrange("p t h -> p (t h)"), ACT.Copy, "wi", width=16)
            evacuate(w_ukT, ACT.Copy, "ukT")
            act.wait_ge(sem("latent_sq"), 1)
            s.activation(cs, cs, ACT.Sqrt).then_inc(sem("latent_root"), 1)
            bank = banks.read(act, "cqT")
            for k in range(2):
                last = s.activation(cqT[:, k, :], bank.ap[:, k * S:(k + 1) * S], ACT.Identity, scale=v2("q_norm_g_2", k))
            last.then_inc(bank.freed, 1)
            evacuate(ckvT, ACT.Copy, "ckvT", width=S)
            for t in range(NT):
                for g in range(4):
                    n = 4 * t + g
                    if n >= 4:
                        act.wait_ge(sem("rel_used"), n - 3)
                    evacuate(rel[:, (n % 4) * 2:(n % 4) * 2 + 2, :], ACT.Relu, "idx", t, g)
            for i in range(2):
                evacuate(q2T[:, 2 * i:2 * i + 2, :], ACT.Copy, "q2", i)
            for g in range(4):
                bank = banks.read(act, "qabs", g)
                h0 = 4 * (g % 2) + g // 2
                s.activation(q_abs[:, h0:h0 + 3:2, :], blocks(bank.ap, 2), ACT.Copy).then_inc(bank.freed, 1)
            banks.wait_read(act, "cvar")
            s.activation(conv_m[:, 0, :], conv_m[:, 0, :], ACT.Sqrt).then_inc(sem("conv_root"), 1)
            act.wait_ge(sem("conv_normed"), 1)
            for c in range(2):
                s.activation(yT[:, c, :], conv_acc[:, c, :], ACT.Silu, scale=v2("conv_ln_g_2", c),
                             bias=v2("conv_ln_b_2", c)).then_inc(sem("conv_out"), 1)
            attend("dsa", prob2, probT2, ctxT)
            for g in range(2):
                rows_ = slice(64 * g, 64 * g + 64)
                for c in range(2):
                    bank = banks.read(act, "yatt", g, c)
                    s.activation(yT[rows_, 2 + 2 * c:4 + 2 * c, :], blocks(bank.ap, 2)[rows_], ACT.Copy)\
                        .then_inc(bank.freed, 1)
            act.wait_ge(sem("mix2_added"), 1)
            norm(6)
            take_turned("h_moe", lambda k: sc2[:, k:k + 1], lambda k: modc[:, 24 + k:25 + k])
            for t in range(NT):
                r = rt[t]
                act.wait_ge(sem("group_shifted"), t + 1)
                s.activation(r[:, 36:40], r[:, 36:40], ACT.Exp).then_inc(sem("route_exp"), 1)
                act.wait_ge(sem("expert_diff"), t + 1)
                s.activation(r[:, 34:35], r[:, 33:34], ACT.Exp).then_inc(sem("route_exp"), 1)
            act.wait_ge(sem("most_ready"), 1)
            crowded = act.value_load(most_int[0:1, 0:1], min_val=0, max_val=S)
            with act.If(crowded > SLOTS_OF):
                dense_act(act)
            with act.Else():
                sparse_act(act)
            act.wait_ge(sem("moe_added"), 1)
            norm(7)

        @block.sync
        def _(sp):
            sp.dma_start(x3, a["x"][0].rearrange("(t p) n -> p t n", p=P)).then_inc(sem("x_landed"), 16)
            for i, (name, parts) in enumerate(units):
                if i >= SLOTS:
                    sp.wait_ge(*unit_read[units[i - SLOTS][0]])
                for dst, src in parts:
                    sp.dma_start(dst(slot(name)), src).then_inc(landed[i % SLOTS], 16)
            sources = [a["exp_w1_2"][0], a["exp_w3_2"][0], a["exp_w2_2"][0]]
            kinds = [(0, 0), (1, 0), (0, 1), (1, 1), (2, 0), (2, 1)]

            def load_pair(p2, i):
                kind, second = kinds[i]
                w = sources[kind]
                sp.dma_start(blocks(moe_slot[i], EC if kind == 2 else KC), kcn(w[p2 + second]))\
                    .then_inc(moe_landed[i], 16)

            for c in range(2):
                sp.wait_ge(*unit_read[("w_out2", c)])
            sp.wait_ge(*unit_read[("dsa",)])
            banks.wait_read(sp, "w_out2", 1, 1)
            for i in range(MOE_SLOTS):
                load_pair(0, i)
            sp.wait_ge(sem("most_ready"), 1)
            crowded = sp.value_load(most_int[0:1, 0:1], min_val=0, max_val=S)
            with sp.If(crowded > SLOTS_OF):
                for i in range(MOE_SLOTS):
                    sp.wait_ge(moe_landed[i], landed_before[i] + 16)
                banks.wait_read(sp, "rank")
                with nc.allow_non_contiguous_dma(reason="a small table, off the usual path"):
                    for t in range(NT):
                        sp.dma_start(gates_dram.rearrange("e (t p) -> t p e", p=P)[t], gates[:, t, 0:N_EXP])\
                            .then_inc(sem("gates_out"), 16)
                sp.wait_ge(sem("gates_out"), 16 * NT)
                sp.dma_start(page(0, 8), gates_dram.rearrange("e t -> (e t)").partition_broadcast(P))\
                    .then_inc(sem("gates_back"), 16)

                def load_expert(e, i):
                    sp.dma_start(blocks(ring[:, i * UNIT:(i + 1) * UNIT], KC if i < 2 else EC), kcn(sources[i][e]))\
                        .then_inc(landed[i], 16)

                for i in range(3):
                    load_expert(0, i)
                with sp.Fori(0, N_EXP - 1) as e:
                    sp.wait_ge(sem("moe_hidden"), e * EC + EC)
                    load_expert(e + 1, 0)
                    load_expert(e + 1, 1)
                    sp.wait_ge(sem("moe_down"), e + 2)
                    load_expert(e + 1, 2)
            with sp.Else():
                with sp.Fori(0, PAIRS - 1) as p2:
                    for i, (b, phase) in enumerate([(0, HIDDEN), (1, HIDDEN), (2, HIDDEN), (3, HIDDEN),
                                                    (1, DOWN), (3, DOWN)]):
                        sp.wait_ge(moe_full[b], p2 * 3 + (phase + 2 - (b == 3)))
                        load_pair(p2 * 2 + 2, i)
            sp.wait_ge(sem("final_ready"), 2)
            sp.dma_start(out[0].rearrange("(t p) n -> p t n", p=P), xn3).then_inc(sem("out_written"), 16)
            sp.wait_ge(sem("out_written"), 16)

        @block.gpsimd
        def _(pool):
            load_vectors(pool, P, VECS2, 1)
            for name, n in ROWS:
                src = a[name]
                flat = src.rearrange("a b c -> (a b c)") if len(src.shape) == 3 else src.rearrange("a b -> (a b)")
                pool.dma_start(row(name), flat.partition_broadcast(P)).then_inc(sem("rows_landed"), 16)
            pool.dma_start(blocks(router[:, :], KC)[:, :, 0:4], kcn(a["router_g_w_2"][0]))\
                .then_inc(sem("router_landed"), 16)
            pool.dma_start(blocks(router[:, :], KC)[:, :, 4:36],
                           a["router_e_w_2"][0].rearrange("(k p) g e -> p k (g e)", p=P)).then_inc(sem("router_landed"), 16)
            pool.dma_start(big_row, a["ple_norm"][0].partition_broadcast(P)).then_inc(sem("big_row_landed"), 16)
            pool.wait_ge(sem("mixed_ready"), 1)
            for i, dst in enumerate((g1_row, g2_row)):
                part = a["mod_b_2"][0, (2 + 3 * i) * D:(3 + 3 * i) * D]
                pool.dma_start(dst, part.partition_broadcast(P)).then_inc(sem("gate_bias_landed"), 16)
            for l in range(2):
                if l:
                    pool.wait_ge(sem("ple_added"), 1)
                pool.dma_start(p_tok, a["p"][l, 0].rearrange("(t p) n -> p t n", p=P)).then_inc(sem("p_landed"), 16)
                if l:
                    pool.dma_start(big_row, a["ple_norm"][1].partition_broadcast(P)).then_inc(sem("big_row_landed"), 16)
            pool.wait_ge(sem("ple_added"), 2)
            pool.dma_start(big_row, a["final_g_2"].partition_broadcast(P)).then_inc(sem("big_row_landed"), 16)


INPUTS = [
    "x", "p", "attn_norm", "mlp_norm", "w_in_ar", "w_out_ar", "hgrn_lb", "hgrn_onorm", "rwkv_mu", "rwkv_w0",
    "rwkv_w2", "rwkv_a0", "rwkv_a2", "rwkv_g2", "rwkv_kk", "rwkv_ka", "rwkv_rk", "rwkv_ln_w", "rwkv_ln_b", "w_qkv",
    "w_o_attn", "q_norm", "k_norm", "w_up", "w_down", "ple_proj", "ple_norm", "ple_gate", "c_2", "mod_w_2", "mod_b_2",
    "norm1_g_2", "w_in_2", "conv_k_2", "conv_b_2", "conv_ln_g_2", "conv_ln_b_2", "q_norm_g_2", "kv_norm_g_2",
    "w_uq_2", "w_uk_2", "w_uv_2", "pool_w_2", "pool_scale_2", "w_out_2", "norm2_g_2", "router_g_w_2",
    "router_g_b_2", "router_e_w_2", "router_e_b_2", "exp_w1_2", "exp_w3_2", "exp_w2_2", "final_g_2",
]


def kernel(**inputs):
    import concourse.bacc as bacc
    from concourse.bass_utils import run_bass_kernel_spmd

    nc = bacc.Bacc("TRN2", target_bir_lowering=False, num_devices=1)
    arrays, args = {}, {}
    for name in INPUTS:
        a = np.ascontiguousarray(inputs[name])
        arrays[f"in_{name}"] = a
        args[name] = nc.dram_tensor(f"in_{name}", a.shape, mybir.dt.from_np(a.dtype), kind="ExternalInput").ap()
    table = constants()
    arrays["constants"] = table
    args["constants"] = nc.dram_tensor("constants", table.shape, F32, kind="ExternalInput").ap()
    out = nc.dram_tensor("out", (1, S, D), F32, kind="ExternalOutput").ap()
    build(nc, args, out)
    r = run_bass_kernel_spmd(nc, [arrays], core_ids=[0])
    return r.results[0]["out"]
```

```python
from contextlib import ExitStack

import numpy as np

import concourse.bass as bass
from concourse import mybir

P = 128
ALU = mybir.AluOpType
ACT = mybir.ActivationFunctionType
F32 = mybir.dt.float32
I32 = mybir.dt.int32
PART = mybir.dt.float32r
AX = mybir.AxisListType

D = 1024
S = 256
NT = S // P
KC = D // P
D_FF = 4 * D
FC = D_FF // P
HG_HEADS = 4
RW_HEADS = 8
RW_PAIRS = RW_HEADS // 2
HEADS = 8
PLE = 256
N_EXP = 32
D_EXP = 512
EC = D_EXP // P
EPS = 1e-6
LN_EPS = 64e-5
NEG = -1e30
TAPS = 31
DECAY_SCALE = -float(np.exp(-0.5))
UNIT = 4096
HALF = UNIT // 2
SLOTS = 3
LEVELS = [1, 2, 4, 8, 16, 32, 64]
MOD_COLUMNS = [(c, m) for c in (0, 1, 2, 3, 6, 7, 8, 9) for m in range(4)]
MOD_ROWS = [4, 5, 10, 11]
SLOTS_OF = 64
PAIRS = N_EXP // 2
MOE_SLOTS = 6
LAG = 4

CONST_WIDTHS = [
    ("ident", P), ("level", P * len(LEVELS)), ("strict", P), ("upto", P), ("ones", P), ("pairs", P),
    ("cos", NT * 64), ("sin", NT * 64), ("causal", S), ("allowed", NT * S), ("pool_inv", 2 * S),
    ("first", 8), ("iota", SLOTS_OF), ("eps", 1), ("ln_eps", 1), ("zero", P),
]

VECS1 = [
    ("attn_norm", 16), ("mlp_norm", 16), ("hgrn_lb", 12), ("hgrn_onorm", 4), ("rwkv_mu", 14), ("rwkv_w0", 4),
    ("rwkv_a0", 4), ("rwkv_kk", 4), ("rwkv_ka", 4), ("rwkv_rk", 4), ("rwkv_ln_w", 4), ("rwkv_ln_b", 4),
]
VECS2 = [
    ("mod_b_2", 48), ("norm1_g_2", 8), ("norm2_g_2", 8), ("conv_b_2", 2), ("conv_ln_g_2", 2), ("conv_ln_b_2", 2),
    ("q_norm_g_2", 2), ("pool_scale_2", 2), ("c_2", 8),
]
ROWS = [("q_norm", 128), ("k_norm", 128), ("kv_norm_g_2", 128), ("router_g_b_2", 4), ("router_e_b_2", 32)]


CONV_ROW = 96


def offsets(table):
    at, out = 0, {}
    for name, width in table:
        out[name] = (at, at + width)
        at += width
    return out, at


def constants():
    at, n = offsets(CONST_WIDTHS)
    c = np.zeros((P, n), np.float32)

    def put(name, value):
        s, e = at[name]
        c[:, s:e] = value

    s_, t_ = np.arange(P)[:, None], np.arange(P)[None, :]
    put("ident", np.eye(P))
    put("level", np.concatenate(
        [(s_ // (2 * m) == t_ // (2 * m)) & (s_ // m % 2 == 0) & (t_ // m % 2 == 1) for m in LEVELS], axis=1))
    put("strict", s_ < t_)
    put("upto", s_ <= t_)
    put("ones", 1.0)
    put("pairs", s_ // 64 == t_ // 64)
    half = 64
    inv = np.power(np.float32(10000.0), -np.arange(half, dtype=np.float32) / half).astype(np.float32)
    ang = np.arange(S, dtype=np.float32)[:, None] * inv[None, :]
    put("cos", np.cos(ang).reshape(NT, P, half).transpose(1, 0, 2).reshape(P, -1))
    put("sin", np.sin(ang).reshape(NT, P, half).transpose(1, 0, 2).reshape(P, -1))
    put("causal", np.concatenate([np.zeros((P, P)), np.where(t_ <= s_, 0.0, NEG)], axis=1))
    q = np.arange(S).reshape(NT, P)
    ok = np.arange(S)[None, None, :] // 64 <= q[:, :, None] // 64
    put("allowed", np.where(ok, 0.0, NEG).transpose(1, 0, 2).reshape(P, -1))
    windows = np.array([[2, 8], [4, 16]])[(np.arange(P) // 64)]
    put("pool_inv", (1.0 / np.minimum(np.arange(1, S + 1)[None, None, :], windows[:, :, None])).reshape(P, -1))
    put("first", 8.0 - np.arange(8))
    put("iota", np.arange(SLOTS_OF))
    put("eps", EPS)
    put("ln_eps", LN_EPS)
    return c


class Bank:

    def __init__(self, ap, full, freed, use):
        self.ap, self.full, self.freed, self.use = ap, full, freed, use


class Banks:

    def __init__(self, aps, full, freed):
        self.aps, self.full, self.freed, self.n, self.uses = aps, full, freed, 0, {}

    def take(self, pe, *name):
        b = self.n % len(self.aps)
        use = self.n // len(self.aps)
        self.n += 1
        assert name not in self.uses, name
        self.uses[name] = Bank(self.aps[b], self.full[b], self.freed[b], use)
        if use:
            pe.wait_ge(self.freed[b], use)
        return self.uses[name]

    def read(self, eng, *name):
        bank = self.uses[name]
        eng.wait_ge(bank.full, bank.use + 1)
        return bank

    def wait_read(self, eng, *name):
        bank = self.uses[name]
        eng.wait_ge(bank.freed, bank.use + 1)


class Chain:

    def __init__(self, eng, sem):
        self.eng, self.sem, self.n = eng, sem, 0

    def __call__(self, ins):
        ins.then_inc(self.sem, 1)
        self.n += 1
        self.eng.wait_ge(self.sem, self.n)


def kcn(w):
    return w.rearrange("(k p) n -> p k n", p=P)


def weight_units(a):
    units = []

    def grid(lo, k, n):
        return lambda s: s[:, lo:lo + k * n].rearrange("p (k n) -> p k n", k=k)

    def whole(name, w, n, width=512):
        for c in range(n):
            units.append(((*name, c), [(grid(0, KC, width), kcn(w[:, c * width:(c + 1) * width]))]))

    whole(("w_in",), a["w_in_ar"][0], 7)
    units.append((("w_in", 7), [(grid(0, KC, 256), kcn(a["w_in_ar"][0][:, 3584:3840]))]))
    units.append((("lora",), [(lambda s: s[0:64, 0:512], a["rwkv_w2"][0]),
                              (lambda s: s[64:128, 0:512], a["rwkv_a2"][0]),
                              (lambda s: s[:, 512:1024], a["rwkv_g2"][0])]))
    whole(("w_out",), a["w_out_ar"][0], 2)
    mods = [(("mod", c), [(grid(0, KC, 512), kcn(a["mod_w_2"][0][:, c * 512:(c + 1) * 512]))]) for c in range(12)]

    def mlp(l):
        for c in range(8):
            units.append((("up", l, c), [(grid(0, KC, 512), kcn(a["w_up"][l][:, c * 512:(c + 1) * 512]))]))
            if l == 0 and c % 2:
                units.append(mods[c // 2])
        for n in range(2):
            for k in range(4):
                part = kcn(a["w_down"][l][k * D:(k + 1) * D, n * 512:(n + 1) * 512])
                units.append((("down", l, n, k), [(grid(0, KC, 512), part)]))
                if l == 0:
                    units.append(mods[4 + 4 * n + k])
        units.append((("ple", l), [(grid(0, 2, D), kcn(a["ple_proj"][l]))]))
        whole(("gate", l), a["ple_gate"][l], 2)

    mlp(0)
    whole(("qkv",), a["w_qkv"][0], 6)
    whole(("w_o",), a["w_o_attn"][0], 2)
    mlp(1)
    w = kcn(a["w_in_2"][0])
    units.append((("in2", 0), [(grid(0, KC, 512), w[:, :, 0:512])]))
    units.append((("in2", 1), [(grid(0, KC, 384), w[:, :, 512:896])]))
    units.append((("in2", 2), [(grid(0, KC, 512), w[:, :, 896:1408])]))
    twice = lambda d: lambda s: s[:, 0:KC * P].rearrange("p (k d n) -> p k d n", k=KC, d=2)[:, :, d, :]
    units.append((("in2", 3), [(twice(0), w[:, :, 1408:1472]), (twice(1), w[:, :, 1408:1472]),
                               (grid(KC * P, KC, 256), w[:, :, 1480:1736]),
                               (grid(KC * 384, KC, 8), w[:, :, 1472:1480])]))
    units.append((("dsa",), [
        (grid(0, 2, 512), a["w_uq_2"][0].rearrange("(k p) h d -> p k (h d)", p=P)),
        (lambda s: s[:, 1024:1536], a["w_uk_2"][0].rearrange("p h d -> p (h d)")),
        (lambda s: s[:, 1536:2048], a["w_uv_2"][0].rearrange("p h d -> p (h d)")),
        (grid(2048, 2, 64), a["pool_w_2"][0].rearrange("(c g) i o -> (g i) c o", c=2)),
    ]))
    whole(("w_out2",), a["w_out_2"][0], 2)
    return units


def build(nc, a, out):
    ctx = ExitStack()
    with ctx:
        def sb(name, cols, dt=F32):
            return ctx.enter_context(nc.sbuf_tensor(name, [P, cols], dt))

        cols_at, n_const = offsets(CONST_WIDTHS)
        v1_at, n_v1 = offsets(VECS1)
        v2_at, n_v2 = offsets(VECS2)
        rows_at, n_rows = offsets(ROWS)

        arena_at = -(-nc.sbuf_base // 32) * 32
        arena = sb("arena", 27 * 1024)
        ring_at = -(-nc.sbuf_base // 32) * 32
        ring = sb("ring", SLOTS * UNIT)
        hT_at = -(-nc.sbuf_base // 32) * 32
        hT = sb("hT", KC * S)
        xn_at = -(-nc.sbuf_base // 32) * 32
        xn = sb("xn", NT * D)
        const = sb("const", n_const)
        rows = sb("rows", n_rows)
        vec = sb("vec", 2 * P)
        x = sb("x", NT * D)
        big_row_t = sb("big_row", D)
        small = sb("small", 896)
        router = sb("router", KC * 36)
        most_int = sb("most_int", 1, I32)
        big_row = big_row_t[:, :]
        gates_dram = nc.dram_tensor("gates_scratch", [N_EXP, S], F32, kind="Internal").ap()

        sems = {}

        def sem(name):
            if name not in sems:
                sems[name] = ctx.enter_context(nc.semaphore(name))
            return sems[name]

        banks_mem = [ctx.enter_context(nc.psum_tensor(f"bank{i}", [P, 512], F32)) for i in range(8)]
        bank_aps = [b[:, :] for b in banks_mem]
        banks = Banks(bank_aps, [sem(f"bank_full{i}") for i in range(8)], [sem(f"bank_freed{i}") for i in range(8)])

        def as_parts(name, at, cols):
            return nc.alloc_sbuf_tensor_at(name, [P, cols], PART, offset=at)[:, :]

        def c_(name, lo=0, hi=None):
            s, e = cols_at[name]
            return const[:, s + lo:(e if hi is None else s + hi)]

        ident, ones, pairs = c_("ident"), c_("ones"), c_("pairs")
        zeros = c_("zero")

        def level_mask(m):
            i = LEVELS.index(m)
            return c_("level", i * P, (i + 1) * P)

        def v1(name, i, n=1):
            s = v1_at[name][0] + i
            return vec[:, s:s + n]

        def v2(name, i, n=1):
            s = P + v2_at[name][0] + i
            return vec[:, s:s + n]

        def row(name, lo=0, hi=None):
            s, e = rows_at[name]
            return rows[:, s + lo:(e if hi is None else s + hi)]

        small_used = [0]

        def tiny(n):
            at = small_used[0]
            small_used[0] += n
            assert small_used[0] <= 896
            return small[:, at:at + n]

        def page(i, n=1):
            return arena[:, i * 1024:(i + n) * 1024]

        def half(i, n=1):
            return arena[:, i * 512:(i + n) * 512]

        def blocks(ap, j):
            return ap.rearrange("p (j t) -> p j t", j=j)

        def mid(ap, n):
            return ap.unsqueeze(1).to_broadcast([ap.shape[0], n, ap.shape[1]])

        def tail(ap, w):
            return ap.unsqueeze(2).to_broadcast([ap.shape[0], ap.shape[1], w])

        x3, xn3, hT3 = blocks(x[:, :], NT), blocks(xn[:, :], NT), blocks(hT[:, :], KC)
        vec_rows = page(26)[:, 0:2 * P]

        raw = arena[:, 0:14 * 257].rearrange("p (b t) -> p b t", b=14)
        mixed = page(4, 4)
        r_mix, k_mix, logdec, kk = (blocks(page(i), 4) for i in (4, 5, 6, 7))
        v_mix, low = blocks(page(8), 4), blocks(half(18), 2)
        a_gate, g_out, cum, k_adj = (blocks(page(i), 4) for i in (10, 11, 12, 13))
        ar = page(14, 2).rearrange("p (j t a s) -> p j t a s", j=4, t=NT, a=2)
        b_til, k_til, bonus = (blocks(page(i), 4) for i in (16, 17, 18))
        v_tok = blocks(page(19), NT)
        bk_tok = page(20).rearrange("p (b j s) -> p b j s", b=2, j=4)
        y_tok = blocks(page(21), NT)
        w_sb, sa_sb = half(44), half(45)
        ab = page(23, 4).rearrange("p (i a s) -> p i a s", i=16, a=2)
        ak = page(4, 4).rearrange("p (i a s) -> p i a s", i=16, a=2)
        inv, invT = blocks(page(0, 2), 16), blocks(page(2, 2), 16)
        a_inv = blocks(xn[:, :], 16)
        s1 = arena[:, 19 * 512:19 * 512 + 256].rearrange("p (j v) -> p j v", j=4)
        hq, hk, hf, hgT = (blocks(page(i), 4) for i in (13, 14, 15, 16))
        hv = blocks(page(17), NT)
        h_end = [page(18), page(22)]
        st = page(19).rearrange("p (t h s) -> p t h s", t=NT, h=4)
        sx = blocks(half(40), 4)
        o_a, o_sq = blocks(page(21), NT), blocks(page(23), NT)

        q_tok, k_tok, v_att = (blocks(page(i, 2), NT) for i in (0, 2, 4))
        qT, kT = blocks(page(6, 2), HEADS), blocks(page(8, 2), HEADS)
        rot, sq = page(10, 2), page(12, 2)
        prob, probT = blocks(page(14, 2), 8), page(16).rearrange("p (b k q) -> p b k q", b=4, k=2)

        actT = blocks(page(0, 8), FC)
        relu = blocks(page(8, 2), 4)
        p_tok, pT = blocks(half(40), NT), blocks(half(41), 2)
        ple_raw, gate_s = blocks(page(21, 2), NT), blocks(page(23, 2), NT)

        mod_acc = blocks(page(10, 6), 12)

        u_pad = arena[:, 0:2 * (S + TAPS - 1)].rearrange("p (c t) -> p c t", c=2)
        conv_acc, conv_sq, sig_gate = blocks(half(2), 2), blocks(half(3), 2), blocks(half(4), 2)
        conv_col = vec[:, :].rearrange("p (c r) -> p c r", c=2)[:, :, CONV_ROW:CONV_ROW + TAPS]
        conv_m = blocks(half(6), 2)
        cq_tok = page(4)[:, 0:768].rearrange("p (t n) -> p t n", t=NT)
        cqT = blocks(half(10), 2)
        ckvT, ckv_tok = page(5)[:, 512:768], blocks(page(5)[:, 768:1024], NT)
        qiT = blocks(page(6), 4)
        kiT, wi = page(7)[:, 0:256], page(7)[:, 256:272].rearrange("p (t h) -> p t h", t=NT)
        cq_sq = page(7)[:, 272:656]
        w_ukT, pool_d = blocks(half(16), 4), blocks(half(17), 2)
        pool_s = [arena[:, i * 1024:i * 1024 + 2 * (S + 16)].rearrange("p (c t) -> p c t", c=2) for i in (9, 10, 11)]
        q2T, q_abs = blocks(page(12), 4), blocks(page(13, 2), 8)
        score, work = blocks(half(30), NT), blocks(half(31), NT)
        rel = blocks(page(16, 2), 8)
        bias2 = blocks(half(36), NT)
        prob2, probT2 = blocks(page(19, 2), 8), page(21).rearrange("p (b k q) -> p b k q", b=4, k=2)
        ctxT = blocks(page(22, 2), 8)
        yT = hT3
        g1_row, g2_row = page(25), page(26)
        scaled = half(48)

        gate_all = blocks(page(0, 8), N_EXP)
        exp_act, exp_silu = blocks(page(8), EC), blocks(page(9), EC)

        gathered = page(0)
        select = [blocks(arena[:, 1024 + i * S:1024 + (i + 1) * S], NT) for i in range(2)]
        spread = [arena[:, 1024 + (2 + i) * S:1024 + (3 + i) * S] for i in range(2)]
        pair_act, pair_silu, pair_y = half(4), half(5), page(4)
        act_high, act_low = (as_parts(f"act_{n}", arena_at + (6 + i) * 2048, 512) for i, n in enumerate(("high", "low")))
        moe_slot = [ring[:, i * UNIT:(i + 1) * UNIT] for i in range(SLOTS)] + \
                   [page(13 + 4 * i, 4) for i in range(MOE_SLOTS - SLOTS)]
        low_w = [as_parts(f"low_w{i}", ring_at + i * UNIT * 4 if i < SLOTS else arena_at + (13 + 4 * (i - SLOTS)) * 4096, UNIT)
                 for i in range(MOE_SLOTS)]
        high_w = [as_parts(f"high_w{i}", arena_at + (5 + 2 * i) * 4096, HALF) for i in range(4)]
        gathered_high, gathered_low = (as_parts(f"gathered_{n}", hT_at + i * 4096, KC * P)
                                       for i, n in enumerate(("high", "low")))
        slot_gate = [tiny(1), tiny(1)]

        ssq, ssq2, rstd, rstd2, flags = tiny(NT), tiny(NT), tiny(NT), tiny(NT), tiny(24)
        lb_d, lb_e, lb, lb_c = tiny(12), tiny(12), tiny(4), tiny(4)
        hg_ss, rw_mu, rw_ss = tiny(8), tiny(16), tiny(16)
        c_mid, c_end, s_scale = tiny(8), tiny(8), tiny(4)
        head_ss = tiny(16)
        nmax, rsum, rinv = tiny(16), tiny(16), tiny(16)
        cond, modc = tiny(8), tiny(48)
        sc1, sc2 = tiny(8), tiny(8)
        cs = tiny(4)
        top8 = tiny(8)
        lg = tiny(72).rearrange("p (t n) -> p t n", t=NT)
        rt = [tiny(64) for _ in range(4)]
        gates = tiny(NT * (N_EXP + 2)).rearrange("p (t n) -> p t n", t=NT)
        rank = tiny(NT * (N_EXP + 4)).rearrange("p (t n) -> p t n", t=NT)
        chosen = tiny(NT * N_EXP).rearrange("p (t n) -> p t n", t=NT)
        most = tiny(1)

        units = weight_units(a)
        unit_of = {name: i for i, (name, _) in enumerate(units)}
        landed_value, slot_total = {}, [0] * SLOTS
        for i, (name, parts) in enumerate(units):
            slot_total[i % SLOTS] += 16 * len(parts)
            landed_value[name] = slot_total[i % SLOTS]
        landed = [sem(f"slot_landed{i}") for i in range(SLOTS)]
        unit_read = {("mod", c): (sem("mod_used"), c + 1) for c in range(12)}

        def slot(name):
            s = unit_of[name] % SLOTS
            return ring[:, s * UNIT:(s + 1) * UNIT]

        def weights(pe, *name):
            pe.wait_ge(landed[unit_of[name] % SLOTS], landed_value[name])
            return slot(name)

        def read_by(bank, *name):
            unit_read[name] = (bank.full, bank.use + 1)

        split_units = [("w_in", c) for c in range(8)] + [("up", 0, c) for c in range(8)] + [("qkv", c) for c in range(6)] + \
                      [("up", 1, c) for c in range(8)] + [("down", 1, n, kb) for n in range(2) for kb in range(3)]
        act_split = 3 * KC
        actT_high = as_parts("actT_high", arena_at, act_split * S)
        actT_low = as_parts("actT_low", arena_at + 10 * 4096, act_split * S)
        split_no = {name: i for i, name in enumerate(split_units)}
        split_buffers, split_buffers_in = (
            [as_parts(f"split_high_{tag}{i}", arena_at + p_ * 4096, HALF) for i, p_ in enumerate(pages)]
            for tag, pages in (("", (16, 18, 21, 23)), ("in", (20, 22, 24, 11))))
        turned_high, turned_low = as_parts("turned_high", xn_at, KC * S), as_parts("turned_low", hT_at, KC * S)
        half_read = {}
        split_turned_count = [0]

        def half_of(ap, name, s):
            if takes_features(name):
                n = unit_columns(name) // 2
                return blocks(ap[:, 0:2 * n * KC], KC)[:, :, s * n:(s + 1) * n]
            return blocks(ap, KC)[:, s * 4:(s + 1) * 4, :]

        def takes_features(name):
            return name[0] == "up" or (name[0] == "w_in" and name[1] != 2)

        def unit_columns(name):
            return 256 if name == ("w_in", 7) else 512

        def high_of(name, s):
            ap = (split_buffers_in if name[0] == "w_in" else split_buffers)[(2 * split_no[name] + s) % 4]
            return blocks(ap[:, 0:unit_columns(name) // 2 * KC], KC) if takes_features(name) else blocks(ap, 4)

        def low_of(name, s):
            return half_of(low_w[unit_of[name] % SLOTS], name, s)


        moe_full = [sem(f"moe_full{b}") for b in range(4)]
        moe_freed = [sem(f"moe_freed{b}") for b in range(4)]
        mb = bank_aps[4:8]
        moe_landed = landed + [sem(f"slot_landed{i}") for i in range(SLOTS, MOE_SLOTS)]
        landed_before = slot_total + [0] * (MOE_SLOTS - SLOTS)
        HIDDEN, MIDDLE, DOWN = 0, 1, 2
        UNIT_FILLS = [(0, HIDDEN), (1, HIDDEN), (2, HIDDEN), (3, HIDDEN), (1, DOWN), (3, DOWN)]

        def filled(p6, q, phase):
            return p6 + (3 * q + phase + 2)

        def half_count(p6, q, j, s):
            return p6 * 4 + (12 * q + 2 * j + s + 1)

        def dense_pe(pe, y_bank):
            mm = nc.tensor.matmul
            w = [blocks(ring[:, i * UNIT:(i + 1) * UNIT], KC if i < 2 else EC) for i in range(3)]
            with pe.Fori(0, N_EXP) as e:
                for m in range(EC):
                    if m == 0:
                        for i in range(2):
                            pe.wait_ge(landed[i], e * 16 + (slot_total[i] + 32))
                    pe.wait_ge(sem("moe_hidden_read"), e * EC + (m + 1))
                    for i in range(2):
                        for k in range(KC):
                            last = mm(bank_aps[4 + m][:, i * S:(i + 1) * S], w[i][:, k, m * P:(m + 1) * P],
                                      hT3[:, k, :], start=(k == 0), stop=(k == KC - 1), skip_group_check=True)
                    last.then_inc(sem("moe_hidden"), 1)
                pe.wait_ge(landed[2], e * 16 + (slot_total[2] + 32))
                for m in range(EC):
                    pe.wait_ge(sem("moe_act"), e * EC + (m + 1))
                    for t in range(NT):
                        for n in range(2):
                            last = mm(y_bank[t][n], exp_act[:, m, t * P:(t + 1) * P],
                                      w[2][:, m, n * 512:(n + 1) * 512], start=False, stop=False,
                                      skip_group_check=True)
                last.then_inc(sem("moe_down"), 1)

        def sparse_pe(pe, y_bank):
            mm = nc.tensor.matmul

            def gather(side, first):
                for k in range(KC):
                    dst = mb[k // 4][:, (k % 4) * P:(k % 4 + 1) * P]
                    for t in range(NT):
                        last = mm(dst, xn3[:, t, k * P:(k + 1) * P], select[side][:, t, :], start=(t == 0),
                                  stop=(t == NT - 1), skip_group_check=True)
                    if k % 4 == 3:
                        last.then_inc(moe_full[k // 4], 1)
                for t in range(NT):
                    nc.tensor.transpose(mb[2][:, t * P:(t + 1) * P], select[side][:, t, :], ident)
                for t in range(NT):
                    last = mm(mb[2][:, S:S + 2], select[side][:, t, :], gates[:, t, bass.ds(first, 2)],
                              start=(t == 0), stop=(t == NT - 1), skip_group_check=True)
                last.then_inc(moe_full[2], 1)

            def scatter(side):
                for t in range(NT):
                    for n in range(2):
                        mm(y_bank[t][n], spread[side][:, t * P:(t + 1) * P], pair_y[:, n * 512:(n + 1) * 512],
                           start=False, stop=False, skip_group_check=True)

            def half_products(p6, q, j, s, high, low, outs):
                pe.wait_ge(sem("moe_low"), half_count(p6, q, j, s))
                n_k = (EC if j > 3 else KC) // 2
                w_high, w_low = blocks(high_w[2 * (j % 2) + s], n_k), blocks(low_w[j][:, s * HALF:(s + 1) * HALF], n_k)
                for k in range(n_k):
                    kk_ = slice((s * n_k + k) * P, (s * n_k + k + 1) * P)
                    for b, n in outs:
                        cols = slice(n * 512, (n + 1) * 512)
                        first, end = s == 0 and k == 0, s == 1 and k == n_k - 1
                        mm(mb[b], high[:, kk_], w_high[:, k, cols], start=first, stop=False, skip_group_check=True)
                        mm(mb[b], low[:, kk_], w_high[:, k, cols], start=False, stop=False, skip_group_check=True)
                        last = mm(mb[b], high[:, kk_], w_low[:, k, cols], start=False, stop=end, skip_group_check=True)
                        if end:
                            last.then_inc(moe_full[b], 1)
                if s == 0:
                    last.then_inc(sem("moe_half_read"), 1)

            for signal in (moe_full[3], sem("moe_half_read"), sem("moe_half_read")):
                mm(mb[3], zeros, const[:, 0:512], start=True, stop=True, skip_group_check=True).then_inc(signal, 1)
            pe.wait_ge(sem("selected"), 1)
            gather(0, 0)
            for b in range(3):
                pe.wait_ge(moe_freed[b], 1)
            with pe.Fori(0, PAIRS // 2) as pp:
                p6 = pp * 6
                for q in range(2):
                    pe.wait_ge(sem("gathered_low"), pp * 4 + (2 * q + 2))
                    for j in range(4):
                        pe.wait_ge(moe_freed[j], filled(p6, q, HIDDEN) - 1)
                        for half_ in range(2):
                            half_products(p6, q, j, half_, gathered_high, gathered_low, [(j, 0)])
                    scatter(1 - q)
                    pe.wait_ge(moe_freed[3], filled(p6, q, MIDDLE) - 1)
                    for m in range(EC):
                        last = nc.tensor.transpose(mb[3][:, m * P:(m + 1) * P], pair_act[:, m * P:(m + 1) * P], ident)
                    last.then_inc(moe_full[3], 1)
                    pe.wait_ge(sem("selected"), pp * 2 + (q + 2))
                    for b in range(3):
                        pe.wait_ge(moe_freed[b], filled(p6, q, MIDDLE) - 1)
                    gather(1 - q, pp * 4 + (2 * q + 2))
                    pe.wait_ge(moe_freed[3], filled(p6, q, DOWN) - 1)
                    for i in range(2):
                        for b in (2 * i, 2 * i + 1):
                            pe.wait_ge(moe_freed[b], filled(p6, q, DOWN) - 1)
                        for half_ in range(2):
                            half_products(p6, q, 4 + i, half_, act_high, act_low, [(2 * i, 0), (2 * i + 1, 1)])
            for b in range(4):
                pe.wait_ge(moe_freed[b], 3 * PAIRS + 1)
            scatter(1)

        def dense_dve(dve):
            v = nc.vector
            dve.wait_ge(sem("gates_back"), 16)
            flag = iter([flags[:, 20 + i:21 + i] for i in range(EC)])
            for m in range(EC):
                v.memset(next(flag), 0.0).then_inc(sem("moe_hidden_read"), 1)
            with dve.Fori(0, N_EXP) as e:
                dve.wait_ge(sem("moe_down"), e + 1)
                for m in range(EC):
                    dve.wait_ge(sem("moe_silu"), e * EC + (m + 1))
                    v.tensor_tensor(exp_act[:, m, :], exp_silu[:, m, :], bank_aps[4 + m][:, S:2 * S], ALU.mult)\
                        .then_inc(sem("moe_hidden_read"), 1)
                    dve.wait_ge(sem("moe_hidden_read"), e * EC + (EC + m + 1))
                    v.tensor_tensor(exp_act[:, m, :], exp_act[:, m, :], gate_all[:, e, :], ALU.mult)\
                        .then_inc(sem("moe_act"), 1)

        def sparse_dve(dve):
            v = nc.vector
            iota = c_("iota")

            def choose(side, first):
                for t in range(NT):
                    for i in range(2):
                        last = v.tensor_scalar(select[side][:, t, i * SLOTS_OF:(i + 1) * SLOTS_OF], iota,
                                               rank[:, t, bass.ds(first + i, 1)], None, ALU.is_equal)
                last.then_inc(sem("selected"), 1)

            def keep_gathered(side, value):
                for b in range(2):
                    dve.wait_ge(moe_full[b], value)
                    for k in range(4 * b, 4 * b + 4):
                        last = v.tensor_scalar(gathered[:, k * P:(k + 1) * P], mb[b][:, (k % 4) * P:(k % 4 + 1) * P],
                                               sc2[:, k:k + 1], modc[:, 24 + k:25 + k], ALU.mult, ALU.add)
                    last.then_inc(moe_freed[b], 1)
                dve.wait_ge(moe_full[2], value)
                v.tensor_copy(spread[side], mb[2][:, 0:S])
                v.tensor_copy(slot_gate[side][0:64, :], mb[2][0:64, S:S + 1])
                v.tensor_copy(slot_gate[side][64:P, :], mb[2][64:P, S + 1:S + 2]).then_inc(moe_freed[2], 1)

            def gathered_lows(count):
                for b in range(2):
                    cols = slice(b * 512, (b + 1) * 512)
                    dve.wait_ge(sem("gathered_high"), count + b)
                    v.tensor_tensor(gathered_low[:, cols], gathered[:, cols], gathered_high[:, cols].bitcast(F32),
                                    ALU.subtract).then_inc(sem("gathered_low"), 1)

            def low(p6, q, j, s):
                cols = slice(s * HALF, (s + 1) * HALF)
                dve.wait_ge(sem("moe_high"), half_count(p6, q, j, s))
                v.tensor_tensor(low_w[j % 6][:, cols], moe_slot[j % 6][:, cols], high_w[2 * (j % 2) + s].bitcast(F32),
                                ALU.subtract).then_inc(sem("moe_low"), 1)

            def gate_hidden(p6, q, i):
                rows_ = slice(64 * i, 64 * i + 64)
                dve.wait_ge(moe_freed[2 * i], filled(p6, q, HIDDEN))
                dve.wait_ge(moe_full[2 * i + 1], filled(p6, q, HIDDEN))
                v.tensor_tensor(pair_act[rows_, :], pair_silu[rows_, :], mb[2 * i + 1][rows_, :], ALU.mult)\
                    .then_inc(moe_freed[2 * i + 1], 1)

            def pair_steps(pp, q, more):
                p6 = pp * 6
                for j in (1, 2):
                    for s in range(2):
                        low(p6, q, j, s)
                gate_hidden(p6, q, 0)
                for j in (3, 4):
                    for s in range(2):
                        low(p6, q, j, s)
                gate_hidden(p6, q, 1)
                for s in range(2):
                    low(p6, q, 5, s)
                dve.wait_ge(sem("act_high"), pp * 2 + (q + 1))
                v.tensor_tensor(act_low, mb[3], act_high.bitcast(F32), ALU.subtract).then_inc(moe_freed[3], 1)
                keep_gathered(1 - q, filled(p6, q, MIDDLE))
                choose(q, pp * 4 + (2 * q + 4))
                gathered_lows(pp * 4 + (2 * q + 3))
                if more:
                    for s in range(2):
                        low(p6, q, 6, s)
                for n in range(2):
                    dve.wait_ge(moe_full[2 + n], filled(p6, q, DOWN))
                    v.tensor_scalar(pair_y[64:P, n * 512:(n + 1) * 512], mb[2 + n][64:P, :],
                                    slot_gate[q][64:P, :], None, ALU.mult).then_inc(moe_freed[2 + n], 1)

            v.memset(pair_y, 0.0).then_inc(sem("dve_moe"), 1)
            v.memset(spread[1], 0.0).then_inc(sem("dve_moe"), 1)
            v.memset(flags[:, 20:21], 0.0).then_inc(moe_freed[3], 1)
            choose(0, 0)
            keep_gathered(0, 1)
            choose(1, 2)
            gathered_lows(1)
            for s in range(2):
                low(0, 0, 0, s)
            with dve.Fori(0, PAIRS // 2 - 1) as pp:
                for q in range(2):
                    pair_steps(pp, q, True)
            for q in range(2):
                pair_steps(PAIRS // 2 - 1, q, q == 0)

        def dense_act(act):
            with act.Fori(0, N_EXP) as e:
                for m in range(EC):
                    act.wait_ge(sem("moe_hidden"), e * EC + (m + 1))
                    act.wait_ge(sem("moe_hidden_read"), e * EC + (m + 1))
                    nc.scalar.activation(exp_silu[:, m, :], bank_aps[4 + m][:, 0:S], ACT.Silu)\
                        .then_inc(sem("moe_silu"), 1)

        def sparse_act(act):
            s_ = nc.scalar

            def high(pp, q, j, s):
                p6 = pp * 6
                if s == 0:
                    act.wait_ge(sem("moe_half_read"), p6 * 2 + (6 * q + j + 1))
                    act.wait_ge(moe_landed[j % 6], pp * 32 + (landed_before[j % 6] + 16 * (q + 1 + j // 6)))
                elif 2 <= j < 6:
                    b, phase = UNIT_FILLS[j - 2]
                    act.wait_ge(moe_full[b], filled(p6, q, phase))
                else:
                    b, phase = UNIT_FILLS[(j + 4) % 6]
                    act.wait_ge(moe_full[b], filled(p6, q + j // 6, phase) - 3)
                s_.activation(high_w[2 * (j % 2) + s], moe_slot[j % 6][:, s * HALF:(s + 1) * HALF], ACT.Copy)\
                    .then_inc(sem("moe_high"), 1)

            def gathered_highs(value):
                for b in range(2):
                    cols = slice(b * 512, (b + 1) * 512)
                    act.wait_ge(moe_freed[b], value)
                    s_.activation(gathered_high[:, cols], gathered[:, cols], ACT.Copy).then_inc(sem("gathered_high"), 1)

            def silu(p6, q, i):
                rows_ = slice(64 * i, 64 * i + 64)
                act.wait_ge(moe_full[2 * i], filled(p6, q, HIDDEN))
                s_.activation(pair_silu[rows_, :], mb[2 * i][rows_, :], ACT.Silu).then_inc(moe_freed[2 * i], 1)

            def pair_steps(pp, q, more):
                p6 = pp * 6
                high(pp, q, 1, 0)
                high(pp, q, 1, 1)
                high(pp, q, 2, 0)
                silu(p6, q, 0)
                high(pp, q, 2, 1)
                high(pp, q, 3, 0)
                high(pp, q, 3, 1)
                high(pp, q, 4, 0)
                silu(p6, q, 1)
                high(pp, q, 4, 1)
                high(pp, q, 5, 0)
                high(pp, q, 5, 1)
                act.wait_ge(moe_full[3], filled(p6, q, MIDDLE))
                s_.activation(act_high, mb[3], ACT.Copy).then_inc(sem("act_high"), 1)
                gathered_highs(filled(p6, q, MIDDLE))
                if more:
                    high(pp, q, 6, 0)
                for n in range(2):
                    act.wait_ge(moe_full[n], filled(p6, q, DOWN))
                    s_.activation(pair_y[0:64, n * 512:(n + 1) * 512], mb[n][0:64, :], ACT.Copy,
                                  scale=slot_gate[q][0:64, :]).then_inc(moe_freed[n], 1)
                if more:
                    high(pp, q, 6, 1)

            act.wait_ge(sem("dve_moe"), 2)
            gathered_highs(1)
            high(0, 0, 0, 0)
            high(0, 0, 0, 1)
            with act.Fori(0, PAIRS // 2 - 1) as pp:
                for q in range(2):
                    pair_steps(pp, q, True)
            for q in range(2):
                pair_steps(PAIRS // 2 - 1, q, q == 0)

        def load_vectors(eng, base, table, half_):
            eng.wait_ge(sem("vec_zero"), 1)
            at = 0
            for name, n in table:
                src = a[name]
                flat = src.rearrange("a b -> (a b)") if len(src.shape) == 2 else src
                eng.dma_start(vec_rows[at:at + n, base:base + P], flat.rearrange("(r c) -> r c", c=P))\
                    .then_inc(sem(f"vecs_landed{half_}"), 16)
                at += n
            assert at <= CONV_ROW
            eng.dma_start(vec_rows[CONV_ROW:CONV_ROW + TAPS, base:base + P], a["conv_k_2"][0, :, base:base + P])\
                .then_inc(sem(f"vecs_landed{half_}"), 16)

        block = ctx.enter_context(nc.Block())

        @block.tensor
        def _(pe):
            mm = nc.tensor.matmul

            def transposes(pairs_, bank):
                for dst, src in pairs_:
                    last = nc.tensor.transpose(dst, src, ident[0:src.shape[0], 0:src.shape[0]])
                last.then_inc(bank.full, 1)

            def norm_turn(tag, count, source=None):
                src = xn3 if source is None else source
                for c in range(KC // 2):
                    bank = banks.take(pe, tag, c)
                    if c == 0 and count:
                        pe.wait_ge(sem("normed"), NT * count)
                    transposes([(bank.ap[:, i * S + t * P:i * S + (t + 1) * P],
                                 src[:, t, (2 * c + i) * P:(2 * c + i + 1) * P])
                                for i in range(2) for t in range(NT)], bank)

            def turned(tag):
                for c in range(KC // 2):
                    banks.wait_read(pe, tag, c)

            def to_features(tag, w, act, kcs, cols):
                for c in range(0, len(cols), 2):
                    bank = banks.take(pe, *tag, c // 2)
                    for i, m in enumerate(cols[c:c + 2]):
                        for k in range(kcs):
                            last = mm(bank.ap[:, i * S:(i + 1) * S], w[:, k, m:m + P], act[:, k, :],
                                      start=(k == 0), stop=(k == kcs - 1))
                    last.then_inc(bank.full, 1)
                return bank

            def to_tokens(tag, w, act, kcs, n):
                for t in range(NT):
                    bank = banks.take(pe, *tag, t)
                    for k in range(kcs):
                        last = mm(bank.ap[:, 0:n], act[:, k, t * P:(t + 1) * P], w[:, k, 0:n],
                                  start=(k == 0), stop=(k == kcs - 1))
                    last.then_inc(bank.full, 1)
                return bank

            def token_units(tag, count, act):
                for c in range(count):
                    w = blocks(weights(pe, *tag, c), KC)
                    read_by(to_tokens((*tag, c), w, act, KC, 512), *tag, c)

            def half_ready(name, s):
                pe.wait_ge(sem("split_low"), 2 * split_no[name] + s + 1)
                return high_of(name, s), low_of(name, s)

            def three_passes(dst, w_high, w_low, a_high, a_low, stationary_weights, start, stop):
                for i, (w, act) in enumerate(((w_high, a_high), (w_high, a_low), (w_low, a_high))):
                    pair = (w, act) if stationary_weights else (act, w)
                    last = mm(dst, *pair, start=(start and i == 0), stop=(stop and i == 2))
                return last

            def split_features(name, tag):
                n = unit_columns(name) // (2 * P)
                for s in range(2):
                    high, low_ = half_ready(name, s)
                    if s == 0 or n == 2:
                        bank = banks.take(pe, *tag, s)
                    for i in range(n):
                        m = slice(i * P, (i + 1) * P)
                        at = (i if n == 2 else s) * S
                        for k in range(KC):
                            a = slice(k * S, (k + 1) * S)
                            last = three_passes(bank.ap[:, at:at + S], high[:, k, m], low_[:, k, m],
                                                turned_high[:, a], turned_low[:, a], True, k == 0, k == KC - 1)
                    if s == 1 or n == 2:
                        last.then_inc(bank.full, 1)
                    half_read[(name, s)] = (bank.full, bank.use + 1)
                read_by(bank, *name)

            def split_tokens(name, tag):
                pair = [banks.take(pe, *tag, t) for t in range(NT)]
                for s in range(2):
                    high, low_ = half_ready(name, s)
                    for t in range(NT):
                        for k in range(4):
                            a = slice((4 * s + k) * S + t * P, (4 * s + k) * S + (t + 1) * P)
                            last = three_passes(pair[t].ap, high[:, k, :], low_[:, k, :], turned_high[:, a],
                                                turned_low[:, a], False, s == 0 and k == 0, s == 1 and k == 3)
                        if s == 1:
                            last.then_inc(pair[t].full, 1)
                    if s == 0:
                        last.then_inc(sem("token_half_read"), 1)
                        token_halves.append(name)
                        half_read[(name, 0)] = (sem("token_half_read"), len(token_halves))
                half_read[(name, 1)] = (pair[1].full, pair[1].use + 1)
                read_by(pair[1], *name)

            token_halves = []

            def split_down(l, n, kb, pair):
                name = ("down", l, n, kb)
                for s in range(2):
                    high, low_ = half_ready(name, s)
                    for t in range(NT):
                        for k in range(4):
                            at = (kb * KC + 4 * s + k) * S + t * P
                            last = three_passes(pair[t].ap, high[:, k, :], low_[:, k, :], actT_high[:, at:at + P],
                                                actT_low[:, at:at + P], False, kb == 0 and s == 0 and k == 0, False)
                    signal, count = (sem("down_half_read"), 3 * n + kb + 1) if s == 0 else \
                                    (sem("down_read"), 6 * l + 3 * n + kb + 1)
                    last.then_inc(signal, 1)
                    half_read[(name, s)] = (signal, count)
                unit_read[name] = half_read[(name, 1)]

            four = [i * P for i in range(4)]

            pe.wait_ge(sem("const_landed"), 16)
            pe.wait_ge(sem("vec_zero"), 1)
            def vector_columns(i, table):
                pe.wait_ge(sem(f"vecs_landed{i}"), 16 * (len(table) + 1))
                bank = banks.take(pe, "vec", i)
                transposes([(bank.ap[:, 0:P], vec_rows[:, i * P:(i + 1) * P])], bank)

            vector_columns(0, VECS1)
            norm_turn("h_mix", 1)
            pe.wait_ge(sem("turned_split"), 4)
            for c in range(8):
                if c == 2:
                    split_tokens(("w_in", c), ("hi",))
                else:
                    split_features(("w_in", c), ("in", c))
                if c == 3:
                    vector_columns(1, VECS2)

            lora = weights(pe, "lora")
            pe.wait_ge(sem("low_ready"), 1)
            for tag, p0, col, b in (("lw", 0, 0, 0), ("la", 64, 0, 0), ("lg", 0, 512, 1)):
                p1 = P if tag != "lw" else 64
                for c in range(2):
                    bank = banks.take(pe, tag, c)
                    for i in range(2):
                        m = col + (2 * c + i) * P
                        last = mm(bank.ap[:, i * S:(i + 1) * S], lora[p0:p1, m:m + P], low[p0:p1, b, :],
                                  start=True, stop=True)
                    last.then_inc(bank.full, 1)
            read_by(bank, "lora")

            for i, m in enumerate([0] + LEVELS):
                pe.wait_ge(sem("hgrn_scaled"), i + 1)
                for t in range(NT):
                    bank = banks.take(pe, "hs", m, t)
                    for h in range(HG_HEADS):
                        last = mm(bank.ap[:, h * P:(h + 1) * P], hk[:, h, t * P:(t + 1) * P],
                                  hq[:, h, t * P:(t + 1) * P], start=True, stop=True)
                    last.then_inc(bank.full, 1)
            pe.wait_ge(sem("hgrn_scaled"), len(LEVELS) + 2)
            bank = banks.take(pe, "hs", P)
            for h in range(HG_HEADS):
                last = mm(bank.ap[:, h * P:(h + 1) * P], hk[:, h, 0:P], hq[:, h, P:S], start=True, stop=True)
            last.then_inc(bank.full, 1)
            for t in range(NT):
                banks.wait_read(pe, "hi", t)
            banks.wait_read(pe, "hs", LEVELS[-1], 0)
            banks.wait_read(pe, "hs", LEVELS[-1], 1)
            banks.wait_read(pe, "hs", P)
            for t in range(NT):
                bank = banks.take(pe, "ho", t)
                for h in range(HG_HEADS):
                    col = slice(h * P, (h + 1) * P)
                    last = mm(bank.ap[:, col], st[:, t, h, :], hv[:, t, col], start=True, stop=(t == 0))
                    if t:
                        last = mm(bank.ap[:, col], sx[:, h, :], hv[:, 0, col], start=False, stop=True)
                last.then_inc(bank.full, 1)
            pe.wait_ge(sem("hgrn_normed"), 1)
            for c in range(2):
                bank = banks.take(pe, "ha", c)
                transposes([(bank.ap[:, i * S + t * P:i * S + (t + 1) * P], o_a[:, t, (2 * c + i) * P:(2 * c + i + 1) * P])
                            for i in range(2) for t in range(NT)], bank)

            pe.wait_ge(sem("kk_sq"), 1)
            for c in range(2):
                bank = banks.take(pe, "kk", c)
                mm(bank.ap[:, :], pairs, page(24)[:, c * 512:(c + 1) * 512], start=True, stop=True).then_inc(bank.full, 1)
            for t in range(NT):
                bank = banks.take(pe, "vt", t)
                transposes([(bank.ap[:, j * P:(j + 1) * P], v_mix[:, j, t * P:(t + 1) * P]) for j in range(4)], bank)
            pe.wait_ge(sem("rk_prod"), 1)
            for c in range(2):
                bank = banks.take(pe, "bonus", c)
                mm(bank.ap[:, :], pairs, page(22)[:, c * 512:(c + 1) * 512], start=True, stop=True).then_inc(bank.full, 1)
            pe.wait_ge(sem("tilded"), 1)
            for b, src in enumerate((b_til, k_til)):
                bank = banks.take(pe, "bk", b)
                transposes([(bank.ap[:, j * P:(j + 1) * P], src[:, j, 0:P]) for j in range(4)], bank)
            for i in range(16):
                t, h = i // 8, i % 8
                j, rows_ = h // 2, slice(64 * (h % 2), 64 * (h % 2) + 64)
                bank = banks.take(pe, "pairs", i)
                for b, src in enumerate((b_til, k_til)):
                    last = mm(bank.ap[:, b * S:(b + 1) * S], src[rows_, j, t * P:(t + 1) * P],
                              ar[rows_, j, t, :, :], start=True, stop=True)
                last.then_inc(bank.full, 1)
            pe.wait_ge(sem("inv_first"), 1)
            for g in range(4):
                bank = banks.take(pe, "x", 1, g)
                transposes([(bank.ap[:, i * P:(i + 1) * P], invT[:, 4 * g + i, :]) for i in range(4)], bank)
            for n, m in enumerate(LEVELS[1:]):
                for g in range(4):
                    banks.wait_read(pe, "x", LEVELS[n], g)
                    bank = banks.take(pe, "ax", m, g)
                    for i in range(4):
                        last = mm(bank.ap[:, i * P:(i + 1) * P], ab[:, 4 * g + i, 0, :], inv[:, 4 * g + i, :],
                                  start=True, stop=True)
                    last.then_inc(bank.full, 1)
                for g in range(4):
                    banks.wait_read(pe, "ax", m, g)
                    bank = banks.take(pe, "xax", m, g)
                    for i in range(4):
                        last = mm(bank.ap[:, i * P:(i + 1) * P], a_inv[:, 4 * g + i, :], invT[:, 4 * g + i, :],
                                  start=True, stop=True)
                    last.then_inc(bank.full, 1)
                if m != LEVELS[-1]:
                    for g in range(4):
                        banks.wait_read(pe, "xax", m, g)
                        bank = banks.take(pe, "x", m, g)
                        transposes([(bank.ap[:, i * P:(i + 1) * P], invT[:, 4 * g + i, :]) for i in range(4)], bank)
            for g in range(4):
                banks.wait_read(pe, "xax", LEVELS[-1], g)
            for t in range(NT):
                for half_ in range(2):
                    rows_ = slice(64 * half_, 64 * half_ + 64)
                    bank = banks.take(pe, "w", t, half_)
                    for j in range(RW_PAIRS):
                        col, h = slice(j * 64, (j + 1) * 64), 2 * j + half_
                        last = mm(bank.ap[:, col], ak[:, 8 * t + h, 0, :], v_tok[:, t, h * 64:(h + 1) * 64],
                                  start=True, stop=(t == 0))
                        if t:
                            last = mm(bank.ap[:, col], ar[rows_, j, t, 0, :], s1[rows_, j, :], start=False, stop=True)
                    last.then_inc(bank.full, 1)
                for half_ in range(2):
                    banks.wait_read(pe, "w", t, half_)
                bank = banks.take(pe, "sa", t)
                for h in range(RW_HEADS):
                    col = slice(h * 64, (h + 1) * 64)
                    last = mm(bank.ap[:, col], invT[:, 8 * t + h, :], w_sb[:, col], start=True, stop=True)
                last.then_inc(bank.full, 1)
                banks.wait_read(pe, "sa", t)
                if t == 0:
                    bank = banks.take(pe, "state")
                    for j in range(4):
                        col = slice(j * P, (j + 1) * P)
                        mm(bank.ap[:, col], bk_tok[:, 0, j, :], sa_sb[:, col], start=True, stop=False)
                        last = mm(bank.ap[:, col], bk_tok[:, 1, j, :], v_tok[:, 0, col], start=False, stop=True)
                    last.then_inc(bank.full, 1)
                for half_ in range(2):
                    rows_ = slice(64 * half_, 64 * half_ + 64)
                    bank = banks.take(pe, "y", t, half_)
                    for j in range(RW_PAIRS):
                        col, h = slice(j * 64, (j + 1) * 64), 2 * j + half_
                        own = slice(h * 64, (h + 1) * 64)
                        mm(bank.ap[:, col], ab[:, 8 * t + h, 1, :], sa_sb[:, own], start=True, stop=False)
                        last = mm(bank.ap[:, col], ak[:, 8 * t + h, 1, :], v_tok[:, t, own],
                                  start=False, stop=(t == 0))
                        if t:
                            last = mm(bank.ap[:, col], ar[rows_, j, t, 1, :], s1[rows_, j, :], start=False, stop=True)
                    last.then_inc(bank.full, 1)
                if t == 0:
                    pe.wait_ge(sem("state_ready"), 1)
                    banks.wait_read(pe, "state")
            pe.wait_ge(sem("rwkv_normed"), 1)
            for c in range(2):
                bank = banks.take(pe, "yb", c)
                transposes([(bank.ap[:, i * S + t * P:i * S + (t + 1) * P], y_tok[:, t, (2 * c + i) * P:(2 * c + i + 1) * P])
                            for i in range(2) for t in range(NT)], bank)

            pe.wait_ge(sem("mixed_ready"), 1)
            token_units(("w_out",), 2, hT3)

            def feed_forward(l):
                for n in range(2):
                    for t in range(NT):
                        banks.wait_read(pe, "w_out" if l == 0 else "w_o", n, t)
                norm_turn(("h_mlp", l), 0, x3)
                pe.wait_ge(sem("turned_split"), 8 if l == 0 else 16)
                for c in range(8):
                    split_features(("up", l, c), ("up", l, c))
                pe.wait_ge(sem("act_ready"), 16 * (l + 1))
                for n in range(2):
                    pair = [banks.take(pe, "down", l, n, t) for t in range(NT)]
                    for kb in range(4):
                        if ("down", l, n, kb) in split_no:
                            split_down(l, n, kb, pair)
                            continue
                        w = blocks(weights(pe, "down", l, n, kb), KC)
                        for t in range(NT):
                            for k in range(KC):
                                last = mm(pair[t].ap[:, :], actT[:, kb * KC + k, t * P:(t + 1) * P], w[:, k, :],
                                          start=(kb == 0 and k == 0), stop=(kb == 3 and k == KC - 1))
                            if kb == 3:
                                last.then_inc(pair[t].full, 1)
                        if kb < 3:
                            last.then_inc(sem("down_read"), 1)
                            unit_read[("down", l, n, kb)] = (sem("down_read"), 6 * l + 3 * n + kb + 1)
                        else:
                            read_by(pair[1], "down", l, n, kb)
                if l == 0:
                    pe.wait_ge(sem("mod_used"), 12)
                    bank = banks.take(pe, "mod_columns")
                    for i, (c, m) in enumerate(MOD_COLUMNS):
                        last = mm(bank.ap[:, i:i + P], mod_acc[:, c, m * P:(m + 1) * P], ones, start=True, stop=True)
                    last.then_inc(bank.full, 1)
                    for i, c in enumerate(MOD_ROWS):
                        bank = banks.take(pe, "mod_row", i)
                        mm(bank.ap[:, :], ones, mod_acc[:, c, :], start=True, stop=True).then_inc(bank.full, 1)
                pe.wait_ge(sem("p_landed"), 16 * (l + 1))
                bank = banks.take(pe, "pT", l)
                transposes([(bank.ap[:, k * S + t * P:k * S + (t + 1) * P], p_tok[:, t, k * P:(k + 1) * P])
                            for k in range(2) for t in range(NT)], bank)
                banks.wait_read(pe, "pT", l)
                w = blocks(weights(pe, "ple", l)[:, 0:2 * D], 2)
                for n in range(2):
                    bank = to_tokens(("ple", l, n), w[:, :, n * 512:(n + 1) * 512], pT, 2, 512)
                read_by(bank, "ple", l)
                for n in range(2):
                    for t in range(NT):
                        banks.wait_read(pe, "down", l, n, t)
                norm_turn(("x_gate", l), 0, x3)
                turned(("x_gate", l))
                token_units(("gate", l), 2, hT3)

            def attend(tag, items_q, items_k, value, landed_sem, probs, probsT):
                n = 2 * HEADS
                for i in range(n + LAG):
                    if i < n:
                        h, t = i // 2, i % 2
                        bank = banks.take(pe, tag, "s", i)
                        mm(bank.ap[:, 0:(t + 1) * P], items_q(h)[:, t * P:(t + 1) * P], items_k(h)[:, 0:(t + 1) * P],
                           start=True, stop=True).then_inc(bank.full, 1)
                    if i >= LAG:
                        i2 = i - LAG
                        h, t = i2 // 2, i2 % 2
                        bank = banks.take(pe, tag, "pT", i2)
                        pe.wait_ge(sem(landed_sem), i2 + 1)
                        transposes([(bank.ap[:, k * P:(k + 1) * P], probs[:, i2 % 8, k * P:(k + 1) * P])
                                    for k in range(t + 1)], bank)
                        if t == 1 and h >= 1:
                            out_of(tag, h - 1, value, probsT)
                out_of(tag, HEADS - 1, value, probsT)

            open_bank = {}

            def out_of(tag, h, value, probsT):
                if h % 2 == 0:
                    open_bank[tag] = banks.take(pe, tag, "o", h // 2)
                bank = open_bank[tag]
                for t in range(NT):
                    banks.wait_read(pe, tag, "pT", 2 * h + t)
                    for k in range(t + 1):
                        last = mm(bank.ap[:, (h % 2) * S + t * P:(h % 2) * S + (t + 1) * P], value(h, k),
                                  probsT[:, (2 * h + t) % 4, k, :], start=(k == 0), stop=(k == t))
                if h % 2:
                    last.then_inc(bank.full, 1)
                else:
                    last.then_inc(sem(tag + "_even_read"), 1)

            feed_forward(0)
            pe.wait_ge(sem("ple_added"), 1)
            norm_turn("h_att", 0, x3)
            pe.wait_ge(sem("turned_split"), 12)
            for c in range(6):
                split_tokens(("qkv", c), ("qkv", c))
            pe.wait_ge(sem("rotated"), 2)
            for tag, src in (("qT", q_tok), ("kT", k_tok)):
                for c in range(4):
                    bank = banks.take(pe, tag, c)
                    transposes([(bank.ap[:, i * S + t * P:i * S + (t + 1) * P], src[:, t, (2 * c + i) * P:(2 * c + i + 1) * P])
                                for i in range(2) for t in range(NT)], bank)
            for tag in ("qT", "kT"):
                for c in range(4):
                    banks.wait_read(pe, tag, c)
            attend("att", lambda h: qT[:, h, :], lambda h: kT[:, h, :],
                   lambda h, k: v_att[:, k, h * P:(h + 1) * P], "att_prob", prob, probT)
            for c in range(4):
                banks.wait_read(pe, "att", "o", c)
            token_units(("w_o",), 2, hT3)
            feed_forward(1)

            norm_turn("h_in2", 2)
            turned("h_in2")
            w = blocks(weights(pe, "in2", 0), KC)
            read_by(to_features(("av",), w, hT3, KC, four), "in2", 0)
            w = blocks(weights(pe, "in2", 1)[:, 0:KC * 384], KC)
            read_by(to_tokens(("cq",), w, hT3, KC, 384), "in2", 1)
            w = blocks(weights(pe, "in2", 2), KC)
            read_by(to_features(("qi",), w, hT3, KC, four), "in2", 2)
            w = weights(pe, "in2", 3)
            to_features(("ki",), blocks(w[:, 0:KC * P], KC), hT3, KC, [0])
            to_features(("pool",), blocks(w[:, KC * P:KC * 384], KC), hT3, KC, [0, P])
            wiw = blocks(w[:, KC * 384:KC * 392], KC)
            bank = banks.take(pe, "wi")
            for t in range(NT):
                for k in range(KC):
                    last = mm(bank.ap[:, t * 8:(t + 1) * 8], hT3[:, k, t * P:(t + 1) * P], wiw[:, k, :],
                              start=(k == 0), stop=(k == KC - 1))
            last.then_inc(bank.full, 1)
            read_by(bank, "in2", 3)
            w = weights(pe, "dsa")
            bank = banks.take(pe, "ukT")
            transposes([(bank.ap[:, j * P:(j + 1) * P], w[:, 1024 + j * P:1024 + (j + 1) * P]) for j in range(4)], bank)
            pe.wait_ge(sem("latents_normed"), 1)
            bank = banks.take(pe, "cqT")
            transposes([(bank.ap[:, k * S + t * P:k * S + (t + 1) * P], cq_tok[:, t, k * P:(k + 1) * P])
                        for k in range(2) for t in range(NT)], bank)
            bank = banks.take(pe, "ckvT")
            transposes([(bank.ap[:, t * P:(t + 1) * P], ckv_tok[:, t, :]) for t in range(NT)], bank)
            banks.wait_read(pe, "qi", 0)
            banks.wait_read(pe, "qi", 1)
            banks.wait_read(pe, "ki", 0)
            for t in range(NT):
                for g in range(4):
                    bank = banks.take(pe, "idx", t, g)
                    rows_ = slice(64 * (g // 2), 64 * (g // 2) + 64)
                    for i in range(2):
                        j = 2 * (g % 2) + i
                        last = mm(bank.ap[:, i * S:(i + 1) * S], qiT[rows_, j, t * P:(t + 1) * P], kiT[rows_, :],
                                  start=True, stop=True)
                    last.then_inc(bank.full, 1)
            banks.wait_read(pe, "cqT")
            to_features(("q2",), blocks(w[:, 0:1024], 2), cqT, 2, four)
            banks.wait_read(pe, "ukT")
            banks.wait_read(pe, "q2", 0)
            banks.wait_read(pe, "q2", 1)
            for g in range(4):
                bank = banks.take(pe, "qabs", g)
                rows_ = slice(64 * (g // 2), 64 * (g // 2) + 64)
                for i in range(2):
                    j = 2 * (g % 2) + i
                    last = mm(bank.ap[:, i * S:(i + 1) * S], w_ukT[rows_, j, :], q2T[rows_, j, :], start=True, stop=True)
                last.then_inc(bank.full, 1)
            pe.wait_ge(sem("conv_done"), 1)
            bank = banks.take(pe, "cmean")
            for c in range(2):
                last = mm(bank.ap[:, 0:S], ones, conv_acc[:, c, :], start=(c == 0), stop=(c == 1))
            last.then_inc(bank.full, 1)
            pe.wait_ge(sem("conv_centred"), 1)
            bank = banks.take(pe, "cvar")
            for c in range(2):
                last = mm(bank.ap[:, 0:S], ones, conv_sq[:, c, :], start=(c == 0), stop=(c == 1))
            last.then_inc(bank.full, 1)
            pe.wait_ge(sem("pool_ready"), 1)
            for g in range(2):
                rows_ = slice(64 * g, 64 * g + 64)
                bank = banks.take(pe, "poolo", g)
                for c in range(2):
                    last = mm(bank.ap[rows_, c * S:(c + 1) * S], w[rows_, 2048 + c * 64:2048 + (c + 1) * 64],
                              pool_d[rows_, c, :], start=True, stop=True)
                last.then_inc(bank.full, 1)
            for g in range(4):
                banks.wait_read(pe, "qabs", g)
            banks.wait_read(pe, "ckvT")
            attend("dsa", lambda h: q_abs[:, h, :], lambda h: ckvT, lambda h, k: ckv_tok[:, k, :],
                   "dsa_prob", prob2, probT2)
            for c in range(4):
                banks.wait_read(pe, "dsa", "o", c)
            for g in range(2):
                rows_ = slice(64 * g, 64 * g + 64)
                for c in range(2):
                    bank = banks.take(pe, "yatt", g, c)
                    for i in range(2):
                        h = 2 * (2 * c + i) + g
                        last = mm(bank.ap[rows_, i * S:(i + 1) * S], w[:, 1536 + h * 64:1536 + (h + 1) * 64],
                                  ctxT[:, h, :], start=True, stop=True)
                    last.then_inc(bank.full, 1)
            read_by(bank, "dsa")
            pe.wait_ge(sem("conv_out"), 2)
            for g in range(2):
                banks.wait_read(pe, "poolo", g)
                for c in range(2):
                    banks.wait_read(pe, "yatt", g, c)
            token_units(("w_out2",), 2, hT3)

            norm_turn("h_moe", 3)
            turned("h_moe")
            pe.wait_ge(sem("router_landed"), 32)
            bank = banks.take(pe, "router")
            rw = blocks(router[:, :], KC)
            for t in range(NT):
                for k in range(KC):
                    last = mm(bank.ap[:, t * 36:(t + 1) * 36], hT3[:, k, t * P:(t + 1) * P], rw[:, k, :],
                              start=(k == 0), stop=(k == KC - 1))
            last.then_inc(bank.full, 1)
            pe.wait_ge(sem("chosen_ready"), 1)
            bank = banks.take(pe, "rank")
            strict = c_("strict")
            for t in range(NT):
                last = mm(bank.ap[:, t * N_EXP:(t + 1) * N_EXP], strict, chosen[:, t, :], start=True, stop=(t == 0))
            mm(bank.ap[:, N_EXP:2 * N_EXP], ones, chosen[:, 0, :], start=False, stop=True)
            for t in range(NT):
                last = mm(bank.ap[:, 2 * N_EXP:3 * N_EXP], ones, chosen[:, t, :], start=(t == 0), stop=(t == 1))
            last.then_inc(bank.full, 1)
            for b in range(8):
                pe.wait_ge(banks.freed[b], (banks.n - 1 - b) // 8 + 1)
            y_bank = [[bank_aps[2 * t + n] for n in range(2)] for t in range(NT)]
            for t in range(NT):
                for n in range(2):
                    last = mm(y_bank[t][n], zeros, const[:, 0:512], start=True, stop=False, skip_group_check=True)
            last.then_inc(sem("moe_down"), 1)
            pe.wait_ge(sem("most_ready"), 1)
            crowded = pe.value_load(most_int[0:1, 0:1], min_val=0, max_val=S)
            with pe.If(crowded > SLOTS_OF):
                dense_pe(pe, y_bank)
            with pe.Else():
                sparse_pe(pe, y_bank)
            for t in range(NT):
                for n in range(2):
                    last = mm(y_bank[t][n], zeros, const[:, 0:512], start=False, stop=True, skip_group_check=True)
            last.then_inc(sem("moe_sum"), 1)

        @block.vector
        def _(dve):
            v = nc.vector
            flag = iter([flags[:, i:i + 1] for i in range(24)])
            step = Chain(dve, sem("dve_step"))

            def evacuate(dst, *name):
                bank = banks.read(dve, *name)
                v.tensor_copy(dst, bank.ap).then_inc(bank.freed, 1)

            def norm(k):
                dve.wait_ge(sem("rms_root"), k)
                step(v.reciprocal(rstd, rstd))
                for t in range(NT):
                    v.tensor_scalar(xn3[:, t, :], x3[:, t, :], rstd[:, t:t + 1], None, ALU.mult)\
                        .then_inc(sem("normed"), 1)

            def scales(k):
                dve.wait_ge(sem("rms_root"), k)
                step(v.reciprocal(rstd, rstd))

            def add_to_x(tag, *key, ns=(0, 1), scale=None):
                for n in ns:
                    for t in range(NT):
                        bank = banks.read(dve, tag, *key, n, t)
                        part = x3[:, t, n * 512:(n + 1) * 512]
                        if scale is None:
                            v.tensor_tensor(part, part, bank.ap, ALU.add).then_inc(bank.freed, 1)
                        else:
                            v.scalar_tensor_tensor(part, bank.ap, scale[:, t:t + 1], part, ALU.mult, ALU.add)\
                                .then_inc(bank.freed, 1)

            def split_low(*name):
                for s in range(2):
                    dve.wait_ge(sem("split_high"), 2 * split_no[name] + s + 1)
                    v.tensor_tensor(low_of(name, s), half_of(slot(name), name, s), high_of(name, s).bitcast(F32),
                                    ALU.subtract).then_inc(sem("split_low"), 1)

            def split_turned(*tag):
                for c in range(KC // 2):
                    cols = slice(c * 512, (c + 1) * 512)
                    banks.wait_read(dve, *tag, c)
                    step(v.tensor_copy(turned_high[:, cols], hT[:, cols]))
                    v.tensor_tensor(turned_low[:, cols], hT[:, cols], turned_high[:, cols].bitcast(F32), ALU.subtract)\
                        .then_inc(sem("turned_split"), 1)

            v.memset(vec_rows, 0.0).then_inc(sem("vec_zero"), 1)
            v.memset(raw[:, :, 0:1], 0.0).then_inc(sem("dve_step"), 1)
            step.n += 1
            step(v.memset(st, 0.0))
            split_low("w_in", 0)
            bank = banks.read(dve, "vec", 0)
            v.tensor_copy(vec[:, 0:P], bank.ap[:, 0:P]).then_inc(bank.freed, 1)
            norm(1)
            banks.wait_read(dve, "vec", 0)
            l3 = v1("hgrn_lb", 0, 12)
            step(v.tensor_tensor(lb, l3[:, 0:4], l3[:, 4:8], ALU.max))
            step(v.tensor_tensor(lb, lb, l3[:, 8:12], ALU.max))
            v.tensor_tensor(blocks(lb_d, 3), blocks(l3, 3), mid(lb, 3), ALU.subtract).then_inc(sem("lb_shifted"), 1)
            dve.wait_ge(sem("lb_exp"), 1)
            step(v.tensor_tensor(lb, lb_e[:, 0:4], lb_e[:, 4:8], ALU.add))
            step(v.tensor_tensor(lb, lb, lb_e[:, 8:12], ALU.add))
            step(v.reciprocal(lb, lb))
            step(v.tensor_tensor(lb, lb, lb_e[:, 0:4], ALU.mult))
            step(v.tensor_scalar(lb_c, lb, -1.0, 1.0, ALU.mult, ALU.add))
            banks.read(dve, "h_mix", KC // 2 - 1)
            split_turned("h_mix")
            for c in range(1, 5):
                split_low("w_in", c)
            bank = banks.read(dve, "vec", 1)
            v.tensor_copy(vec[:, P:2 * P], bank.ap[:, 0:P]).then_inc(bank.freed, 1)
            for c in range(4, 8):
                if c < 7:
                    split_low("w_in", c + 1)
                for i in range(2 if c < 7 else 1):
                    b = 4 * (c - 4) + 2 * i
                    bank = banks.read(dve, "in", c, i)
                    v.tensor_copy(raw[:, b:b + 2, 1:S + 1], blocks(bank.ap, 2)).then_inc(bank.freed, 1)
            for c in range(4, 8):
                for i in range(2 if c < 7 else 1):
                    banks.wait_read(dve, "in", c, i)

            def shift_mix(dst, b0, n):
                step(v.tensor_tensor(dst, raw[:, b0:b0 + n, 0:S], raw[:, b0:b0 + n, 1:S + 1], ALU.subtract))
                for i in range(n):
                    last = v.scalar_tensor_tensor(dst[:, i, :], dst[:, i, :], v1("rwkv_mu", b0 + i),
                                                  raw[:, b0 + i, 1:S + 1], ALU.mult, ALU.add)
                    last.then_inc(sem("dve_step"), 1)
                    step.n += 1
                dve.wait_ge(sem("dve_step"), step.n)

            shift_mix(low, 12, 2)
            v.memset(next(flag), 0.0).then_inc(sem("low_mixed"), 1)

            for i in range(2):
                banks.wait_read(dve, "in", 0, i)
                banks.wait_read(dve, "in", 1, i)
            for j in range(4):
                step(v.tensor_scalar(hf[:, j, :], hf[:, j, :], lb_c[:, j:j + 1], lb[:, j:j + 1], ALU.mult, ALU.add))
            v.tensor_scalar(hk, hf, -1.0, 1.0, ALU.mult, ALU.add).then_inc(sem("hgrn_scaled"), 1)

            def take_scores(m):
                for t in range(NT):
                    bank = banks.read(dve, "hs", m, t)
                    mask = mid(level_mask(m) if m else ident, HG_HEADS).bitcast(I32)
                    v.copy_predicated(st[:, t], mask, blocks(bank.ap, HG_HEADS)).then_inc(bank.freed, 1)

            cum8, log8 = blocks(page(12), 8), blocks(page(6), 8)

            def rwkv_ahead(i):
                if i == 0:
                    shift_mix(r_mix, 0, 4)
                elif i == 1:
                    shift_mix(k_mix, 4, 4)
                elif i == 2:
                    shift_mix(v_mix, 8, 4)
                elif i == 3:
                    for c in range(2):
                        banks.wait_read(dve, "lw", c)
                        banks.wait_read(dve, "la", c)
                        banks.wait_read(dve, "lg", c)
                    step(v.tensor_scalar(logdec, logdec, DECAY_SCALE, None, ALU.mult))
                    for j in range(4):
                        last = v.tensor_scalar(kk[:, j, :], k_mix[:, j, :], v1("rwkv_kk", j), None, ALU.mult)
                    step(last)
                    v.tensor_tensor(page(24), page(7), page(7), ALU.mult).then_inc(sem("kk_sq"), 1)
                elif i == 4:
                    for b in range(8):
                        last = v.tensor_tensor_scan(cum8[:, b, :], ones, log8[:, b, :], 0.0, ALU.mult, ALU.add)
                    step(last)
                elif i == 5:
                    step(v.tensor_copy(c_mid, cum8[:, :, 63]))
                    step(v.tensor_tensor(cum8, cum8, tail(c_mid, P), ALU.subtract))
                    step(v.tensor_tensor(s_scale, cum8[:, 0:8:2, P - 1], c_mid[:, 1:8:2], ALU.add))

            take_scores(0)
            v.tensor_tensor(hq, hq, hf, ALU.mult).then_inc(sem("hgrn_scaled"), 1)
            take_scores(1)
            ends = page(15)
            for i, m in enumerate(LEVELS):
                n = 4 * S // (2 * m)
                e2 = ends[:, 0:2 * n].rearrange("p (b a) -> p b a", a=2)
                q4 = page(13).rearrange("p (b a s) -> p b a s", a=2, s=m)
                k4 = page(14).rearrange("p (b a s) -> p b a s", a=2, s=m)
                dve.wait_ge(sem("hgrn_scaled"), i + 2)
                step(v.tensor_tensor(q4[:, :, 1, :], q4[:, :, 1, :], tail(e2[:, :, 0], m), ALU.mult))
                if m < LEVELS[-1]:
                    step(v.tensor_tensor(h_end[i % 2][:, 0:n], e2[:, :, 0], e2[:, :, 1], ALU.mult))
                v.tensor_tensor(k4[:, :, 0, :], k4[:, :, 0, :], tail(e2[:, :, 1], m), ALU.mult)\
                    .then_inc(sem("hgrn_scaled"), 1)
                ends = h_end[i % 2]
                rwkv_ahead(i)
                if m < LEVELS[-1]:
                    take_scores(2 * m)
            bank = banks.read(dve, "hs", P)
            v.tensor_copy(sx, blocks(bank.ap, HG_HEADS)).then_inc(bank.freed, 1)
            for t in range(NT):
                evacuate(o_a[:, t, :], "ho", t)
            for t in range(NT):
                banks.wait_read(dve, "ho", t)
            o8 = blocks(page(21), 8)
            step(v.tensor_tensor(page(23), page(21), page(21), ALU.mult))
            step(v.tensor_reduce(hg_ss, blocks(page(23), 8), AX.X, ALU.add))
            v.tensor_scalar(hg_ss, hg_ss, 1.0 / P, EPS, ALU.mult, ALU.add).then_inc(sem("hgrn_sq"), 1)
            dve.wait_ge(sem("hgrn_root"), 1)
            step(v.reciprocal(hg_ss, hg_ss))
            v.tensor_tensor(o8, o8, tail(hg_ss, P), ALU.mult).then_inc(sem("hgrn_normed"), 1)
            for c in range(2):
                bank = banks.read(dve, "ha", c)
                for i in range(2):
                    h = 2 * c + i
                    last = v.scalar_tensor_tensor(hT3[:, h, :], bank.ap[:, i * S:(i + 1) * S], v1("hgrn_onorm", h),
                                                  hgT[:, h, :], ALU.mult, ALU.mult)
                last.then_inc(bank.freed, 1)
            for c in range(2):
                banks.wait_read(dve, "ha", c)

            for j in range(4):
                step(v.tensor_scalar(k_adj[:, j, :], a_gate[:, j, :], -1.0, v1("rwkv_ka", j), ALU.add, ALU.mult))
            step(v.scalar_tensor_tensor(page(13), page(13), 1.0, page(5), ALU.add, ALU.mult))
            for j in range(4):
                last = v.scalar_tensor_tensor(blocks(page(22), 4)[:, j, :], r_mix[:, j, :], v1("rwkv_rk", j),
                                              k_adj[:, j, :], ALU.mult, ALU.mult)
                if j < 3:
                    step(last)
            last.then_inc(sem("rk_prod"), 1)
            for c in range(2):
                bank = banks.read(dve, "kk", c)
                v.tensor_scalar(page(21)[:, c * 512:(c + 1) * 512], bank.ap, 1e-24, None, ALU.max).then_inc(bank.freed, 1)
            for t in range(NT):
                evacuate(v_tok[:, t, :], "vt", t)
            for c in range(2):
                bank = banks.read(dve, "bonus", c)
                v.tensor_tensor(page(18)[:, c * 512:(c + 1) * 512], bank.ap, page(8)[:, c * 512:(c + 1) * 512],
                                ALU.mult).then_inc(bank.freed, 1)
            dve.wait_ge(sem("kk_root"), 1)
            step(v.reciprocal(page(21), page(21)))
            step(v.tensor_tensor(page(7), page(7), page(21), ALU.mult))
            v.tensor_tensor(page(21), page(12), page(6), ALU.subtract).then_inc(sem("cum_ready"), 1)
            step(v.tensor_tensor(page(16), page(7), page(10), ALU.mult))
            dve.wait_ge(sem("decays_exp"), 1)
            ar8 = page(14, 2).rearrange("p (i a s) -> p i a s", i=8, a=2)
            step(v.scalar_tensor_tensor(ar8[:, :, 0, :], blocks(page(7), 8), -1.0, blocks(page(21), 8), ALU.mult, ALU.mult))
            step(v.tensor_tensor(ar8[:, :, 1, :], blocks(page(4), 8), blocks(page(22), 8), ALU.mult))
            step(v.tensor_tensor(page(16), page(16), page(12), ALU.mult))
            v.tensor_tensor(page(17), page(13), page(12), ALU.mult).then_inc(sem("tilded"), 1)
            dve.wait_ge(sem("tilded"), 1)
            step(v.tensor_copy(invT, mid(ident, 16)))
            both = const[:, cols_at["strict"][0]:cols_at["upto"][1]]
            for i in range(16):
                bank = banks.read(dve, "pairs", i)
                v.tensor_tensor(ab[:, i].rearrange("p a s -> p (a s)"), bank.ap[:, 0:S], both, ALU.mult)
                v.tensor_tensor(ak[:, i].rearrange("p a s -> p (a s)"), bank.ap[:, S:2 * S], both, ALU.mult)\
                    .then_inc(bank.freed, 1)
            for i in range(8, 16):
                banks.wait_read(dve, "pairs", i)
            v.copy_predicated(invT, mid(level_mask(1), 16).bitcast(I32), ab[:, :, 0, :]).then_inc(sem("inv_first"), 1)
            dve.wait_ge(sem("inv_first"), 1)
            for m in LEVELS[1:]:
                for g in range(4):
                    bank = banks.read(dve, "xax", m, g)
                    v.copy_predicated(invT[:, 4 * g:4 * g + 4, :], mid(level_mask(m), 4).bitcast(I32),
                                      blocks(bank.ap, 4)).then_inc(bank.freed, 1)
            def take_halves(dst, tag, t):
                for half_ in range(2):
                    bank = banks.read(dve, tag, t, half_)
                    v.tensor_copy(dst.rearrange("p (j a v) -> p j a v", a=2, v=64)[:, :, half_, :],
                                  blocks(bank.ap[:, 0:S], 4)).then_inc(bank.freed, 1)

            dve.wait_ge(sem("scale_exp"), 1)
            for t in range(NT):
                take_halves(w_sb, "w", t)
                evacuate(sa_sb, "sa", t)
                if t == 0:
                    bank = banks.read(dve, "state")
                    b4 = blocks(bank.ap, 4)
                    v.tensor_tensor(s1[0:64], b4[0:64, :, 0:64], tail(s_scale[0:64, :], 64), ALU.mult)\
                        .then_inc(sem("state_ready"), 1)
                    v.tensor_tensor(s1[64:P], b4[64:P, :, 64:P], tail(s_scale[64:P, :], 64), ALU.mult)\
                        .then_inc(bank.freed, 1)
                take_halves(y_tok[:, t, :], "y", t)
            for t in range(NT):
                for half_ in range(2):
                    banks.wait_read(dve, "y", t, half_)
            y16 = blocks(page(21), 16)
            step(v.tensor_reduce(rw_mu, y16, AX.X, ALU.add))
            step(v.tensor_scalar(rw_mu, rw_mu, 1.0 / 64, None, ALU.mult))
            step(v.tensor_tensor(y16, y16, tail(rw_mu, 64), ALU.subtract))
            step(v.tensor_tensor(page(13), page(21), page(21), ALU.mult))
            step(v.tensor_reduce(rw_ss, blocks(page(13), 16), AX.X, ALU.add))
            v.tensor_scalar(rw_ss, rw_ss, 1.0 / 64, LN_EPS, ALU.mult, ALU.add).then_inc(sem("rwkv_sq"), 1)
            dve.wait_ge(sem("rwkv_root"), 1)
            step(v.reciprocal(rw_ss, rw_ss))
            v.tensor_tensor(y16, y16, tail(rw_ss, 64), ALU.mult).then_inc(sem("rwkv_normed"), 1)
            for c in range(2):
                bank = banks.read(dve, "yb", c)
                for i in range(2):
                    j = 2 * c + i
                    last = v.tensor_scalar(hT3[:, 4 + j, :], bank.ap[:, i * S:(i + 1) * S], v1("rwkv_ln_w", j),
                                           v1("rwkv_ln_b", j), ALU.mult, ALU.add)
                    if i == 0:
                        step(last)
                last.then_inc(bank.freed, 1)
                banks.wait_read(dve, "yb", c)
            out4 = hT[:, 4 * S:8 * S]
            step(v.tensor_tensor(out4, out4, page(18), ALU.add))
            v.tensor_tensor(out4, out4, page(11), ALU.mult).then_inc(sem("mixed_ready"), 1)

            split_low("up", 0, 0)
            add_to_x("w_out")

            def modulate(c):
                s = unit_of[("mod", c)] % SLOTS
                dve.wait_ge(landed[s], landed_value[("mod", c)])
                w = blocks(slot(("mod", c)), KC)
                dst = mod_acc[:, c, :]
                step(v.tensor_scalar(dst, w[:, 0, :], cond[:, 0:1], None, ALU.mult))
                for k in range(1, KC):
                    last = v.scalar_tensor_tensor(dst, w[:, k, :], cond[:, k:k + 1], dst, ALU.mult, ALU.add)
                    if k < KC - 1:
                        step(last)
                last.then_inc(sem("mod_used"), 1)

            dve.wait_ge(sem("cond_ready"), 1)

            def feed_forward(l):
                split_turned(("h_mlp", l))
                for c in range(8):
                    if c < 7:
                        split_low("up", l, c + 1)
                    elif l:
                        split_low("down", 1, 0, 0)
                    if c == 0:
                        scales(2 if l == 0 else 4)
                        step(v.tensor_tensor(rstd2, rstd, rstd, ALU.mult))
                    for i in range(2):
                        banks.wait_read(dve, "up", l, c, i)
                        buf = relu[:, (2 * c + i) % 4, :]
                        chunk = 4 * c + 2 * i
                        if l == 0 or chunk >= act_split:
                            v.tensor_tensor(actT[:, chunk:chunk + 2, :], blocks(buf, 2), blocks(buf, 2), ALU.mult)\
                                .then_inc(sem("act_ready"), 1)
                        else:
                            cols = slice(chunk * S, (chunk + 2) * S)
                            step(v.tensor_tensor(buf, buf, buf, ALU.mult))
                            step(v.tensor_copy(actT_high[:, cols], buf))
                            v.tensor_tensor(actT_low[:, cols], buf, actT_high[:, cols].bitcast(F32), ALU.subtract)\
                                .then_inc(sem("act_ready"), 1)
                    if l == 0 and c % 2:
                        modulate(c // 2)
                for n in range(2):
                    if l == 0:
                        for c in range(4):
                            modulate(4 + 4 * n + c)
                    else:
                        for unit in (((0, 1), (0, 2), (1, 0), (1, 1)), ((1, 2),))[n]:
                            split_low("down", 1, *unit)
                    add_to_x("down", l, ns=(n,), scale=rstd2)
                if l == 0:
                    bank = banks.read(dve, "mod_columns")
                    v.tensor_tensor(modc[:, 0:16], bank.ap[:, 0:16], v2("mod_b_2", 0, 16), ALU.add)
                    v.tensor_tensor(modc[:, 24:40], bank.ap[:, 16:32], v2("mod_b_2", 24, 16), ALU.add)\
                        .then_inc(bank.freed, 1)
                    banks.wait_read(dve, "mod_columns")
                    step(v.scalar_tensor_tensor(sc1, modc[:, 8:16], 1.0, v2("norm1_g_2", 0, 8), ALU.add, ALU.mult))
                    step(v.scalar_tensor_tensor(sc2, modc[:, 32:40], 1.0, v2("norm2_g_2", 0, 8), ALU.add, ALU.mult))
                    dve.wait_ge(sem("gate_bias_landed"), 32)
                    for i in range(4):
                        bank = banks.read(dve, "mod_row", i)
                        part = (g1_row if i < 2 else g2_row)[:, (i % 2) * 512:(i % 2 + 1) * 512]
                        v.tensor_tensor(part, part, bank.ap, ALU.add).then_inc(bank.freed, 1)
                dve.wait_ge(sem("ple_root"), l + 1)
                step(v.reciprocal(ssq, ssq))
                dve.wait_ge(sem("big_row_landed"), 16 * (l + 1))
                for t in range(NT):
                    step(v.scalar_tensor_tensor(ple_raw[:, t, :], ple_raw[:, t, :], ssq[:, t:t + 1], big_row,
                                                ALU.mult, ALU.mult))
                if l == 0:
                    split_low("qkv", 0)
                for n in range(2):
                    for t in range(NT):
                        banks.wait_read(dve, "gate", l, n, t)
                step(v.tensor_tensor(page(21, 2), page(21, 2), page(23, 2), ALU.mult))
                v.tensor_tensor(x[:, :], x[:, :], page(21, 2), ALU.add).then_inc(sem("ple_added"), 1)
                dve.wait_ge(sem("ple_added"), l + 1)

            def head_norm(tok, gain, k):
                flat = tok.rearrange("p t n -> p (t n)")
                t16 = blocks(flat, 16)
                step(v.tensor_tensor(sq, flat, flat, ALU.mult))
                step(v.tensor_reduce(head_ss, blocks(sq, 16), AX.X, ALU.add))
                v.tensor_scalar(head_ss, head_ss, 1.0 / P, EPS, ALU.mult, ALU.add).then_inc(sem("head_sq"), 1)
                dve.wait_ge(sem("head_root"), k)
                step(v.reciprocal(head_ss, head_ss))
                step(v.tensor_tensor(t16, t16, tail(head_ss, P), ALU.mult))
                step(v.tensor_tensor(t16, t16, mid(gain, 16), ALU.mult))
                s4 = sq.rearrange("p (t h d) -> p t h d", t=NT, h=HEADS)
                f4 = flat.rearrange("p (t h d) -> p t h d", t=NT, h=HEADS)
                for t in range(NT):
                    cos = mid(c_("cos", t * 64, (t + 1) * 64), HEADS)
                    sin = mid(c_("sin", t * 64, (t + 1) * 64), HEADS)
                    lo, hi = f4[:, t, :, 0:64], f4[:, t, :, 64:P]
                    step(v.tensor_tensor(s4[:, t, :, 0:64], lo, sin, ALU.mult))
                    step(v.tensor_tensor(s4[:, t, :, 64:P], hi, sin, ALU.mult))
                    step(v.tensor_tensor(lo, lo, cos, ALU.mult))
                    step(v.tensor_tensor(hi, hi, cos, ALU.mult))
                    step(v.tensor_tensor(lo, lo, s4[:, t, :, 64:P], ALU.subtract))
                    last = v.tensor_tensor(hi, hi, s4[:, t, :, 0:64], ALU.add)
                    if t < NT - 1:
                        step(last)
                last.then_inc(sem("rotated"), 1)
                dve.wait_ge(sem("rotated"), k)

            def attend(tag, scale, mask, probs, extra=None):
                n = 2 * HEADS
                for i in range(n + 2):
                    if i < n:
                        t = i % 2
                        bank = banks.read(dve, tag, "s", i)
                        if i >= 8:
                            banks.read(dve, tag, "pT", i - 8)
                        part = probs[:, i % 8, 0:(t + 1) * P]
                        v.scalar_tensor_tensor(part, bank.ap[:, 0:(t + 1) * P], scale, mask(t), ALU.mult, ALU.add)\
                            .then_inc(bank.freed, 1)
                        banks.wait_read(dve, tag, "s", i)
                        v.tensor_reduce(nmax[:, i:i + 1], part, AX.X, ALU.max, negate=True).then_inc(sem(tag + "_max"), 1)
                    if i >= 2:
                        i2 = i - 2
                        t = i2 % 2
                        dve.wait_ge(sem(tag + "_exp"), i2 + 1)
                        step(v.reciprocal(rinv[:, i2:i2 + 1], rsum[:, i2:i2 + 1]))
                        part = probs[:, i2 % 8, 0:(t + 1) * P]
                        v.tensor_scalar(part, part, rinv[:, i2:i2 + 1], None, ALU.mult).then_inc(sem(tag + "_prob"), 1)

            feed_forward(0)
            split_turned("h_att")
            dve.wait_ge(sem("rms_root"), 3)
            v.reciprocal(rstd, rstd).then_inc(sem("scales_ready"), 1)
            dve.wait_ge(sem("rows_landed"), 16 * len(ROWS))
            for c in range(1, 4):
                split_low("qkv", c)
            for c in range(2):
                for t in range(NT):
                    banks.wait_read(dve, "qkv", c, t)
            head_norm(q_tok, row("q_norm"), 1)
            for c in range(4, 6):
                split_low("qkv", c)
            for c in range(2, 4):
                for t in range(NT):
                    banks.wait_read(dve, "qkv", c, t)
            head_norm(k_tok, row("k_norm"), 2)
            causal = c_("causal")
            attend("att", float(P) ** -0.5, lambda t: causal[:, (1 - t) * P:S], prob)
            split_low("up", 1, 0)
            add_to_x("w_o")
            feed_forward(1)

            norm(5)
            v.memset(arena[:, 0:2 * (S + TAPS - 1)], 0.0).then_inc(sem("dve_step"), 1)
            step.n += 1
            for i in range(3):
                v.memset(arena[:, (9 + i) * 1024:(9 + i) * 1024 + 2 * (S + 16)], 0.0).then_inc(sem("dve_step"), 1)
                step.n += 1
            dve.wait_ge(sem("dve_step"), step.n)
            v.memset(next(flag), 0.0).then_inc(sem("pool_zero"), 1)
            banks.wait_read(dve, "av", 1)
            bank = banks.read(dve, "av", 0)
            v.tensor_tensor(u_pad[:, :, TAPS - 1:], blocks(bank.ap, 2), sig_gate, ALU.mult).then_inc(bank.freed, 1)
            banks.wait_read(dve, "av", 0)
            for k in range(TAPS):
                for c in range(2):
                    src = u_pad[:, c, k:k + S]
                    if k == 0:
                        last = v.tensor_scalar(conv_acc[:, c, :], src, conv_col[:, c, 0:1], v2("conv_b_2", c),
                                               ALU.mult, ALU.add)
                    else:
                        last = v.scalar_tensor_tensor(conv_acc[:, c, :], src, conv_col[:, c, k:k + 1],
                                                      conv_acc[:, c, :], ALU.mult, ALU.add)
                    last.then_inc(sem("dve_step"), 1)
                    step.n += 1
                dve.wait_ge(sem("dve_step"), step.n)
            v.memset(next(flag), 0.0).then_inc(sem("conv_done"), 1)
            for t in range(NT):
                bank = banks.read(dve, "cq", t)
                v.tensor_copy(cq_tok[:, t, :], bank.ap[:, 0:384]).then_inc(bank.freed, 1)
                banks.wait_read(dve, "cq", t)
                step(v.tensor_tensor(cq_sq, cq_tok[:, t, :], cq_tok[:, t, :], ALU.mult))
                step(v.tensor_reduce(cs[:, 2 * t:2 * t + 1], cq_sq[:, 0:256], AX.X, ALU.add))
                step(v.tensor_reduce(cs[:, 2 * t + 1:2 * t + 2], cq_sq[:, 256:384], AX.X, ALU.add))
                step(v.tensor_scalar(cs[:, 2 * t:2 * t + 1], cs[:, 2 * t:2 * t + 1], 1.0 / 256, EPS, ALU.mult, ALU.add))
                step(v.tensor_scalar(cs[:, 2 * t + 1:2 * t + 2], cs[:, 2 * t + 1:2 * t + 2], 1.0 / P, EPS, ALU.mult,
                                     ALU.add))
            v.memset(next(flag), 0.0).then_inc(sem("latent_sq"), 1)
            dve.wait_ge(sem("latent_root"), 1)
            step(v.reciprocal(cs, cs))
            for t in range(NT):
                step(v.tensor_scalar(cq_tok[:, t, 0:256], cq_tok[:, t, 0:256], cs[:, 2 * t:2 * t + 1], None, ALU.mult))
                step(v.scalar_tensor_tensor(ckv_tok[:, t, :], cq_tok[:, t, 256:384], cs[:, 2 * t + 1:2 * t + 2],
                                            row("kv_norm_g_2"), ALU.mult, ALU.mult))
            v.memset(next(flag), 0.0).then_inc(sem("latents_normed"), 1)
            banks.wait_read(dve, "wi")
            for t in range(NT):
                for g in range(4):
                    banks.wait_read(dve, "idx", t, g)
                    for i in range(2):
                        h = 2 * (2 * (g % 2) + i) + g // 2
                        buf = rel[:, (4 * t + g) % 4 * 2 + i, :]
                        if g == 0 and i == 0:
                            last = v.tensor_scalar(score[:, t, :], buf, wi[:, t, h:h + 1], None, ALU.mult)
                        else:
                            last = v.scalar_tensor_tensor(score[:, t, :], buf, wi[:, t, h:h + 1], score[:, t, :],
                                                          ALU.mult, ALU.add)
                        if i == 0:
                            step(last)
                    last.then_inc(sem("rel_used"), 1)
                    dve.wait_ge(sem("rel_used"), 4 * t + g + 1)
            for t in range(NT):
                step(v.scalar_tensor_tensor(work[:, t, :], score[:, t, :], float(512) ** -0.5,
                                            c_("allowed", t * S, (t + 1) * S), ALU.mult, ALU.add))
                for r in range(8):
                    step(v.max(top8, work[:, t, :]))
                    step(v.match_replace(work[:, t, :], top8, work[:, t, :], -3e38))
                step(v.tensor_scalar(bias2[:, t, :], work[:, t, :], -2e38, NEG, ALU.is_gt, ALU.mult))
            bank = banks.read(dve, "cmean")
            v.tensor_scalar(conv_m[:, 0, :], bank.ap[:, 0:S], 1.0 / 256, None, ALU.mult).then_inc(bank.freed, 1)
            banks.wait_read(dve, "cmean")
            step(v.tensor_tensor(conv_acc, conv_acc, mid(conv_m[:, 0, :], 2), ALU.subtract))
            v.tensor_tensor(conv_sq, conv_acc, conv_acc, ALU.mult).then_inc(sem("conv_centred"), 1)
            banks.wait_read(dve, "pool", 0)
            u = pool_s[0]
            src, spare = pool_s[0], [pool_s[1], pool_s[2]]
            inv_n = blocks(c_("pool_inv"), 2)
            for n, w_ in enumerate((1, 2, 4, 8)):
                dst = spare[n % 2]
                step(v.tensor_tensor(dst[:, :, 16:], src[:, :, 16:], src[:, :, 16 - w_:16 - w_ + S], ALU.add))
                c, g = n // 2, slice(64 * (n % 2), 64 * (n % 2) + 64)
                step(v.tensor_tensor(pool_d[g, c, :], dst[g, c, 16:], inv_n[g, c, :], ALU.mult))
                src = dst
            v.tensor_tensor(pool_d, pool_d, u[:, :, 16:], ALU.subtract).then_inc(sem("pool_ready"), 1)
            bank = banks.read(dve, "cvar")
            v.tensor_scalar(conv_m[:, 0, :], bank.ap[:, 0:S], 1.0 / 256, EPS, ALU.mult, ALU.add).then_inc(bank.freed, 1)
            dve.wait_ge(sem("conv_root"), 1)
            step(v.reciprocal(conv_m[:, 0, :], conv_m[:, 0, :]))
            v.tensor_tensor(conv_acc, conv_acc, mid(conv_m[:, 0, :], 2), ALU.mult).then_inc(sem("conv_normed"), 1)
            for g in range(2):
                rows_ = slice(64 * g, 64 * g + 64)
                bank = banks.read(dve, "poolo", g)
                for c in range(2):
                    last = v.tensor_scalar(yT[rows_, 6 + c, :], bank.ap[rows_, c * S:(c + 1) * S],
                                           v2("pool_scale_2", c)[rows_, :], None, ALU.mult)
                last.then_inc(bank.freed, 1)
            attend("dsa", 64.0 ** -0.5, lambda t: bias2[:, t, 0:(t + 1) * P], prob2)
            for n in range(2):
                for t in range(NT):
                    bank = banks.read(dve, "w_out2", n, t)
                    part = x3[:, t, n * 512:(n + 1) * 512]
                    v.tensor_tensor(scaled, bank.ap, g1_row[:, n * 512:(n + 1) * 512], ALU.mult)\
                        .then_inc(bank.freed, 1)
                    banks.wait_read(dve, "w_out2", n, t)
                    step(v.tensor_tensor(part, part, scaled, ALU.add))
            v.memset(next(flag), 0.0).then_inc(sem("mix2_added"), 1)

            norm(6)
            step(v.memset(gates[:, :, N_EXP:], 0.0))
            step(v.memset(rank[:, :, N_EXP:], -1.0))
            bank = banks.read(dve, "router")
            bias_row = rows[:, rows_at["router_g_b_2"][0]:rows_at["router_e_b_2"][1]]
            v.tensor_tensor(lg, bank.ap[:, 0:72].rearrange("p (t n) -> p t n", t=NT), mid(bias_row, NT), ALU.add)\
                .then_inc(bank.freed, 1)
            banks.wait_read(dve, "router")
            first = c_("first")

            def one_hot(dst, logits, best, spare_):
                n = logits.shape[1]
                step(v.tensor_reduce(best, logits, AX.X, ALU.max))
                step(v.scalar_tensor_tensor(dst, logits, best, first[:, 0:n], ALU.is_equal, ALU.mult))
                step(v.tensor_reduce(spare_, dst, AX.X, ALU.max))
                step(v.tensor_scalar(dst, dst, spare_, None, ALU.is_equal))

            for t in range(NT):
                r = rt[t]
                group, e_sel, h1, h2 = r[:, 0:4], r[:, 4:12], r[:, 12:20], r[:, 20:28]
                g_max, g_sum, e1, e2, tmp, diff, expd = (r[:, 28 + i:29 + i] for i in range(7))
                shifted, hit = r[:, 36:40], r[:, 40:48]
                one_hot(group, lg[:, t, 0:4], g_max, tmp)
                v.tensor_scalar(shifted, lg[:, t, 0:4], g_max, None, ALU.subtract).then_inc(sem("group_shifted"), 1)
                step(v.tensor_scalar(e_sel, lg[:, t, 4:12], group[:, 0:1], None, ALU.mult))
                for g in range(1, 4):
                    step(v.scalar_tensor_tensor(e_sel, lg[:, t, 4 + 8 * g:12 + 8 * g], group[:, g:g + 1], e_sel,
                                                ALU.mult, ALU.add))
                one_hot(h1, e_sel, e1, tmp)
                step(v.scalar_tensor_tensor(e_sel, h1, NEG, e_sel, ALU.mult, ALU.add))
                one_hot(h2, e_sel, e2, tmp)
                v.tensor_tensor(diff, e2, e1, ALU.subtract).then_inc(sem("expert_diff"), 1)
                dve.wait_ge(sem("route_exp"), 2 * (t + 1))
                step(v.tensor_reduce(g_sum, shifted, AX.X, ALU.add))
                step(v.tensor_scalar(tmp, expd, 1.0, g_sum, ALU.add, ALU.mult))
                step(v.reciprocal(tmp, tmp))
                step(v.tensor_tensor(hit, h1, h2, ALU.add))
                step(v.scalar_tensor_tensor(h1, h2, expd, h1, ALU.mult, ALU.add))
                step(v.tensor_scalar(h1, h1, tmp, None, ALU.mult))
                for g in range(4):
                    step(v.tensor_scalar(gates[:, t, 8 * g:8 * g + 8], h1, group[:, g:g + 1], None, ALU.mult))
                    step(v.tensor_scalar(chosen[:, t, 8 * g:8 * g + 8], hit, group[:, g:g + 1], None, ALU.mult))
            v.memset(next(flag), 0.0).then_inc(sem("chosen_ready"), 1)
            bank = banks.read(dve, "rank")
            step(v.tensor_scalar(chosen, chosen, -float(1 << 20), float(1 << 20), ALU.mult, ALU.add))
            step(v.tensor_reduce(most, bank.ap[:, 2 * N_EXP:3 * N_EXP], AX.X, ALU.max))
            v.tensor_tensor(rank[:, :, 0:N_EXP], bank.ap[:, 0:2 * N_EXP].rearrange("p (t n) -> p t n", t=NT), chosen,
                            ALU.add).then_inc(bank.freed, 1)
            banks.wait_read(dve, "rank")
            v.tensor_copy(most_int[:, :], most).then_inc(sem("most_ready"), 1)
            dve.wait_ge(sem("most_ready"), 1)
            crowded = dve.value_load(most_int[0:1, 0:1], min_val=0, max_val=S)
            with dve.If(crowded > SLOTS_OF):
                dense_dve(dve)
            with dve.Else():
                sparse_dve(dve)
            dve.wait_ge(sem("moe_sum"), 1)
            for t in range(NT):
                for n in range(2):
                    part = x3[:, t, n * 512:(n + 1) * 512]
                    step(v.tensor_tensor(scaled, bank_aps[2 * t + n], g2_row[:, n * 512:(n + 1) * 512], ALU.mult))
                    step(v.tensor_tensor(part, part, scaled, ALU.add))
            v.memset(next(flag), 0.0).then_inc(sem("moe_added"), 1)
            dve.wait_ge(sem("rms_root"), 7)
            step(v.reciprocal(rstd, rstd))
            dve.wait_ge(sem("big_row_landed"), 48)
            for t in range(NT):
                v.scalar_tensor_tensor(xn3[:, t, :], x3[:, t, :], rstd[:, t:t + 1], big_row, ALU.mult, ALU.mult)\
                    .then_inc(sem("final_ready"), 1)

        @block.scalar
        def _(act):
            s = nc.scalar
            step = Chain(act, sem("act_step"))
            eps_col, ln_col = c_("eps"), c_("ln_eps")

            def evacuate(dst, func, *name, scale=1.0, width=512, bias=None):
                bank = banks.read(act, *name)
                src = bank.ap[:, 0:width]
                if len(dst.shape) == 3:
                    src = blocks(src, dst.shape[1])
                s.activation(dst, src, func, scale=scale).then_inc(bank.freed, 1)

            def norm(k, squares=xn3):
                for t in range(NT):
                    step(s.activation(squares[:, t, :], x3[:, t, :], ACT.Square, accum_out=ssq2[:, t:t + 1]))
                s.activation(rstd, ssq2, ACT.Sqrt, scale=1.0 / D, bias=eps_col).then_inc(sem("rms_root"), 1)

            def split_high(*name):
                for s in range(2):
                    no = 2 * split_no[name] + s
                    if s == 0:
                        act.wait_ge(landed[unit_of[name] % SLOTS], landed_value[name])
                    if no >= 4:
                        act.wait_ge(*half_read[(split_units[no // 2 - 2], s)])
                    nc.scalar.activation(high_of(name, s), half_of(slot(name), name, s), ACT.Copy)\
                        .then_inc(sem("split_high"), 1)

            def take_turned(tag, scale, bias=None):
                for c in range(KC // 2):
                    bank = banks.read(act, tag, c)
                    for i in range(2):
                        k = 2 * c + i
                        kw = {} if bias is None else {"bias": bias(k)}
                        if scale is None:
                            last = s.activation(hT3[:, k, :], bank.ap[:, i * S:(i + 1) * S], ACT.Copy)
                        else:
                            last = s.activation(hT3[:, k, :], bank.ap[:, i * S:(i + 1) * S], ACT.Identity,
                                                scale=scale(k), **kw)
                    last.then_inc(bank.freed, 1)

            act.dma_start(const[:, :], a["constants"]).then_inc(sem("const_landed"), 16)
            load_vectors(act, 0, VECS1, 0)
            act.wait_ge(sem("const_landed"), 16)
            act.wait_ge(sem("x_landed"), 16)
            norm(1)
            split_high("w_in", 0)
            act.wait_ge(sem("lb_shifted"), 1)
            s.activation(lb_e, lb_d, ACT.Exp).then_inc(sem("lb_exp"), 1)
            banks.wait_read(act, "vec", 0)
            take_turned("h_mix", lambda k: v1("attn_norm", k))
            split_high("w_in", 1)
            for i in range(2):
                evacuate(hq[:, 2 * i:2 * i + 2, :], ACT.Silu, "in", 0, i)
            split_high("w_in", 2)
            for i in range(2):
                evacuate(hf[:, 2 * i:2 * i + 2, :], ACT.Sigmoid, "in", 1, i)
            split_high("w_in", 3)
            for t in range(NT):
                evacuate(hv[:, t, :], ACT.Copy, "hi", t)
            split_high("w_in", 4)
            for i in range(2):
                evacuate(hgT[:, 2 * i:2 * i + 2, :], ACT.Silu, "in", 3, i)
            split_high("w_in", 5)
            banks.wait_read(act, "vec", 1)
            s.activation(cond, v2("c_2", 0, 8), ACT.Silu).then_inc(sem("cond_ready"), 1)
            for c in (6, 7):
                split_high("w_in", c)
            act.wait_ge(sem("low_mixed"), 1)
            step(s.activation(low[0:64, 0, :], low[0:64, 0, :], ACT.Tanh))
            s.activation(low[:, 1, :], low[:, 1, :], ACT.Sigmoid).then_inc(sem("low_ready"), 1)
            for tag, dst, col in (("lw", logdec, "rwkv_w0"), ("la", a_gate, "rwkv_a0")):
                for c in range(2):
                    bank = banks.read(act, tag, c)
                    for i in range(2):
                        j = 2 * c + i
                        last = s.activation(dst[:, j, :], bank.ap[:, i * S:(i + 1) * S], ACT.Sigmoid, bias=v1(col, j))
                    last.then_inc(bank.freed, 1)
            for c in range(2):
                evacuate(g_out[:, 2 * c:2 * c + 2, :], ACT.Copy, "lg", c)
            act.wait_ge(sem("hgrn_sq"), 1)
            s.activation(hg_ss, hg_ss, ACT.Sqrt).then_inc(sem("hgrn_root"), 1)
            for c in range(2):
                banks.wait_read(act, "kk", c)
            s.activation(page(21), page(21), ACT.Sqrt).then_inc(sem("kk_root"), 1)
            act.wait_ge(sem("cum_ready"), 1)
            step(s.activation(page(21), page(21), ACT.Exp))
            step(s.activation(page(22), page(12), ACT.Exp))
            s.activation(page(12), page(12), ACT.Exp, scale=-1.0).then_inc(sem("decays_exp"), 1)
            s.activation(s_scale, s_scale, ACT.Exp).then_inc(sem("scale_exp"), 1)
            for b in range(2):
                evacuate(bk_tok[:, b], ACT.Copy, "bk", b)
            for g in range(4):
                evacuate(inv[:, 4 * g:4 * g + 4, :], ACT.Copy, "x", 1, g)
            for m in LEVELS[1:]:
                for g in range(4):
                    evacuate(a_inv[:, 4 * g:4 * g + 4, :], ACT.Copy, "ax", m, g)
                if m != LEVELS[-1]:
                    for g in range(4):
                        evacuate(inv[:, 4 * g:4 * g + 4, :], ACT.Copy, "x", m, g)
            act.wait_ge(sem("rwkv_sq"), 1)
            s.activation(rw_ss, rw_ss, ACT.Sqrt).then_inc(sem("rwkv_root"), 1)

            def feed_forward(l):
                banks.read(act, "w_out" if l == 0 else "w_o", 0, 0)
                split_high("up", l, 0)
                take_turned(("h_mlp", l), lambda k: v1("mlp_norm", 8 * l + k))
                for n in range(2):
                    for t in range(NT):
                        banks.wait_read(act, "w_out" if l == 0 else "w_o", n, t)
                norm(2 if l == 0 else 4, blocks(page(8, 2), NT))
                for c in range(8):
                    if c < 7:
                        split_high("up", l, c + 1)
                    elif l:
                        split_high("down", 1, 0, 0)
                    for i in range(2):
                        n = 2 * c + i
                        if n >= 4 or l:
                            act.wait_ge(sem("act_ready"), 16 * l + n - 3)
                        evacuate(relu[:, n % 4, :], ACT.Relu, "up", l, c, i)
                if l:
                    for unit in ((0, 1), (0, 2), (1, 0), (1, 1), (1, 2)):
                        split_high("down", 1, *unit)
                evacuate(pT, ACT.Copy, "pT", l)
                for n in range(2):
                    for t in range(NT):
                        evacuate(ple_raw[:, t, n * 512:(n + 1) * 512], ACT.Copy, "ple", l, n, t)
                for n in range(2):
                    for t in range(NT):
                        banks.wait_read(act, "ple", l, n, t)
                for t in range(NT):
                    step(s.activation(xn3[:, t, :], ple_raw[:, t, :], ACT.Square, accum_out=ssq2[:, t:t + 1]))
                s.activation(ssq, ssq2, ACT.Sqrt, scale=1.0 / D, bias=eps_col).then_inc(sem("ple_root"), 1)
                take_turned(("x_gate", l), None)
                if l == 0:
                    split_high("qkv", 0)
                for n in range(2):
                    for t in range(NT):
                        evacuate(gate_s[:, t, n * 512:(n + 1) * 512], ACT.Sigmoid, "gate", l, n, t)

            def attend(tag, probs, probsT, dst):
                n = 2 * HEADS
                for i in range(n + LAG):
                    if i < n:
                        t = i % 2
                        part = probs[:, i % 8, 0:(t + 1) * P]
                        act.wait_ge(sem(tag + "_max"), i + 1)
                        s.activation(part, part, ACT.Exp, bias=nmax[:, i:i + 1], accum_out=rsum[:, i:i + 1])\
                            .then_inc(sem(tag + "_exp"), 1)
                    if i >= LAG:
                        i2 = i - LAG
                        h, t = i2 // 2, i2 % 2
                        if i2 >= 4:
                            last_head = (i2 - 4) // 2
                            if last_head % 2:
                                banks.read(act, tag, "o", last_head // 2)
                            else:
                                act.wait_ge(sem(tag + "_even_read"), last_head // 2 + 1)
                        bank = banks.read(act, tag, "pT", i2)
                        s.activation(probsT[:, i2 % 4, 0:t + 1, :], blocks(bank.ap[:, 0:(t + 1) * P], t + 1), ACT.Copy)\
                            .then_inc(bank.freed, 1)
                        if i2 >= 5 and (i2 - 5) % 4 == 0:
                            c = (i2 - 5) // 4
                            evacuate(dst[:, 2 * c:2 * c + 2, :], ACT.Copy, tag, "o", c)
                evacuate(dst[:, 6:8, :], ACT.Copy, tag, "o", 3)

            feed_forward(0)
            take_turned("h_att", lambda k: v1("attn_norm", 8 + k))
            act.wait_ge(sem("ple_added"), 1)
            norm(3, blocks(page(6, 2), NT))
            for u, dst in enumerate((q_tok, q_tok, k_tok, k_tok, v_att, v_att)):
                if u < 5:
                    split_high("qkv", u + 1)
                if u in (2, 4):
                    k = u // 2 - 1
                    act.wait_ge(sem("head_sq"), k + 1)
                    s.activation(head_ss, head_ss, ACT.Sqrt).then_inc(sem("head_root"), 1)
                if u == 0:
                    act.wait_ge(sem("scales_ready"), 1)
                for t in range(NT):
                    evacuate(dst[:, t, (u % 2) * 512:(u % 2 + 1) * 512], ACT.Copy, "qkv", u, t, scale=rstd[:, t:t + 1])
            for tag, dst in (("qT", qT), ("kT", kT)):
                for c in range(4):
                    evacuate(dst[:, 2 * c:2 * c + 2, :], ACT.Copy, tag, c)
            attend("att", prob, probT, hT3)
            feed_forward(1)
            act.wait_ge(sem("ple_added"), 2)
            norm(5)
            take_turned("h_in2", lambda k: sc1[:, k:k + 1], lambda k: modc[:, k:k + 1])
            evacuate(sig_gate, ACT.Sigmoid, "av", 1)
            for i in range(2):
                evacuate(qiT[:, 2 * i:2 * i + 2, :], ACT.Copy, "qi", i)
            evacuate(kiT, ACT.Copy, "ki", 0, width=S)
            act.wait_ge(sem("pool_zero"), 1)
            bank = banks.read(act, "pool", 0)
            s.activation(pool_s[0][:, :, 16:], blocks(bank.ap, 2), ACT.Copy).then_inc(bank.freed, 1)
            evacuate(wi.rearrange("p t h -> p (t h)"), ACT.Copy, "wi", width=16)
            evacuate(w_ukT, ACT.Copy, "ukT")
            act.wait_ge(sem("latent_sq"), 1)
            s.activation(cs, cs, ACT.Sqrt).then_inc(sem("latent_root"), 1)
            bank = banks.read(act, "cqT")
            for k in range(2):
                last = s.activation(cqT[:, k, :], bank.ap[:, k * S:(k + 1) * S], ACT.Identity, scale=v2("q_norm_g_2", k))
            last.then_inc(bank.freed, 1)
            evacuate(ckvT, ACT.Copy, "ckvT", width=S)
            for t in range(NT):
                for g in range(4):
                    n = 4 * t + g
                    if n >= 4:
                        act.wait_ge(sem("rel_used"), n - 3)
                    evacuate(rel[:, (n % 4) * 2:(n % 4) * 2 + 2, :], ACT.Relu, "idx", t, g)
            for i in range(2):
                evacuate(q2T[:, 2 * i:2 * i + 2, :], ACT.Copy, "q2", i)
            for g in range(4):
                bank = banks.read(act, "qabs", g)
                h0 = 4 * (g % 2) + g // 2
                s.activation(q_abs[:, h0:h0 + 3:2, :], blocks(bank.ap, 2), ACT.Copy).then_inc(bank.freed, 1)
            banks.wait_read(act, "cvar")
            s.activation(conv_m[:, 0, :], conv_m[:, 0, :], ACT.Sqrt).then_inc(sem("conv_root"), 1)
            act.wait_ge(sem("conv_normed"), 1)
            for c in range(2):
                s.activation(yT[:, c, :], conv_acc[:, c, :], ACT.Silu, scale=v2("conv_ln_g_2", c),
                             bias=v2("conv_ln_b_2", c)).then_inc(sem("conv_out"), 1)
            attend("dsa", prob2, probT2, ctxT)
            for g in range(2):
                rows_ = slice(64 * g, 64 * g + 64)
                for c in range(2):
                    bank = banks.read(act, "yatt", g, c)
                    s.activation(yT[rows_, 2 + 2 * c:4 + 2 * c, :], blocks(bank.ap, 2)[rows_], ACT.Copy)\
                        .then_inc(bank.freed, 1)
            act.wait_ge(sem("mix2_added"), 1)
            norm(6)
            take_turned("h_moe", lambda k: sc2[:, k:k + 1], lambda k: modc[:, 24 + k:25 + k])
            for t in range(NT):
                r = rt[t]
                act.wait_ge(sem("group_shifted"), t + 1)
                s.activation(r[:, 36:40], r[:, 36:40], ACT.Exp).then_inc(sem("route_exp"), 1)
                act.wait_ge(sem("expert_diff"), t + 1)
                s.activation(r[:, 34:35], r[:, 33:34], ACT.Exp).then_inc(sem("route_exp"), 1)
            act.wait_ge(sem("most_ready"), 1)
            crowded = act.value_load(most_int[0:1, 0:1], min_val=0, max_val=S)
            with act.If(crowded > SLOTS_OF):
                dense_act(act)
            with act.Else():
                sparse_act(act)
            act.wait_ge(sem("moe_added"), 1)
            norm(7)

        @block.sync
        def _(sp):
            sp.dma_start(x3, a["x"][0].rearrange("(t p) n -> p t n", p=P)).then_inc(sem("x_landed"), 16)
            for i, (name, parts) in enumerate(units):
                if i >= SLOTS:
                    sp.wait_ge(*unit_read[units[i - SLOTS][0]])
                for dst, src in parts:
                    sp.dma_start(dst(slot(name)), src).then_inc(landed[i % SLOTS], 16)
            sources = [a["exp_w1_2"][0], a["exp_w3_2"][0], a["exp_w2_2"][0]]
            kinds = [(0, 0), (1, 0), (0, 1), (1, 1), (2, 0), (2, 1)]

            def load_pair(p2, i):
                kind, second = kinds[i]
                w = sources[kind]
                sp.dma_start(blocks(moe_slot[i], EC if kind == 2 else KC), kcn(w[p2 + second]))\
                    .then_inc(moe_landed[i], 16)

            for c in range(2):
                sp.wait_ge(*unit_read[("w_out2", c)])
            sp.wait_ge(*unit_read[("dsa",)])
            banks.wait_read(sp, "w_out2", 1, 1)
            for i in range(MOE_SLOTS):
                if i == MOE_SLOTS - 1:
                    sp.wait_ge(sem("mix2_added"), 1)
                load_pair(0, i)
            sp.wait_ge(sem("most_ready"), 1)
            crowded = sp.value_load(most_int[0:1, 0:1], min_val=0, max_val=S)
            with sp.If(crowded > SLOTS_OF):
                for i in range(MOE_SLOTS):
                    sp.wait_ge(moe_landed[i], landed_before[i] + 16)
                banks.wait_read(sp, "rank")
                with nc.allow_non_contiguous_dma(reason="a small table, off the usual path"):
                    for t in range(NT):
                        sp.dma_start(gates_dram.rearrange("e (t p) -> t p e", p=P)[t], gates[:, t, 0:N_EXP])\
                            .then_inc(sem("gates_out"), 16)
                sp.wait_ge(sem("gates_out"), 16 * NT)
                sp.dma_start(page(0, 8), gates_dram.rearrange("e t -> (e t)").partition_broadcast(P))\
                    .then_inc(sem("gates_back"), 16)

                def load_expert(e, i):
                    sp.dma_start(blocks(ring[:, i * UNIT:(i + 1) * UNIT], KC if i < 2 else EC), kcn(sources[i][e]))\
                        .then_inc(landed[i], 16)

                for i in range(3):
                    load_expert(0, i)
                with sp.Fori(0, N_EXP - 1) as e:
                    sp.wait_ge(sem("moe_hidden"), e * EC + EC)
                    load_expert(e + 1, 0)
                    load_expert(e + 1, 1)
                    sp.wait_ge(sem("moe_down"), e + 2)
                    load_expert(e + 1, 2)
            with sp.Else():
                with sp.Fori(0, PAIRS - 1) as p2:
                    for i, (b, phase) in enumerate(UNIT_FILLS):
                        sp.wait_ge(moe_full[b], p2 * 3 + (phase + 2))
                        load_pair(p2 * 2 + 2, i)
            sp.wait_ge(sem("final_ready"), 2)
            sp.dma_start(out[0].rearrange("(t p) n -> p t n", p=P), xn3).then_inc(sem("out_written"), 16)
            sp.wait_ge(sem("out_written"), 16)

        @block.gpsimd
        def _(pool):
            load_vectors(pool, P, VECS2, 1)
            for name, n in ROWS:
                src = a[name]
                flat = src.rearrange("a b c -> (a b c)") if len(src.shape) == 3 else src.rearrange("a b -> (a b)")
                pool.dma_start(row(name), flat.partition_broadcast(P)).then_inc(sem("rows_landed"), 16)
            pool.dma_start(blocks(router[:, :], KC)[:, :, 0:4], kcn(a["router_g_w_2"][0]))\
                .then_inc(sem("router_landed"), 16)
            pool.dma_start(blocks(router[:, :], KC)[:, :, 4:36],
                           a["router_e_w_2"][0].rearrange("(k p) g e -> p k (g e)", p=P)).then_inc(sem("router_landed"), 16)
            pool.dma_start(big_row, a["ple_norm"][0].partition_broadcast(P)).then_inc(sem("big_row_landed"), 16)
            pool.wait_ge(sem("mixed_ready"), 1)
            for i, dst in enumerate((g1_row, g2_row)):
                part = a["mod_b_2"][0, (2 + 3 * i) * D:(3 + 3 * i) * D]
                pool.dma_start(dst, part.partition_broadcast(P)).then_inc(sem("gate_bias_landed"), 16)
            for l in range(2):
                if l:
                    pool.wait_ge(sem("ple_added"), 1)
                pool.dma_start(p_tok, a["p"][l, 0].rearrange("(t p) n -> p t n", p=P)).then_inc(sem("p_landed"), 16)
                if l:
                    pool.dma_start(big_row, a["ple_norm"][1].partition_broadcast(P)).then_inc(sem("big_row_landed"), 16)
            pool.wait_ge(sem("ple_added"), 2)
            pool.dma_start(big_row, a["final_g_2"].partition_broadcast(P)).then_inc(sem("big_row_landed"), 16)


INPUTS = [
    "x", "p", "attn_norm", "mlp_norm", "w_in_ar", "w_out_ar", "hgrn_lb", "hgrn_onorm", "rwkv_mu", "rwkv_w0",
    "rwkv_w2", "rwkv_a0", "rwkv_a2", "rwkv_g2", "rwkv_kk", "rwkv_ka", "rwkv_rk", "rwkv_ln_w", "rwkv_ln_b", "w_qkv",
    "w_o_attn", "q_norm", "k_norm", "w_up", "w_down", "ple_proj", "ple_norm", "ple_gate", "c_2", "mod_w_2", "mod_b_2",
    "norm1_g_2", "w_in_2", "conv_k_2", "conv_b_2", "conv_ln_g_2", "conv_ln_b_2", "q_norm_g_2", "kv_norm_g_2",
    "w_uq_2", "w_uk_2", "w_uv_2", "pool_w_2", "pool_scale_2", "w_out_2", "norm2_g_2", "router_g_w_2",
    "router_g_b_2", "router_e_w_2", "router_e_b_2", "exp_w1_2", "exp_w3_2", "exp_w2_2", "final_g_2",
]


def kernel(**inputs):
    import concourse.bacc as bacc
    from concourse.bass_utils import run_bass_kernel_spmd

    nc = bacc.Bacc("TRN2", target_bir_lowering=False, num_devices=1)
    arrays, args = {}, {}
    for name in INPUTS:
        a = np.ascontiguousarray(inputs[name])
        arrays[f"in_{name}"] = a
        args[name] = nc.dram_tensor(f"in_{name}", a.shape, mybir.dt.from_np(a.dtype), kind="ExternalInput").ap()
    table = constants()
    arrays["constants"] = table
    args["constants"] = nc.dram_tensor("constants", table.shape, F32, kind="ExternalInput").ap()
    out = nc.dram_tensor("out", (1, S, D), F32, kind="ExternalOutput").ap()
    build(nc, args, out)
    r = run_bass_kernel_spmd(nc, [arrays], core_ids=[0])
    return r.results[0]["out"]
```
